# Optimizing a Trainium2 kernel written in Bass

```python
import math
import jax, jax.numpy as jnp
from jax import lax
import numpy as np
import jax
import jax.numpy as jnp

D_MODEL = 1024
BATCH = 1
SEQ = 512
DEPTH = 1

HG_HEADS = 4
HG_DK = 128
HG_DV = 128
HG_WIDTH = HG_HEADS * HG_DK
HG_CHUNK = 64
DA_HEADS = 4
DA_HEAD = 64
DA_VDIM = 2 * DA_HEAD
DA_QK_WIDTH = DA_HEADS * 2 * DA_HEAD
DA_WIDTH = DA_HEADS * DA_VDIM
Q_BLOCK = 128
ROPE_THETA = 10000.0
N_GROUPS = 4
EXPERTS_PER_GROUP = 8
N_EXPERTS = N_GROUPS * EXPERTS_PER_GROUP
TOP_K = 2
D_FF_EXPERT = 512
MOE_BLOCK = 128
EPS = 1e-6
IN_COLS = 4 * HG_WIDTH + 2 * DA_QK_WIDTH + DA_WIDTH + 2 * D_MODEL


def rms_norm(x, gain):
    xf = x.astype(jnp.float32)
    y = xf * lax.rsqrt(jnp.mean(xf * xf, axis=-1, keepdims=True) + EPS)
    return (y * gain.astype(jnp.float32)).astype(x.dtype)

def rope(x, pos):
    half = x.shape[-1] // 2
    inv = ROPE_THETA ** (-jnp.arange(half, dtype=jnp.float32) / half)
    ang = pos.astype(jnp.float32)[:, None] * inv[None, :]
    cos = jnp.cos(ang)[None, :, None, :]
    sin = jnp.sin(ang)[None, :, None, :]
    x1, x2 = x[..., :half].astype(jnp.float32), x[..., half:].astype(jnp.float32)
    return jnp.concatenate([x1 * cos - x2 * sin, x1 * sin + x2 * cos], axis=-1).astype(x.dtype)

def hgrn2_chunked(q, k, v, log_f):
    B, S, H, DK = q.shape
    DV = v.shape[-1]
    C = HG_CHUNK
    NC = S // C

    def to_chunks(t):
        return t.astype(jnp.float32).reshape(B, NC, C, H, t.shape[-1]).transpose(1, 0, 3, 2, 4)

    qc, kc, vc, gc = to_chunks(q), to_chunks(k), to_chunks(v), to_chunks(log_f)
    causal = jnp.tril(jnp.ones((C, C), dtype=bool))

    def step(state, inp):
        qi, ki, vi, gi = inp
        b = jnp.cumsum(gi, axis=-2)
        b_ref = b[..., C // 2 - 1:C // 2, :]
        q_rel = qi * jnp.exp(b - b_ref)
        k_rel = ki * jnp.exp(b_ref - b)
        scores = jnp.einsum('bhtk,bhsk->bhts', q_rel, k_rel)
        scores = jnp.where(causal, scores, 0.0)
        o = (jnp.einsum('bhts,bhsv->bhtv', scores, vi)
             + jnp.einsum('bhtk,bhkv->bhtv', qi * jnp.exp(b), state))
        b_end = b[..., -1:, :]
        k_end = ki * jnp.exp(b_end - b)
        new_state = (jnp.exp(b_end[..., 0, :])[..., None] * state
                     + jnp.einsum('bhsk,bhsv->bhkv', k_end, vi))
        return new_state, o

    state0 = jnp.zeros((B, H, DK, DV), jnp.float32)
    _, o = lax.scan(step, state0, (qc, kc, vc, gc))
    return o.transpose(1, 0, 3, 2, 4).reshape(B, S, H, DV)

def diff_attention(q1, q2, k1, k2, v, lam):
    B, S, H, D = q1.shape
    NQ = S // Q_BLOCK
    scale = D ** -0.5
    key_pos = jnp.arange(S)

    def block(i):
        start = i * Q_BLOCK
        qb1 = lax.dynamic_slice_in_dim(q1, start, Q_BLOCK, axis=1)
        qb2 = lax.dynamic_slice_in_dim(q2, start, Q_BLOCK, axis=1)
        qpos = start + jnp.arange(Q_BLOCK)
        mask = key_pos[None, :] <= qpos[:, None]

        def probs(qb, kk):
            s = jnp.einsum('bqhd,bshd->bhqs', qb, kk).astype(jnp.float32) * scale
            return jax.nn.softmax(jnp.where(mask, s, -jnp.inf), axis=-1)

        a = probs(qb1, k1) - lam * probs(qb2, k2)
        return jnp.einsum('bhqs,bshv->bqhv', a.astype(v.dtype), v)

    o = lax.map(block, jnp.arange(NQ))
    return o.transpose(1, 0, 2, 3, 4).reshape(B, S, H, v.shape[-1])

def hier_moe(xn, w_rg, b_rg, w_re, b_re, w1, w3, w2):
    B, S, D = xn.shape
    T = B * S
    xt = xn.reshape(T, D)
    g_logits = (xt @ w_rg).astype(jnp.float32) + b_rg.astype(jnp.float32)
    g_sel = jnp.argmax(g_logits, axis=-1)
    g_w = jnp.max(jax.nn.softmax(g_logits, axis=-1), axis=-1, keepdims=True)
    e_logits = ((xt @ w_re).astype(jnp.float32) + b_re.astype(jnp.float32)).reshape(
        T, N_GROUPS, EXPERTS_PER_GROUP)
    e_in_group = jnp.sum(e_logits * jax.nn.one_hot(g_sel, N_GROUPS, dtype=jnp.float32)[:, :, None], axis=1)
    top_v, top_i = lax.top_k(e_in_group, TOP_K)
    e_w = jax.nn.softmax(top_v, axis=-1) * g_w

    A = T * TOP_K
    expert_id = (g_sel[:, None] * EXPERTS_PER_GROUP + top_i).reshape(A).astype(jnp.int32)
    token_id = jnp.repeat(jnp.arange(T, dtype=jnp.int32), TOP_K)
    weight = e_w.reshape(A)

    order = jnp.argsort(expert_id)
    se = expert_id[order]
    counts = jnp.zeros((N_EXPERTS,), jnp.int32).at[expert_id].add(1)
    padded = (counts + MOE_BLOCK - 1) // MOE_BLOCK * MOE_BLOCK
    pad_end = jnp.cumsum(padded)
    pad_start = pad_end - padded
    start = jnp.cumsum(counts) - counts
    dest = pad_start[se] + jnp.arange(A, dtype=jnp.int32) - start[se]
    P = A + N_EXPERTS * MOE_BLOCK
    NB = P // MOE_BLOCK
    buf_tok = jnp.full((P,), T, jnp.int32).at[dest].set(token_id[order])
    buf_w = jnp.zeros((P,), jnp.float32).at[dest].set(weight[order])
    block_start = jnp.arange(NB, dtype=jnp.int32) * MOE_BLOCK
    block_expert = jnp.minimum(
        jnp.sum(pad_end[None, :] <= block_start[:, None], axis=1), N_EXPERTS - 1).astype(jnp.int32)
    x_pad = jnp.concatenate([xt, jnp.zeros((1, D), xt.dtype)], axis=0)

    def run_block(args):
        tok, w, e = args
        xb = x_pad[tok]
        hid = jax.nn.silu(xb @ w1[e]) * (xb @ w3[e])
        return (hid @ w2[e]) * w[:, None].astype(xb.dtype)

    y = lax.map(run_block, (buf_tok.reshape(NB, MOE_BLOCK), buf_w.reshape(NB, MOE_BLOCK), block_expert))
    out = jnp.zeros((T + 1, D), xt.dtype).at[buf_tok].add(y.reshape(P, D))
    return out[:T].reshape(B, S, D)

def first_inputs(seed: int = 0) -> dict:
    key = jax.random.key(seed)
    ks = jax.random.split(key, 20)

    def nrm(k, shape, scale):
        return jax.random.normal(k, shape, jnp.float32) * scale

    def gain(k, shape):
        return 1.0 + nrm(k, shape, 0.02)

    return {
        "x": nrm(ks[0], (BATCH, SEQ, D_MODEL), 1.0),
        "norm_mix": gain(ks[1], (DEPTH, D_MODEL)),
        "w_in": nrm(ks[2], (DEPTH, D_MODEL, IN_COLS), D_MODEL ** -0.5),
        "hg_lb": nrm(ks[3], (DEPTH + 1, HG_WIDTH), 0.1),
        "hg_out_norm": gain(ks[4], (DEPTH, HG_DV)),
        "da_q_norm": gain(ks[5], (DEPTH, DA_HEAD)),
        "da_k_norm": gain(ks[6], (DEPTH, DA_HEAD)),
        "da_lambda": nrm(ks[7], (DEPTH, 4, DA_HEAD), 0.1),
        "da_out_norm": gain(ks[8], (DEPTH, DA_VDIM)),
        "w_branch_hg": nrm(ks[9], (DEPTH, HG_WIDTH, D_MODEL), HG_WIDTH ** -0.5),
        "w_branch_da": nrm(ks[10], (DEPTH, DA_WIDTH, D_MODEL), DA_WIDTH ** -0.5),
        "w_out": nrm(ks[11], (DEPTH, D_MODEL, D_MODEL), D_MODEL ** -0.5),
        "norm_moe": gain(ks[12], (DEPTH, D_MODEL)),
        "w_router_group": nrm(ks[13], (DEPTH, D_MODEL, N_GROUPS), D_MODEL ** -0.5),
        "b_router_group": nrm(ks[14], (DEPTH, N_GROUPS), 0.01),
        "w_router_expert": nrm(ks[15], (DEPTH, D_MODEL, N_EXPERTS), D_MODEL ** -0.5),
        "b_router_expert": nrm(ks[16], (DEPTH, N_EXPERTS), 0.01),
        "w1": nrm(ks[17], (DEPTH, N_EXPERTS, D_MODEL, D_FF_EXPERT), D_MODEL ** -0.5),
        "w3": nrm(ks[18], (DEPTH, N_EXPERTS, D_MODEL, D_FF_EXPERT), D_MODEL ** -0.5),
        "w2": nrm(ks[19], (DEPTH, N_EXPERTS, D_FF_EXPERT, D_MODEL), D_FF_EXPERT ** -0.5),
    }

def first_block(x, norm_mix, w_in, hg_lb, hg_out_norm, da_q_norm, da_k_norm, da_lambda,
              da_out_norm, w_branch_hg, w_branch_da, w_out, norm_moe, w_router_group,
              b_router_group, w_router_expert, b_router_expert, w1, w3, w2):
    B, S, _ = x.shape
    pos = jnp.arange(S)
    widths = [HG_WIDTH] * 4 + [DA_QK_WIDTH, DA_QK_WIDTH, DA_WIDTH, D_MODEL, D_MODEL]
    splits = [int(v) for v in np.cumsum(widths)[:-1]]
    lb_all = jnp.cumsum(jax.nn.softmax(hg_lb.astype(jnp.float32), axis=0), axis=0)

    for l in range(DEPTH):
        h = rms_norm(x, norm_mix[l])
        proj = h @ w_in[l]
        hq, hf, hi, hog, dq, dk, dv, gate_hg, gate_da = jnp.split(proj, splits, axis=-1)

        lb = lb_all[l]
        f = lb + (1.0 - lb) * jax.nn.sigmoid(hf.astype(jnp.float32))
        heads_hg = lambda t: t.reshape(B, S, HG_HEADS, t.shape[-1] // HG_HEADS)
        o_hg = hgrn2_chunked(heads_hg(hq), heads_hg(1.0 - f), heads_hg(hi), heads_hg(jnp.log(f)))
        o_hg = rms_norm(o_hg, hg_out_norm[l]) * jax.nn.silu(heads_hg(hog).astype(jnp.float32))
        y_hg = o_hg.reshape(B, S, HG_WIDTH).astype(x.dtype) @ w_branch_hg[l]

        qn = rope(rms_norm(dq.reshape(B, S, 2 * DA_HEADS, DA_HEAD), da_q_norm[l]), pos)
        kn = rope(rms_norm(dk.reshape(B, S, 2 * DA_HEADS, DA_HEAD), da_k_norm[l]), pos)
        qn = qn.reshape(B, S, DA_HEADS, 2, DA_HEAD)
        kn = kn.reshape(B, S, DA_HEADS, 2, DA_HEAD)
        v = dv.reshape(B, S, DA_HEADS, DA_VDIM)
        lam_p = da_lambda[l].astype(jnp.float32)
        lam_init = 0.8 - 0.6 * math.exp(-0.3 * l)
        lam = jnp.exp(jnp.sum(lam_p[0] * lam_p[1])) - jnp.exp(jnp.sum(lam_p[2] * lam_p[3])) + lam_init
        o_da = diff_attention(qn[..., 0, :], qn[..., 1, :], kn[..., 0, :], kn[..., 1, :], v, lam)
        o_da = rms_norm(o_da, da_out_norm[l]) * (1.0 - lam_init)
        y_da = o_da.reshape(B, S, DA_WIDTH).astype(x.dtype) @ w_branch_da[l]

        mixed = jax.nn.sigmoid(gate_hg) * y_hg + jax.nn.sigmoid(gate_da) * y_da
        x = x + (mixed @ w_out[l]).astype(x.dtype)

        x = x + hier_moe(rms_norm(x, norm_moe[l]), w_router_group[l], b_router_group[l],
                         w_router_expert[l], b_router_expert[l], w1[l], w3[l], w2[l]).astype(x.dtype)
    return x


N_MEM = 256
RMS_EPS = 1e-6

RW_HEADS = 8
RW_HEAD_DIM = 64
RW_WIDTH = RW_HEADS * RW_HEAD_DIM
RW_DECAY_LORA = 64
RW_AAA_LORA = 64
RW_GATE_LORA = 128
RW_GN_EPS = 64e-5

DSA_HEADS = 8
DSA_HEAD_DIM = 64
DSA_WIDTH = DSA_HEADS * DSA_HEAD_DIM
DSA_KV_RANK = 128
IDX_HEADS = 4
IDX_DIM = 64
IDX_TOPK_MAX = 256

X_HEADS = 4
X_HEAD_DIM = 256
X_WIDTH = X_HEADS * X_HEAD_DIM

N_EXPERTS_2 = N_GROUPS * EXPERTS_PER_GROUP
TOP_K_INNER = 2
D_EXPERT = 512
MOE_BLOCK_2 = 256

RW_SIZES = (RW_WIDTH, RW_WIDTH, RW_WIDTH, RW_DECAY_LORA, RW_AAA_LORA, RW_GATE_LORA)
DSA_SIZES = (DSA_WIDTH, DSA_KV_RANK, IDX_HEADS * IDX_DIM, IDX_DIM, IDX_HEADS)
RW_COLS = sum(RW_SIZES)
DSA_COLS = sum(DSA_SIZES)
GATE_COLS = 2 * D_MODEL
IN_COLS_2 = RW_COLS + DSA_COLS + GATE_COLS


def _split(t, sizes):
    cuts = [int(c) for c in np.cumsum(sizes)[:-1]]
    return jnp.split(t, cuts, axis=-1)

def rmsnorm(x, g):
    xf = x.astype(jnp.float32)
    y = xf * lax.rsqrt(jnp.mean(xf * xf, axis=-1, keepdims=True) + RMS_EPS)
    return (y * g.astype(jnp.float32)).astype(x.dtype)

def rwkv7_branch(z, mu, w0, w2, a0, a2, g2, k_k, k_a, r_k, ln_w, ln_b):
    B, S, _ = z.shape
    H, N = RW_HEADS, RW_HEAD_DIM
    f32 = jnp.float32
    z_prev = jnp.pad(z, ((0, 0), (1, 0), (0, 0)))[:, :-1]
    z = z + (z_prev - z) * mu
    r, k, v, xw, xa, xg = _split(z, RW_SIZES)
    w = -jax.nn.softplus(-(w0 + jnp.tanh(xw) @ w2).astype(f32)) - 0.5
    decay = jnp.exp(-jnp.exp(w))
    a = jax.nn.sigmoid(a0 + xa @ a2)
    g = jax.nn.sigmoid(xg) @ g2
    heads = lambda t: t.astype(f32).reshape(B, S, H, N)
    kk = heads(k * k_k)
    kk = kk / jnp.maximum(jnp.sqrt(jnp.sum(kk * kk, -1, keepdims=True)), 1e-12)
    k = k * (1.0 + (a - 1.0) * k_a)
    r_h, k_h, v_h, a_h = heads(r), heads(k), heads(v), heads(a)
    seq_major = lambda t: jnp.moveaxis(t, 1, 0)
    xs = (seq_major(r_h), seq_major(heads(decay)), seq_major(k_h),
          seq_major(v_h), seq_major(kk), seq_major(a_h))

    def step(state, inp):
        r_t, w_t, k_t, v_t, kk_t, a_t = inp
        sa = jnp.einsum('bhij,bhj->bhi', state, -kk_t)
        state = (state * w_t[:, :, None, :]
                 + sa[..., None] * (kk_t * a_t)[:, :, None, :]
                 + v_t[..., None] * k_t[:, :, None, :])
        return state, jnp.einsum('bhij,bhj->bhi', state, r_t)

    _, y = lax.scan(step, jnp.zeros((B, H, N, N), f32), xs)
    y = jnp.moveaxis(y, 0, 1)
    mean = jnp.mean(y, -1, keepdims=True)
    var = jnp.mean(jnp.square(y - mean), -1, keepdims=True)
    y = ((y - mean) * lax.rsqrt(var + RW_GN_EPS)).reshape(B, S, RW_WIDTH)
    y = y * ln_w.astype(f32) + ln_b.astype(f32)
    bonus = jnp.sum(r_h * k_h * r_k.astype(f32), -1, keepdims=True) * v_h
    y = y + bonus.reshape(B, S, RW_WIDTH)
    return (y * g.astype(f32)).astype(z.dtype)

def dsa_branch(z, kv_norm, w_uk, w_uv):
    B, S, _ = z.shape
    f32 = jnp.float32
    k_sel = min(IDX_TOPK_MAX, S // 4)
    q, c_kv, q_idx, k_idx, w_idx = _split(z, DSA_SIZES)
    q = q.reshape(B, S, DSA_HEADS, DSA_HEAD_DIM)
    c_kv = rmsnorm(c_kv, kv_norm)
    q_lat = jnp.einsum('bshd,rhd->bshr', q, w_uk) * (DSA_HEAD_DIM ** -0.5)
    q_idx = q_idx.reshape(B, S, IDX_HEADS, IDX_DIM)
    w_idx = w_idx * ((IDX_HEADS * IDX_DIM) ** -0.5)
    nb = S // Q_BLOCK
    to_blocks = lambda t: jnp.moveaxis(t.reshape(B, nb, Q_BLOCK, *t.shape[2:]), 1, 0)
    key_pos = jnp.arange(S)

    def block(args):
        b, ql, qi, wi = args
        t_pos = b * Q_BLOCK + jnp.arange(Q_BLOCK)
        rel = jax.nn.relu(jnp.einsum('bqhd,bsd->bqhs', qi, k_idx).astype(f32))
        iscore = jnp.einsum('bqh,bqhs->bqs', wi.astype(f32), rel)
        causal = key_pos[None, :] <= t_pos[:, None]
        iscore = jnp.where(causal[None], iscore, -jnp.inf)
        _, idx = lax.top_k(iscore, k_sel)
        valid = idx <= t_pos[None, :, None]
        c_sel = jax.vmap(lambda c, i: c[i])(c_kv, idx)
        s = jnp.einsum('bqhr,bqkr->bhqk', ql, c_sel).astype(f32)
        s = jnp.where(valid[:, None], s, -jnp.inf)
        p = jax.nn.softmax(s, axis=-1).astype(c_sel.dtype)
        o_lat = jnp.einsum('bhqk,bqkr->bqhr', p, c_sel)
        return jnp.einsum('bqhr,rhd->bqhd', o_lat, w_uv)

    o = lax.map(block, (jnp.arange(nb), to_blocks(q_lat), to_blocks(q_idx), to_blocks(w_idx)))
    return jnp.moveaxis(o, 0, 1).reshape(B, S, DSA_WIDTH)

def cross_attention(hn, mem_n, w_cq, w_ckv, w_co):
    B, S, _ = hn.shape
    M = mem_n.shape[1]
    q = (hn @ w_cq).reshape(B, S, X_HEADS, X_HEAD_DIM)
    k, v = jnp.split((mem_n @ w_ckv).reshape(B, M, 2, X_HEADS, X_HEAD_DIM), 2, axis=2)
    k, v = k[:, :, 0], v[:, :, 0]
    s = jnp.einsum('bshd,bmhd->bhsm', q, k).astype(jnp.float32) * (X_HEAD_DIM ** -0.5)
    p = jax.nn.softmax(s, axis=-1).astype(v.dtype)
    o = jnp.einsum('bhsm,bmhd->bshd', p, v).reshape(B, S, X_WIDTH)
    return o @ w_co

def hier_moe_2(hn, w_rg, b_rg, w_re, b_re, w_gate, w_up, w_down):
    B, S, D = hn.shape
    T = B * S
    xt = hn.reshape(T, D)
    g_prob = jax.nn.softmax((xt @ w_rg + b_rg).astype(jnp.float32), axis=-1)
    p_grp, grp = lax.top_k(g_prob, 1)
    e_logits = (xt @ w_re + b_re).astype(jnp.float32).reshape(T, N_GROUPS, EXPERTS_PER_GROUP)
    e_logits = jnp.take_along_axis(e_logits, grp[:, :, None], axis=1)[:, 0]
    p_e, e_loc = lax.top_k(jax.nn.softmax(e_logits, axis=-1), TOP_K_INNER)
    gate = p_grp * p_e / jnp.sum(p_e, -1, keepdims=True)
    expert = grp * EXPERTS_PER_GROUP + e_loc
    A = T * TOP_K_INNER
    e_flat = expert.reshape(A)
    tok_flat = jnp.repeat(jnp.arange(T, dtype=jnp.int32), TOP_K_INNER)
    g_flat = gate.reshape(A)
    order = jnp.argsort(e_flat)
    e_sorted = e_flat[order]
    counts = jnp.bincount(e_flat, length=N_EXPERTS_2)
    start = jnp.cumsum(counts) - counts
    padded = (counts + MOE_BLOCK_2 - 1) // MOE_BLOCK_2 * MOE_BLOCK_2
    pend = jnp.cumsum(padded)
    pstart = pend - padded
    dest = pstart[e_sorted] + (jnp.arange(A) - start[e_sorted])
    P = A + N_EXPERTS_2 * MOE_BLOCK_2
    buf_tok = jnp.full((P,), T, jnp.int32).at[dest].set(tok_flat[order])
    buf_gate = jnp.zeros((P,), jnp.float32).at[dest].set(g_flat[order])
    n_blocks = P // MOE_BLOCK_2
    blk_expert = jnp.minimum(
        jnp.searchsorted(pend, jnp.arange(n_blocks) * MOE_BLOCK_2, side='right'), N_EXPERTS_2 - 1)
    x_pad = jnp.concatenate([xt, jnp.zeros((1, D), xt.dtype)], axis=0)

    def run_block(args):
        e, toks, gts = args
        xb = x_pad[toks]
        hid = jax.nn.silu(xb @ w_gate[e]) * (xb @ w_up[e])
        return (hid @ w_down[e]) * gts[:, None].astype(xb.dtype)

    yb = lax.map(run_block, (blk_expert, buf_tok.reshape(n_blocks, MOE_BLOCK_2),
                             buf_gate.reshape(n_blocks, MOE_BLOCK_2)))
    y = jnp.zeros((T + 1, D), hn.dtype).at[buf_tok].add(yb.reshape(P, D))[:T]
    return y.reshape(B, S, D)

def hybrid_layer(h, mem, norm_mix, w_in, shift_mu, rw_w0, rw_w2, rw_a0, rw_a2, rw_g2,
                 rw_k_k, rw_k_a, rw_r_k, rw_ln_w, rw_ln_b, kv_norm, w_uk, w_uv,
                 w_proj_a, w_proj_b, b_gate, w_out, norm_cross, norm_mem, w_cq, w_ckv, w_co,
                 norm_ffn, w_router_g, b_router_g, w_router_e, b_router_e,
                 w_e_gate, w_e_up, w_e_down):
    z = rmsnorm(h, norm_mix) @ w_in
    z_rw, z_dsa, z_gate = _split(z, (RW_COLS, DSA_COLS, GATE_COLS))
    y_a = rwkv7_branch(z_rw, shift_mu, rw_w0, rw_w2, rw_a0, rw_a2, rw_g2,
                       rw_k_k, rw_k_a, rw_r_k, rw_ln_w, rw_ln_b)
    y_b = dsa_branch(z_dsa, kv_norm, w_uk, w_uv)
    g_a, g_b = jnp.split(jax.nn.sigmoid(z_gate + b_gate), 2, axis=-1)
    h = h + (g_a * (y_a @ w_proj_a) + g_b * (y_b @ w_proj_b)) @ w_out
    h = h + cross_attention(rmsnorm(h, norm_cross), rmsnorm(mem, norm_mem), w_cq, w_ckv, w_co)
    h = h + hier_moe_2(rmsnorm(h, norm_ffn), w_router_g, b_router_g, w_router_e, b_router_e,
                     w_e_gate, w_e_up, w_e_down)
    return h

def second_inputs(seed: int = 0) -> dict:
    key = jax.random.key(seed)
    ks = iter(jax.random.split(key, 48))
    f32 = jnp.float32
    L = DEPTH

    def nrm(shape, scale):
        return jax.random.normal(next(ks), shape, f32) * scale

    def gain(shape):
        return 1.0 + nrm(shape, 0.02)

    return {
        'x': nrm((BATCH, SEQ, D_MODEL), 1.0),
        'mem': nrm((BATCH, N_MEM, D_MODEL), 1.0),
        'norm_mix': gain((L, D_MODEL)),
        'w_in': nrm((L, D_MODEL, IN_COLS_2), D_MODEL ** -0.5),
        'shift_mu': jax.random.uniform(next(ks), (L, RW_COLS), f32),
        'rw_w0': jax.random.uniform(next(ks), (L, RW_WIDTH), f32, -5.0, 1.0),
        'rw_w2': nrm((L, RW_DECAY_LORA, RW_WIDTH), 0.1 * RW_DECAY_LORA ** -0.5),
        'rw_a0': nrm((L, RW_WIDTH), 0.1),
        'rw_a2': nrm((L, RW_AAA_LORA, RW_WIDTH), 0.1 * RW_AAA_LORA ** -0.5),
        'rw_g2': nrm((L, RW_GATE_LORA, RW_WIDTH), RW_GATE_LORA ** -0.5),
        'rw_k_k': 0.85 + nrm((L, RW_WIDTH), 0.02),
        'rw_k_a': gain((L, RW_WIDTH)),
        'rw_r_k': nrm((L, RW_HEADS, RW_HEAD_DIM), 0.1),
        'rw_ln_w': gain((L, RW_WIDTH)),
        'rw_ln_b': nrm((L, RW_WIDTH), 0.01),
        'kv_norm': gain((L, DSA_KV_RANK)),
        'w_uk': nrm((L, DSA_KV_RANK, DSA_HEADS, DSA_HEAD_DIM), DSA_KV_RANK ** -0.5),
        'w_uv': nrm((L, DSA_KV_RANK, DSA_HEADS, DSA_HEAD_DIM), DSA_KV_RANK ** -0.5),
        'w_proj_a': nrm((L, RW_WIDTH, D_MODEL), RW_WIDTH ** -0.5),
        'w_proj_b': nrm((L, DSA_WIDTH, D_MODEL), DSA_WIDTH ** -0.5),
        'b_gate': nrm((L, GATE_COLS), 0.01),
        'w_out': nrm((L, D_MODEL, D_MODEL), D_MODEL ** -0.5),
        'norm_cross': gain((L, D_MODEL)),
        'norm_mem': gain((L, D_MODEL)),
        'w_cq': nrm((L, D_MODEL, X_WIDTH), D_MODEL ** -0.5),
        'w_ckv': nrm((L, D_MODEL, 2 * X_WIDTH), D_MODEL ** -0.5),
        'w_co': nrm((L, X_WIDTH, D_MODEL), X_WIDTH ** -0.5),
        'norm_ffn': gain((L, D_MODEL)),
        'w_router_g': nrm((L, D_MODEL, N_GROUPS), D_MODEL ** -0.5),
        'b_router_g': nrm((L, N_GROUPS), 0.01),
        'w_router_e': nrm((L, D_MODEL, N_EXPERTS_2), D_MODEL ** -0.5),
        'b_router_e': nrm((L, N_EXPERTS_2), 0.01),
        'w_e_gate': nrm((L, N_EXPERTS_2, D_MODEL, D_EXPERT), D_MODEL ** -0.5),
        'w_e_up': nrm((L, N_EXPERTS_2, D_MODEL, D_EXPERT), D_MODEL ** -0.5),
        'w_e_down': nrm((L, N_EXPERTS_2, D_EXPERT, D_MODEL), D_EXPERT ** -0.5),
        'norm_final': gain((D_MODEL,)),
    }

def second_block(x, mem, norm_mix, w_in, shift_mu, rw_w0, rw_w2, rw_a0, rw_a2, rw_g2,
              rw_k_k, rw_k_a, rw_r_k, rw_ln_w, rw_ln_b, kv_norm, w_uk, w_uv,
              w_proj_a, w_proj_b, b_gate, w_out, norm_cross, norm_mem, w_cq, w_ckv, w_co,
              norm_ffn, w_router_g, b_router_g, w_router_e, b_router_e,
              w_e_gate, w_e_up, w_e_down, norm_final):
    h = x
    for l in range(DEPTH):
        h = hybrid_layer(h, mem, norm_mix[l], w_in[l], shift_mu[l], rw_w0[l], rw_w2[l],
                         rw_a0[l], rw_a2[l], rw_g2[l], rw_k_k[l], rw_k_a[l], rw_r_k[l],
                         rw_ln_w[l], rw_ln_b[l], kv_norm[l], w_uk[l], w_uv[l],
                         w_proj_a[l], w_proj_b[l], b_gate[l], w_out[l],
                         norm_cross[l], norm_mem[l], w_cq[l], w_ckv[l], w_co[l],
                         norm_ffn[l], w_router_g[l], b_router_g[l], w_router_e[l], b_router_e[l],
                         w_e_gate[l], w_e_up[l], w_e_down[l])
    return rmsnorm(h, norm_final)


def setup_inputs(seed=0):
    out = dict(first_inputs(seed))
    for name, value in second_inputs(seed + 1).items():
        if name != "x":
            out[name + "_2"] = value
    return out


def reference(
    x, norm_mix, w_in, hg_lb, hg_out_norm, da_q_norm, da_k_norm, da_lambda, da_out_norm,
    w_branch_hg, w_branch_da, w_out, norm_moe, w_router_group, b_router_group, w_router_expert,
    b_router_expert, w1, w3, w2, mem_2, norm_mix_2, w_in_2, shift_mu_2, rw_w0_2, rw_w2_2,
    rw_a0_2, rw_a2_2, rw_g2_2, rw_k_k_2, rw_k_a_2, rw_r_k_2, rw_ln_w_2, rw_ln_b_2, kv_norm_2,
    w_uk_2, w_uv_2, w_proj_a_2, w_proj_b_2, b_gate_2, w_out_2, norm_cross_2, norm_mem_2, w_cq_2,
    w_ckv_2, w_co_2, norm_ffn_2, w_router_g_2, b_router_g_2, w_router_e_2, b_router_e_2,
    w_e_gate_2, w_e_up_2, w_e_down_2, norm_final_2,
):
    x = first_block(
        x, norm_mix, w_in, hg_lb, hg_out_norm, da_q_norm, da_k_norm, da_lambda, da_out_norm,
        w_branch_hg, w_branch_da, w_out, norm_moe, w_router_group, b_router_group,
        w_router_expert, b_router_expert, w1, w3, w2,
    )
    return second_block(
        x, mem_2, norm_mix_2, w_in_2, shift_mu_2, rw_w0_2, rw_w2_2, rw_a0_2, rw_a2_2, rw_g2_2,
        rw_k_k_2, rw_k_a_2, rw_r_k_2, rw_ln_w_2, rw_ln_b_2, kv_norm_2, w_uk_2, w_uv_2,
        w_proj_a_2, w_proj_b_2, b_gate_2, w_out_2, norm_cross_2, norm_mem_2, w_cq_2, w_ckv_2,
        w_co_2, norm_ffn_2, w_router_g_2, b_router_g_2, w_router_e_2, b_router_e_2, w_e_gate_2,
        w_e_up_2, w_e_down_2, norm_final_2,
    )


_drawn_inputs = setup_inputs


def setup_inputs(seed=0):
    import zlib

    import numpy as np

    out = dict(_drawn_inputs(seed))
    spreads = {}
    factors = {'rw_w2_2': 5.525,
     'rw_a0_2': 3.102,
     'rw_k_k_2': 4.039,
     'rw_k_a_2': 3.235,
     'rw_ln_w_2': 3.67,
     'rw_ln_b_2': 5.35,
     'kv_norm_2': 5.374,
     'b_gate_2': 8.0,
     'norm_cross_2': 6.153,
     'norm_mem_2': 7.185,
     'b_router_g_2': 50.6,
     'b_router_e_2': 31.152,
     'norm_final_2': 7.755,
     'norm_ffn_2': 8.0}
    for name, (base, spread) in spreads.items():
        noise = np.random.default_rng([zlib.crc32(name.encode()), seed]).standard_normal(out[name].shape)
        drawn = base * np.exp(spread * noise) if base else spread * noise
        out[name] = jnp.asarray(drawn.astype(out[name].dtype))
    for name, factor in factors.items():
        out[name] = (out[name] * factor).astype(out[name].dtype)
    return out
```

```python
import math
from contextlib import ExitStack

import numpy as np
import concourse.bass as bass
from concourse import mybir

F = mybir.dt.float32
I32 = mybir.dt.int32
U32 = mybir.dt.uint32
A = mybir.AluOpType
AF = mybir.ActivationFunctionType
AX = mybir.AxisListType.X
ENG = ("sp", "act", "dve", "pool", "pe")

T = 512
NT = 4
D = 1024
NEG = -1.0e30
CAP = 64
NE = 32
NOV = 16
NRING = 4
NSC = 12
LAM_INIT = 0.8 - 0.6 * math.exp(0.0)


class Prog:

    def __init__(self, nc, ctx, tag):
        self.nc = nc
        self.q = {e: [] for e in ENG}
        self.sem = {e: ctx.enter_context(nc.semaphore(f"{tag}_{e}")) for e in ENG if e != "sp"}
        self.sems = dict(self.sem)
        self.n = {}
        self.tag = tag
        self.ctx = ctx

    def flat(self, deps, out):
        for d in deps:
            if d is None:
                continue
            if isinstance(d, list):
                self.flat(d, out)
            else:
                out.append(d)
        return out

    def count(self, name, by):
        self.n[name] = self.n.get(name, 0) + by
        return (name, self.n[name])

    def now(self, *engs):
        return [(e, self.n[e]) for e in (engs or ("act", "dve", "pool", "pe")) if self.n.get(e)]

    def op(self, eng, fn, *deps):
        deps = self.flat(deps, [])
        if eng != "pe" and self.n.get(eng):
            deps.append((eng, self.n[eng]))
        tok = self.count(eng, 1)
        self.q[eng].append((deps, fn, eng, 1))
        return tok

    def dve(self, fn, *deps):
        return self.op("dve", fn, *deps)

    def act(self, fn, *deps):
        return self.op("act", fn, *deps)

    def pool(self, fn, *deps):
        return self.op("pool", fn, *deps)

    def pe(self, fns, *deps):
        def run(e):
            for f in fns:
                last = f(e)
            return last
        return self.op("pe", run, *deps)

    def dma(self, eng, fn, sem, *deps):
        if sem not in self.sems:
            self.sems[sem] = self.ctx.enter_context(self.nc.semaphore(f"{self.tag}_{sem}"))
        tok = self.count(sem, 16)
        self.q[eng].append((self.flat(deps, []), fn, sem, 16))
        return tok

    def raw(self, eng, fn, *deps):
        self.q[eng].append((self.flat(deps, []), fn, None, 0))

    def emit(self, eng, e, start=0, end=None, seen=None):
        seen = {} if seen is None else seen
        for deps, fn, sem, by in self.q[eng][start:end]:
            for name, val in deps:
                if seen.get(name, 0) < val:
                    e.wait_ge(self.sems[name], val)
                    seen[name] = val
            ins = fn(e)
            if sem is not None:
                ins.then_inc(self.sems[sem], by)


def mm(out, l, r, st, sp):
    return lambda e: e.matmul(out, l, r, start=st, stop=sp, skip_group_check=True)


def tr(out, in_, ident):
    return lambda e: e.transpose(out, in_, ident)


PARAMS = [("norm_mix", 8), ("hg_lb", 8), ("hg_out_norm", 1), ("da_out_norm", 1), ("norm_mix_2", 8),
          ("shift_mu_2", 14), ("rw_w0_2", 4), ("rw_a0_2", 4), ("rw_k_k_2", 4), ("rw_k_a_2", 4),
          ("rw_r_k_2", 4), ("rw_ln_w_2", 4), ("rw_ln_b_2", 4), ("b_gate_2", 16),
          ("norm_cross_2", 8), ("norm_mem_2", 8), ("kv_norm_2", 1)]


def program(nc, t, out, dbg):
    with ExitStack() as ctx:
        build(nc, ctx, t, out, dbg)


def build(nc, ctx, t, out, dbg):
    P = Prog(nc, ctx, "m")

    def sb(name, shape, dt=F):
        return ctx.enter_context(nc.sbuf_tensor(name, shape, dt))

    X = sb("X", [128, NT, D])
    XT = sb("XT", [128, 8, T])
    RING = sb("RING", [128, NRING, 4096])
    SC = sb("SC", [128, NSC, 2048])
    ST = sb("ST", [128, 1400])
    PR = SC[:, NSC - 1, 0:128]
    PC = sb("PC", [128, 128])
    ident = sb("ident", [128, 128])
    CH = sb("CH", [128, T])
    mk = sb("mk", [128, 4, 128], mybir.dt.int8)
    mband = sb("mband", [128, 6, 128], mybir.dt.int8)
    diagm = sb("diagm", [128, 128])
    PS = [ctx.enter_context(nc.psum_tensor(f"ps{i}", [128, 512], F)) for i in range(8)]
    ytab = nc.dram_tensor("ytab", [2 * T, D], F, kind="Internal").ap()
    xrows = nc.dram_tensor("xrows", [T, D], F, kind="Internal").ap()
    tabs = [nc.dram_tensor(f"tab{i}", [(NE + NOV) * CAP, 1], I32, kind="Internal").ap() for i in range(2)]

    stn = [0]

    def st(n):
        a = ST[:, stn[0]:stn[0] + n]
        stn[0] += n
        assert stn[0] <= 1400, stn
        return a

    bank_no = [0]
    bank_free = [[] for _ in range(8)]

    def bank():
        while bank_free[bank_no[0] % 8] is None:
            bank_no[0] += 1
        i = bank_no[0] % 8
        bank_no[0] += 1
        free = bank_free[i]
        bank_free[i] = None
        return i, PS[i], free

    def done(i, *toks):
        bank_free[i] = list(toks)

    ring_no = [0]
    slots = [RING[:, i, :] for i in range(NRING)]
    ring_free = [[] for _ in range(NRING)]

    def unit(srcs):
        i = ring_no[0] % len(slots)
        ring_no[0] += 1
        slot = slots[i]
        free = ring_free[i]
        assert free is not None
        ring_free[i] = None
        tok = None
        for dst, src in srcs:
            tok = P.dma("sp", (lambda d, s: lambda e: e.dma_start(d, s))(dst(slot), src), f"ring{i}", free)
        return i, slot, tok

    def unit_done(i, *toks):
        ring_free[i] = list(toks)

    def wcols(w, c0, n):
        return unit([(lambda s: s[:, 0:8 * n].rearrange("p (k n) -> p k n", k=8),
                      w.rearrange("(k p) n -> p k n", p=128)[:, :, c0:c0 + n])])

    flip = [0]

    def evac(dst, src, *deps, scale=None):
        flip[0] += 1
        if flip[0] % 2:
            if scale is None:
                return P.act(lambda e: e.activation(dst, src, AF.Copy), *deps)
            return P.act(lambda e: e.activation(dst, src, AF.Identity, scale=scale), *deps)
        if scale is None:
            return P.dve(lambda e: e.tensor_copy(dst, src), *deps)
        return P.dve(lambda e: e.tensor_scalar(dst, src, scale, None, A.mult), *deps)

    def rsq(src, n, scale, eps, *deps):
        a, y, u = st(n), st(n), st(n)
        t0 = P.dve(lambda e: e.tensor_scalar(a, src, scale, eps, A.mult, A.add), *deps)
        t1 = P.act(lambda e: e.activation(y, a, AF.Ln), t0)
        t1 = P.act(lambda e: e.activation(y, y, AF.Exp, scale=-0.5), t1)
        P.dve(lambda e: e.scalar_tensor_tensor(u, y, -0.5, y, A.mult, A.mult), t1)
        P.dve(lambda e: e.tensor_tensor(u, u, a, A.mult))
        return y, P.dve(lambda e: e.scalar_tensor_tensor(y, u, 1.5, y, A.add, A.mult))

    ld = []
    for tt in range(NT):
        ld.append(P.dma("act", (lambda tt: lambda e: e.dma_start(X[:, tt, :], t["x"][0, tt * 128:(tt + 1) * 128, :]))(tt), "x"))
    x_in = ld[-1]
    col = {}
    row = 0
    for name, n in PARAMS:
        v = t[name]
        if name == "rw_r_k_2":
            v = v.rearrange("l h n -> l (h n)")
        v = v.rearrange("l n -> (l n)") if len(v.shape) == 2 else v
        tok = P.dma("act", (lambda v, row, n: lambda e: e.dma_start(PR[row:row + n, :], v.rearrange("(a b) -> a b", b=128)))(v, row, n), "par")
        col[name] = row
        row += n
    NPR = row
    G64 = sb("G64", [128, 2, 64])
    LAMP = sb("LAMP", [128, 256])
    ROPE = sb("ROPE", [128, 2, NT, 32])
    RB = sb("RB", [128, 2, 36])
    WR = sb("WR", [128, 2, 8, 36])
    tok = P.dma("act", lambda e: e.dma_start(G64[:, 0, :], t["da_q_norm"].to_broadcast([128, 64])), "par")
    tok = P.dma("act", lambda e: e.dma_start(G64[:, 1, :], t["da_k_norm"].to_broadcast([128, 64])), "par")
    tok = P.dma("act", lambda e: e.dma_start(LAMP[:, :], t["da_lambda"].rearrange("l a b -> l (a b)").to_broadcast([128, 256])), "par")
    tok = P.dma("act", lambda e: e.dma_start(ROPE[:, 0, :, :], t["rope_cos"].rearrange("(t p) n -> p t n", p=128)), "par")
    tok = P.dma("act", lambda e: e.dma_start(ROPE[:, 1, :, :], t["rope_sin"].rearrange("(t p) n -> p t n", p=128)), "par")
    for b, (g, e_) in enumerate((("router_group", "router_expert"), ("router_g_2", "router_e_2"))):
        tok = P.dma("act", (lambda b, g: lambda e: e.dma_start(RB[:, b, 0:4], t["b_" + g].to_broadcast([128, 4])))(b, g), "par")
        tok = P.dma("act", (lambda b, g: lambda e: e.dma_start(RB[:, b, 4:36], t["b_" + g].to_broadcast([128, 32])))(b, e_), "par")
        tok = P.dma("act", (lambda b, g: lambda e: e.dma_start(WR[:, b, :, 0:4], t["w_" + g][0].rearrange("(k p) n -> p k n", p=128)))(b, g), "par")
        tok = P.dma("act", (lambda b, g: lambda e: e.dma_start(WR[:, b, :, 4:36], t["w_" + g][0].rearrange("(k p) n -> p k n", p=128)))(b, e_), "par")
    par = tok

    ones = sb("ones", [128, 128])
    upper = sb("upper", [128, 128])
    BO = sb("BO", [128, 128])
    iotf = sb("iotf", [128, 40])
    iotm = sb("iotm", [128, 8])
    ival = sb("ival", [128, 2, NT], I32)
    tmpm = SC[:, NSC - 2, 0:1024]
    P.pool(lambda e: e.memset(ones[:, :], 1.0))

    def sel(dst, src, pattern, op, fill, base, cm):
        return P.pool(lambda e: e.affine_select(out=dst, in_=src, pattern=pattern, compare_op=op, fill=fill, base=base, channel_multiplier=cm))

    P.pool(lambda e: e.memset(ident[:, :], 0.0))
    sel(ident[:, :], ident[:, :], [[-1, 128]], A.not_equal, 1.0, 0, 1)
    sel(upper[:, :], ones[:, :], [[1, 128]], A.is_gt, 0.0, 0, -1)
    P.pool(lambda e: e.memset(diagm[:, :], 0.0))
    sel(diagm[:, :], diagm[:, :], [[-1, 128]], A.is_ge, NEG, 0, 1)
    P.pool(lambda e: e.memset(BO[:, :], 0.0))
    P.pool(lambda e: e.memset(BO[0:64, 0:64], 1.0))
    P.pool(lambda e: e.memset(BO[64:128, 64:128], 1.0))
    P.pool(lambda e: e.memset(CH[:, :], 1.0))
    P.pool(lambda e: e.memset(CH[:, :].rearrange("p (c j) -> p c j", j=64)[:, :, 0], 0.0))
    P.pool(lambda e: e.iota(iotf[:, :], [[1, 40]], base=0, channel_multiplier=0, allow_small_or_imprecise_dtypes=True))
    P.pool(lambda e: e.iota(iotm[:, :], [[1, 8]], base=-8, channel_multiplier=0, allow_small_or_imprecise_dtypes=True))
    for k in range(2):
        P.pool((lambda k: lambda e: e.iota(ival[:, k, :], [[256, NT]], base=k, channel_multiplier=2))(k))
    m0, m1, m16, m32 = (tmpm[:, 128 * i:128 * (i + 1)] for i in range(4))
    BOv = BO[:, :]

    def blocks(dst, size):
        v = dst.rearrange("p (a b) -> p a b", b=size)
        sel(v, ones[:, :].rearrange("p (a b) -> p a b", b=size), [[-size, 128 // size], [0, size]], A.is_ge, 0.0, 0, 1)
        sel(v, v, [[size, 128 // size], [0, size]], A.is_ge, 0.0, size - 1, -1)

    blocks(m16, 16)
    blocks(m32, 32)
    u = tmpm[:, 512:640]
    w = tmpm[:, 640:768]
    lower = tmpm[:, 768:896]
    sel(lower, ones[:, :], [[-1, 128]], A.is_gt, 0.0, 0, 1)
    sel(m0, BOv, [[1, 128]], A.is_ge, 0.0, 0, -1)
    tk = P.pool(lambda e: e.tensor_copy(mk[:, 0, :], m0))

    def band(i, tri, hi, lo):
        P.pool(lambda e: e.tensor_tensor(u, tri, hi, A.mult))
        if lo is not None:
            P.pool(lambda e: e.tensor_tensor(w, u, lo, A.mult))
            P.pool(lambda e: e.tensor_tensor(u, u, w, A.subtract))
        return P.pool(lambda e: e.tensor_copy(mband[:, i, :], u))

    band(0, upper[:, :], m16, None)
    band(1, lower, m16, None)
    band(2, upper[:, :], m32, m16)
    band(3, lower, m32, m16)
    band(4, lower, BOv, m32)
    cst = band(5, upper[:, :], BOv, None)

    i, b, fr = bank()
    tk = P.pe([tr(b[:, 0:NPR], PR[0:NPR, :], ident[0:NPR, 0:NPR])], cst, par)
    pc = P.dve(lambda e: e.tensor_copy(PC[:, 0:NPR], b[:, 0:NPR]), tk)
    done(i, pc)

    def pcol(name, j=0):
        c = col[name] + j
        return PC[:, c:c + 1]

    def pcols(name, n):
        return PC[:, col[name]:col[name] + n]

    def scv(i, a, n=1):
        v = SC[:, i:i + n, :].rearrange("p s b -> p (s b)")
        return v.rearrange("p (a b) -> p a b", a=a)

    def rms(src, nt, n, *deps):
        ss = st(nt)
        junk = SC[:, NSC - 1, 0:n]
        for i in range(nt):
            tk = P.act((lambda i: lambda e: e.activation(junk, src[:, i, :], AF.Square, accum_out=ss[:, i:i + 1]))(i), *deps)
        return rsq(ss, nt, 1.0 / n, 1e-6, tk)

    def to_xt(src, nt, rs, rtok, gain, dst, xn, free):
        tk = None
        for i in range(nt):
            tk = P.dve((lambda i: lambda e: e.tensor_scalar(xn[:, i, :], src[:, i, :], rs[:, i:i + 1], None, A.mult))(i), rtok, free)
        return transposed(xn, nt, gain, dst, tk, free)

    def transposed(xn, nt, gain, dst, tk, free):
        out_ = []
        for k in range(8):
            i, b, fr = bank()
            t1 = P.pe([tr(b[:, j * 128:(j + 1) * 128], xn[:, j, k * 128:(k + 1) * 128], ident[:, :]) for j in range(nt)], tk, fr, cst)
            t2 = evac(dst[:, k, :], b[:, 0:nt * 128], t1, free, pc, scale=None if gain is None else gain[:, k:k + 1])
            done(i, t2)
            out_.append(t2)
        return out_[-2:]

    def proj_f(wv, c, n, rhs, nk, *deps, at=0, bk=None):
        if bk is None:
            bk = bank()
        i, b, fr = bk
        N = rhs.shape[-1]
        tk = P.pe([mm(b[at:at + n, 0:N], wv[:, k, c:c + n], rhs[:, k, :], k == 0, k == nk - 1) for k in range(nk)], fr, *deps)
        return i, b, tk

    def proj_t(wv, c, n, lhs, tt, nk, *deps):
        i, b, fr = bank()
        tk = P.pe([mm(b[:, 0:n], lhs[:, k, tt * 128:(tt + 1) * 128], wv[:, k, c:c + n], k == 0, k == nk - 1) for k in range(nk)], fr, *deps)
        return i, b, tk

    def gated(wgate, gcol0, wa, ya, ya_t, wb, yb, yb_t, bias, wout, xtt, mbuf, tmp, free):
        E, Y = tmp
        last = [free] * 2
        for br, (w_, y, yt) in enumerate(((wa, ya, ya_t), (wb, yb, yb_t))):
            wu, ws, wt = unit([(lambda s: s.rearrange("p (k n) -> p k n", k=4), w_.rearrange("(k p) n -> p k n", p=128))])
            wv = ws.rearrange("p (k n) -> p k n", k=4)
            for half in range(2):
                gu, gs, gt = wcols(wgate, gcol0 + br * 1024 + half * 512, 512)
                gv = gs.rearrange("p (k n) -> p k n", k=8)
                for j in range(4):
                    dt_ = half * 4 + j
                    s_ = dt_ % 2
                    e_, y_ = E[s_], Y[s_]
                    i, b, tk = proj_f(gv, j * 128, 128, XT, 8, gt, xtt)
                    nb = None if bias is None else bias[:, br * 8 + dt_:br * 8 + dt_ + 1]
                    ta = P.act((lambda e_, b, nb: lambda e: e.activation(e_, b[:, :], AF.Exp, scale=-1.0, **({} if nb is None else {"bias": nb})))(e_, b, nb), tk, last[s_])
                    done(i, ta)
                    P.dve((lambda e_: lambda e: e.tensor_scalar(e_, e_, 1.0, None, A.add))(e_), ta)
                    P.dve((lambda e_: lambda e: e.reciprocal(e_, e_))(e_))
                    i2, b2, tk2 = proj_f(wv, dt_ * 128, 128, y, 4, wt, yt)
                    dst = mbuf[:, dt_, :] if br == 0 else y_
                    tv = P.dve((lambda dst, e_, b2: lambda e: e.tensor_tensor(dst, e_, b2[:, :], A.mult))(dst, e_, b2), tk2, free)
                    done(i2, tv)
                    last[s_] = tv
                    if br == 1:
                        tv = last[s_] = P.dve((lambda m, y_: lambda e: e.tensor_tensor(m, m, y_, A.add))(mbuf[:, dt_, :], y_))
                unit_done(gu, tk)
            unit_done(wu, tk2)
        return add_proj(wout, mbuf, tv)

    def add_proj(wout, src, tv):
        for half in range(2):
            u_, s_, wt = wcols(wout, half * 512, 512)
            v = s_.rearrange("p (k n) -> p k n", k=8)
            for tt in range(NT):
                i, b, tk = proj_t(v, 0, 512, src, tt, 8, wt, tv)
                xs = X[:, tt, half * 512:(half + 1) * 512]
                tx = P.dve((lambda xs, b: lambda e: e.tensor_tensor(xs, xs, b[:, :], A.add))(xs, b), tk)
                done(i, tx)
            unit_done(u_, tk)
        return tx


    def heads_out(o, tok, n, gain, dst, const, free, mul=None, bias=None):
        ss = st(16)
        junk = SC[:, NSC - 1, 0:2048]
        t1 = P.act(lambda e: e.activation(junk, o.rearrange("p a b -> p (a b)"), AF.Square), tok)
        t2 = P.dve(lambda e: e.tensor_reduce(ss, junk.rearrange("p (a b) -> p a b", b=128), AX, A.add), t1)
        rs, t3 = rsq(ss, 16, 1.0 / 128, 1e-6, t2)
        ov = o.rearrange("p a (h b) -> p (a h) b", b=128)
        t4 = P.dve(lambda e: e.tensor_tensor(ov, ov, rs.unsqueeze(2).to_broadcast([128, 16, 128]), A.mult), t3)
        if mul is not None:
            t4 = P.dve(lambda e: e.tensor_tensor(o, o, mul, A.mult))
        g = st(1)
        t5 = P.dve(lambda e: e.tensor_scalar(g, gain, const, None, A.mult), pc)
        outs = []
        for h in range(4):
            i, b, fr = bank()
            t6 = P.pe([tr(b[:, j * 128:(j + 1) * 128], o[:, j, h * 128:(h + 1) * 128], ident[:, :]) for j in range(NT)], t4, fr)
            t7 = evac(dst[:, h, :], b[:, :], t6, t5, free, scale=g)
            done(i, t7)
            outs.append(t7)
        return outs[-2:]

    def block1_mix():
        rs, rt = rms(X, NT, D, x_in, pc)
        xn = scv(8, 4, 2)
        xtt = to_xt(X, NT, rs, rt, pcols("norm_mix", 8), XT, xn, cst)
        keep["xt1"] = xtt
        w_in = t["w_in"][0]
        q, k, b_, qr, kr, v, og, kt, o, E = (scv(i, 4) for i in (0, 1, 2, 3, 4, 5, 6, 7, 8, 9))
        SB = scv(10, 4)
        lb, oml, l1, l2 = st(4), st(4), st(4), st(4)
        a0, a1 = pcols("hg_lb", 8)[:, 0:4], pcols("hg_lb", 8)[:, 4:8]
        P.dve(lambda e: e.tensor_tensor(lb, a0, a1, A.max))
        P.dve(lambda e: e.tensor_tensor(l1, a0, lb, A.subtract))
        t1 = P.dve(lambda e: e.tensor_tensor(l2, a1, lb, A.subtract))
        P.act(lambda e: e.activation(l1, l1, AF.Exp), t1)
        t1 = P.act(lambda e: e.activation(l2, l2, AF.Exp))
        P.dve(lambda e: e.tensor_tensor(l2, l1, l2, A.add), t1)
        P.dve(lambda e: e.reciprocal(l2, l2))
        P.dve(lambda e: e.tensor_tensor(lb, l1, l2, A.mult))
        P.dve(lambda e: e.tensor_scalar(oml, lb, -1.0, 1.0, A.mult, A.add))

        u_, s_, ut = wcols(w_in, 0, 512)
        wv = s_.rearrange("p (k n) -> p k n", k=8)
        for h in range(4):
            i, b, tk = proj_f(wv, h * 128, 128, XT, 8, ut, xtt)
            tq = evac(q[:, h, :], b[:, :], tk)
            done(i, tq)
        unit_done(u_, tk)
        qdone = P.now("act", "dve")
        u_, s_, ut = wcols(w_in, 512, 512)
        wv2 = s_.rearrange("p (k n) -> p k n", k=8)
        for h in range(4):
            i, b, tk = proj_f(wv2, h * 128, 128, XT, 8, ut, xtt)
            kh, lh, bh = k[:, h, :], qr[:, h, :], b_[:, h, :]
            ta = P.act(lambda e, kh=kh, b=b: e.activation(kh, b[:, :], AF.Exp, scale=-1.0), tk)
            done(i, ta)
            P.dve(lambda e, kh=kh: e.tensor_scalar(kh, kh, 1.0, None, A.add), ta)
            P.dve(lambda e, kh=kh: e.reciprocal(kh, kh))
            tf = P.dve(lambda e, kh=kh, h=h: e.tensor_scalar(kh, kh, oml[:, h:h + 1], lb[:, h:h + 1], A.mult, A.add))
            tl = P.act(lambda e, kh=kh, lh=lh: e.activation(lh, kh, AF.Ln), tf)
            P.dve(lambda e, kh=kh: e.tensor_scalar(kh, kh, -1.0, 1.0, A.mult, A.add), tl)
            P.dve(lambda e, bh=bh, lh=lh: e.tensor_tensor_scan(bh, CH[:, :], lh, 0.0, A.mult, A.add), tl, cst)
        unit_done(u_, tk)

        def ch(x):
            return x.rearrange("p h (c j) -> p (h c) j", j=64)

        bc = ch(b_)
        eref, eend = st(32), st(32)
        P.dve(lambda e: e.tensor_tensor(ch(qr), bc, bc[:, :, 31:32].to_broadcast([128, 32, 64]), A.subtract))
        t1 = P.dve(lambda e: e.tensor_tensor(eend, bc[:, :, 63], bc[:, :, 31], A.subtract))
        P.act(lambda e: e.activation(eend, eend, AF.Exp), t1)
        P.act(lambda e: e.activation(eref, bc[:, :, 31], AF.Exp))
        P.act(lambda e: e.activation(kr, qr, AF.Exp, scale=-1.0))
        t1 = P.act(lambda e: e.activation(qr, qr, AF.Exp))
        P.dve(lambda e: e.tensor_tensor(kr, kr, k, A.mult), t1)
        tqk = P.dve(lambda e: e.tensor_tensor(qr, qr, q, A.mult), qdone)
        er, ee = (x.rearrange("p (h c) -> p h c", h=4) for x in (eref, eend))
        tes = P.dve(lambda e: e.tensor_tensor(ee[:, :, 0:7], ee[:, :, 0:7], er[:, :, 1:8], A.mult))

        u_, s_, ut = wcols(w_in, 1024, 512)
        wv3 = s_.rearrange("p (k n) -> p k n", k=8)
        for tt in range(NT):
            i, b, tk = proj_t(wv3, 0, 512, XT, tt, 8, ut, xtt)
            tv = evac(v[:, tt, :], b[:, :], tk)
            done(i, tv)
        unit_done(u_, tk)
        vdone = P.now("act", "dve")
        u_, s_, ut = wcols(w_in, 1536, 512)
        wv4 = s_.rearrange("p (k n) -> p k n", k=8)
        for tt in range(NT):
            i, b, tk = proj_t(wv4, 0, 512, XT, tt, 8, ut, xtt)
            e_ = E[:, tt, :]
            ta = P.act(lambda e, e_=e_, b=b: e.activation(e_, b[:, :], AF.Exp, scale=-1.0), tk, xtt)
            P.dve(lambda e, e_=e_: e.tensor_scalar(e_, e_, 1.0, None, A.add), ta)
            P.dve(lambda e, e_=e_: e.reciprocal(e_, e_))
            tv = P.dve(lambda e, e_=e_, b=b, tt=tt: e.tensor_tensor(og[:, tt, :], e_, b[:, :], A.mult))
            done(i, tv)
        unit_done(u_, tk)
        for tt in range(NT):
            i, b, fr = bank()
            t2 = P.pe([tr(b[:, h * 128:(h + 1) * 128], kr[:, h, tt * 128:(tt + 1) * 128], ident[:, :]) for h in range(4)], tqk, fr)
            tkt = evac(kt[:, tt, :], b[:, :], t2)
            done(i, tkt)
        ktdone = P.now("act", "dve")
        tz = P.dve(lambda e: e.memset(SC[:, 10, :], 0.0), cst)
        free_sc = [tz, tz]
        mfree = [tz, tz]
        tm = tz
        mask = mk[:, 0, :].unsqueeze(1).to_broadcast([128, 4, 128])
        for tt in range(NT):
            i, b, fr = bank()
            cs = slice(tt * 128, (tt + 1) * 128)
            t2 = P.pe([mm(b[:, h * 128:(h + 1) * 128], kr[:, h, cs], qr[:, h, cs], True, True) for h in range(4)], tqk, fr)
            scm = SB[:, tt % 2, :]
            t3 = P.dve(lambda e, scm=scm, b=b: e.copy_predicated(scm.rearrange("p (h n) -> p h n", h=4), mask, b[:, :].rearrange("p (h n) -> p h n", h=4)), t2, free_sc[tt % 2])
            done(i, t3)
            i, b, fr = bank()
            t4 = P.pe([mm(b[:, h * 128:(h + 1) * 128], scm[:, h * 128:(h + 1) * 128], v[:, tt, h * 128:(h + 1) * 128], h == 0, tt == 0) for h in range(4)], t3, fr, vdone)
            free_sc[tt % 2] = t4
            for hb in range(2):
                c = 2 * tt + hb
                c0 = c * 64
                p0 = hb * 64
                M = SB[:, 2 + c % 2, :]
                Mn = SB[:, 2 + (c + 1) % 2, :]
                if c:
                    t4 = P.pe([mm(b[p0:p0 + 64, h * 128:(h + 1) * 128], qr[:, h, c0:c0 + 64], M[:, h * 128:(h + 1) * 128], False, True) for h in range(4)], tm)
                    mfree[c % 2] = t4
                if c < 7:
                    i2, b2, fr2 = bank()
                    t5 = P.pe([mm(b2[:, h * 128:(h + 1) * 128], kt[p0:p0 + 64, tt, h * 128:(h + 1) * 128], v[p0:p0 + 64, tt, h * 128:(h + 1) * 128], True, True) for h in range(4)], fr2, ktdone)
                    t6 = P.dve(lambda e, M=M, Mn=Mn, b2=b2: e.tensor_tensor(Mn, M, b2[:, :], A.add), t5, mfree[(c + 1) % 2])
                    done(i2, t6)
                    tm = P.dve(lambda e, Mn=Mn, c=c: e.tensor_tensor(Mn.rearrange("p (h n) -> p h n", h=4), Mn.rearrange("p (h n) -> p h n", h=4), ee[:, :, c:c + 1].to_broadcast([128, 4, 128]), A.mult), tes)
            t7 = evac(o[:, tt, :], b[:, :], t4)
            done(i, t7)
        ohg = scv(1, 4)
        toh = heads_out(o, P.now("act", "dve"), 128, pcol("hg_out_norm"), ohg, 1.0, P.now(), mul=og)

        fr0 = P.now()
        dq, dk, dv, E1, E2, qT, kT, o2, odT = (scv(i, 4) for i in (0, 2, 3, 4, 5, 6, 8, 0, 7))
        raws = {}
        for n, dst in ((0, dq), (1, dk), (2, dv)):
            u_, s_, ut = wcols(w_in, 2048 + 512 * n, 512)
            wn = s_.rearrange("p (k n) -> p k n", k=8)
            for tt in range(NT):
                i, b, tk = proj_t(wn, 0, 512, XT, tt, 8, ut, xtt)
                tv = evac(dst[:, tt, :], b[:, :], tk, fr0)
                done(i, tv)
            unit_done(u_, tk)
        dvdone = P.now("act", "dve")
        for n, (src, dstT) in enumerate(((dq, qT), (dk, kT))):
            ss = st(32)
            t1 = P.act(lambda e, src=src: e.activation(E1, src, AF.Square), dvdone, P.now("pe"))
            t2 = P.dve(lambda e, ss=ss: e.tensor_reduce(ss, E1.rearrange("p a (j b) -> p (a j) b", b=64), AX, A.add), t1)
            rs_, t3 = rsq(ss, 32, 1.0 / 64, 1e-6, t2)
            sv = src.rearrange("p a (j b) -> p (a j) b", b=64)
            P.dve(lambda e, sv=sv, rs_=rs_: e.tensor_tensor(sv, sv, rs_.unsqueeze(2).to_broadcast([128, 32, 64]), A.mult), t3)
            P.dve(lambda e, sv=sv, n=n: e.tensor_tensor(sv, sv, G64[:, n:n + 1, :].to_broadcast([128, 32, 64]), A.mult), par)
            for tt in range(NT):
                s3 = src[:, tt, :].rearrange("p (j b) -> p j b", b=64)
                x1, x2 = s3[:, :, 0:32], s3[:, :, 32:64]
                e1 = E1[:, tt, :].rearrange("p (j b) -> p j b", b=64)
                e2 = E2[:, tt, :].rearrange("p (j b) -> p j b", b=64)
                cb = ROPE[:, 0, tt:tt + 1, :].to_broadcast([128, 8, 32])
                sb_ = ROPE[:, 1, tt:tt + 1, :].to_broadcast([128, 8, 32])
                P.dve(lambda e, a=e1[:, :, 0:32], x=x1, c=cb: e.tensor_tensor(a, x, c, A.mult), t1)
                P.dve(lambda e, a=e1[:, :, 32:64], x=x2, c=cb: e.tensor_tensor(a, x, c, A.mult))
                P.dve(lambda e, a=e2[:, :, 0:32], x=x2, c=sb_: e.tensor_tensor(a, x, c, A.mult))
                P.dve(lambda e, a=e2[:, :, 32:64], x=x1, c=sb_: e.tensor_tensor(a, x, c, A.mult))
                P.dve(lambda e, a=x1, x=e1[:, :, 0:32], y=e2[:, :, 0:32]: e.tensor_tensor(a, x, y, A.subtract))
                tx = P.dve(lambda e, a=x2, x=e1[:, :, 32:64], y=e2[:, :, 32:64]: e.tensor_tensor(a, x, y, A.add))
            for h in range(4):
                i, b, fr = bank()
                t6 = P.pe([tr(b[:, j * 128:(j + 1) * 128], src[:, j, h * 128:(h + 1) * 128], ident[:, :]) for j in range(NT)], tx, fr)
                t7 = evac(dstT[:, h, :], b[:, :], t6, fr0)
                done(i, t7)
        tqk = P.now("act", "dve", "pe")
        l = st(4)
        P.dve(lambda e: e.tensor_tensor_reduce(LAMP[:, 0:64], LAMP[:, 0:64], LAMP[:, 64:128], 1.0, 0.0, A.mult, A.add, l[:, 0:1]), par)
        t1 = P.dve(lambda e: e.tensor_tensor_reduce(LAMP[:, 128:192], LAMP[:, 128:192], LAMP[:, 192:256], 1.0, 0.0, A.mult, A.add, l[:, 1:2]))
        t1 = P.act(lambda e: e.activation(l[:, 0:2], l[:, 0:2], AF.Exp), t1)
        P.dve(lambda e: e.tensor_tensor(l[:, 2:3], l[:, 1:2], l[:, 0:1], A.subtract), t1)
        P.dve(lambda e: e.tensor_scalar(l[:, 3:4], l[:, 2:3], -LAM_INIT, None, A.add))
        nlam = l[:, 3:4]
        pfree = [tqk, tqk]
        afree = [tqk, tqk]
        n = 0
        for qt in range(NT):
            nk = 128 * (qt + 1)
            io, bo, fro = bank()
            for h in range(4):
                s = n % 2
                n += 1
                sts = st(8)
                ps = []
                for c in range(2):
                    i, b, fr = bank()
                    t2 = P.pe([mm(b[:, 0:nk], qT[64 * c:64 * c + 64, h, qt * 128:(qt + 1) * 128], kT[64 * c:64 * c + 64, h, 0:nk], True, True)], tqk, fr)
                    P.dve(lambda e, b=b, nk=nk: e.tensor_tensor(b[:, nk - 128:nk], b[:, nk - 128:nk], diagm[:, :], A.add), t2, cst)
                    P.dve(lambda e, b=b, nk=nk, m=sts[:, c:c + 1]: e.tensor_reduce(m, b[:, 0:nk], AX, A.max))
                    t3 = P.dve(lambda e, m=sts[:, c:c + 1]: e.tensor_scalar(m, m, -0.125, None, A.mult))
                    p_ = E1[:, 2 * s + c, 0:nk]
                    t4 = P.act(lambda e, p_=p_, b=b, nk=nk, m=sts[:, c:c + 1], z=sts[:, 2 + c:3 + c]: e.activation(p_, b[:, 0:nk], AF.Exp, bias=m, scale=0.125, accum_out=z), t3, pfree[s])
                    done(i, t4)
                    ps.append(p_)
                P.dve(lambda e, a=sts: e.reciprocal(a[:, 4:6], a[:, 2:4]), t4)
                P.dve(lambda e, a=sts: e.tensor_tensor(a[:, 5:6], a[:, 5:6], nlam, A.mult))
                P.dve(lambda e, a=sts, p=ps[1]: e.tensor_scalar(p, p, a[:, 5:6], None, A.mult))
                t5 = P.dve(lambda e, a=sts, p=ps[0], p1=ps[1]: e.scalar_tensor_tensor(p, p, a[:, 4:5], p1, A.mult, A.add))
                i, b, fr = bank()
                t6 = P.pe([tr(b[:, j * 128:(j + 1) * 128], ps[0][:, j * 128:(j + 1) * 128], ident[:, :]) for j in range(qt + 1)], t5, fr)
                pfree[s] = t6
                aT = E2[:, s, 0:nk]
                t7 = evac(aT, b[:, 0:nk], t6, afree[s])
                done(i, t7)
                t8 = P.pe([mm(bo[:, h * 128:(h + 1) * 128], aT[:, j * 128:(j + 1) * 128], dv[:, j, h * 128:(h + 1) * 128], j == 0, j == qt) for j in range(qt + 1)], t7, fro)
                afree[s] = t8
            t9 = evac(o2[:, qt, :], bo[:, :], t8, tqk)
            done(io, t9)
        tod = heads_out(o2, P.now("act", "dve"), 128, pcol("da_out_norm"), odT, 1.0 - LAM_INIT, P.now())
        fr1 = P.now()
        mb = scv(2, 8, 2)
        E4, Y4 = scv(4, 4), scv(5, 4)
        keep["x1"] = gated(w_in, 3584, t["w_branch_hg"][0], ohg, toh, t["w_branch_da"][0], odT, tod, None,
                           t["w_out"][0], xtt, mb, ([E4[:, 0, :], E4[:, 1, :]], [Y4[:, 0, :], Y4[:, 1, :]]), fr1)

    def first_hot(dst, vals, mx, n, *deps):
        tmp, m = st(NT * n).rearrange("p (a b) -> p a b", b=n), st(NT)
        io = iotm[:, 0:n].unsqueeze(1).to_broadcast([128, NT, n])
        P.dve(lambda e: e.tensor_tensor(dst, vals, mx.unsqueeze(2).to_broadcast([128, NT, n]), A.is_equal), *deps)
        P.dve(lambda e: e.tensor_tensor(tmp, dst, io, A.mult))
        P.dve(lambda e: e.tensor_reduce(m, tmp, AX, A.min))
        return P.dve(lambda e: e.tensor_tensor(dst, io, m.unsqueeze(2).to_broadcast([128, NT, n]), A.is_equal))

    def moe(bi):
        stn[0] = ST_KEEP
        wa, wb, wc, gname = ((("w1", "w3", "w2", "norm_moe"), ("w_e_gate_2", "w_e_up_2", "w_e_down_2", "norm_ffn_2"))[bi])
        W1, W3, W2 = t[wa][0], t[wb][0], t[wc][0]
        tab = tabs[bi]
        fr = P.now()
        xn = scv(0, 4, 2)
        gr = scv(2, 2)[:, 0, :]
        tg = P.dma("act", lambda e: e.dma_start(gr, t[gname].to_broadcast([128, D])), f"moeg{bi}", fr)
        rs, rt = rms(X, NT, D, fr)
        for i in range(NT):
            P.dve(lambda e, i=i: e.tensor_scalar(xn[:, i, :], X[:, i, :], rs[:, i:i + 1], None, A.mult), rt)
            tx = P.dve(lambda e, i=i: e.tensor_tensor(xn[:, i, :], xn[:, i, :], gr, A.mult), tg)
        txr = P.dma("act", lambda e: e.dma_start(xrows.rearrange("(t p) n -> p t n", p=128), xn), f"moex{bi}", tx)
        xtt = transposed(xn, NT, None, XT, tx, fr)
        i, b, frb = bank()
        for tt in range(NT):
            tk = P.pe([mm(b[:, tt * 64:tt * 64 + 36], XT[:, k, tt * 128:(tt + 1) * 128], WR[:, bi, k, :], k == 0, k == 7) for k in range(8)], frb, xtt, par)
        L = st(NT * 36).rearrange("p (a b) -> p a b", b=36)
        tl = P.dve(lambda e, b=b: e.tensor_tensor(L, b[:, 0:256].rearrange("p (a b) -> p a b", b=64)[:, :, 0:36], RB[:, bi:bi + 1, :].to_broadcast([128, NT, 36]), A.add), tk)
        done(i, tl)
        gl = L[:, :, 0:4]

        def s3(n):
            return st(NT * n).rearrange("p (a b) -> p a b", b=n)

        gm, gs, goh, ge, ein, tmp8, oh1, oh2 = st(NT), st(NT), s3(4), s3(4), s3(8), s3(8), s3(8), s3(8)
        P.dve(lambda e: e.tensor_reduce(gm, gl, AX, A.max))
        t1 = P.dve(lambda e: e.tensor_tensor(ge, gl, gm.unsqueeze(2).to_broadcast([128, NT, 4]), A.subtract))
        t1 = P.act(lambda e: e.activation(ge, ge, AF.Exp), t1)
        P.dve(lambda e: e.tensor_reduce(gs, ge, AX, A.add), t1)
        P.dve(lambda e: e.reciprocal(gs, gs))
        first_hot(goh, gl, gm, 4)
        for g in range(4):
            dst = ein if g == 0 else tmp8
            P.dve(lambda e, g=g, dst=dst: e.tensor_tensor(dst, L[:, :, 4 + 8 * g:12 + 8 * g], goh[:, :, g:g + 1].to_broadcast([128, NT, 8]), A.mult))
            if g:
                P.dve(lambda e: e.tensor_tensor(ein, ein, tmp8, A.add))
        v1, v2, g1, g2 = st(NT), st(NT), st(NT), st(NT)
        P.dve(lambda e: e.tensor_reduce(v1, ein, AX, A.max))
        first_hot(oh1, ein, v1, 8)
        P.dve(lambda e: e.scalar_tensor_tensor(tmp8, oh1, NEG, ein, A.mult, A.add))
        P.dve(lambda e: e.tensor_reduce(v2, tmp8, AX, A.max))
        first_hot(oh2, tmp8, v2, 8)
        t1 = P.dve(lambda e: e.tensor_tensor(v2, v2, v1, A.subtract))
        t1 = P.act(lambda e: e.activation(v2, v2, AF.Exp), t1)
        P.dve(lambda e: e.tensor_scalar(v1, v2, 1.0, None, A.add), t1)
        P.dve(lambda e: e.reciprocal(v1, v1))
        P.dve(lambda e: e.tensor_tensor(g1, v1, gs, A.mult))
        P.dve(lambda e: e.tensor_tensor(g2, g1, v2, A.mult))
        OH = [s3(32), s3(32)]
        M = s3(32)
        for k, oh in ((0, oh1), (1, oh2)):
            for g in range(4):
                P.dve(lambda e, k=k, g=g, oh=oh: e.tensor_tensor(OH[k][:, :, 8 * g:8 * g + 8], oh, goh[:, :, g:g + 1].to_broadcast([128, NT, 8]), A.mult))
        tM = P.dve(lambda e: e.tensor_tensor(M, OH[0], OH[1], A.add))
        i, b, frb = bank()
        for tt in range(NT):
            o_ = b[:, 32 * tt:32 * tt + 32]
            tk = P.pe([mm(o_, ones[:, :], M[:, j, :], j == 0, False) for j in range(tt)] + [mm(o_, upper[:, :], M[:, tt, :], tt == 0, True)], frb, tM, cst)
        tk = P.pe([mm(b[:, 128:160], ones[:, :], M[:, j, :], j == 0, j == 3) for j in range(NT)])
        tot, ov, ove, hi, lo = st(32), st(32), st(32), st(32), st(32)
        pos, c1 = s3(32), s3(32)
        P.dve(lambda e, b=b: e.tensor_copy(tot, b[:, 128:160]), tk)
        P.dve(lambda e: e.tensor_scalar(ov, tot, float(CAP), None, A.is_gt))
        for m in range(2, T // CAP):
            P.dve(lambda e, m=m: e.tensor_scalar(ove, tot, float(CAP * m), None, A.is_gt))
            P.dve(lambda e: e.tensor_tensor(ov, ov, ove, A.add))
        P.dve(lambda e: e.tensor_tensor_scan(ove, ones[:, 0:32], ov, 0.0, A.mult, A.add), cst)
        P.dve(lambda e: e.tensor_tensor(hi, ove, ov, A.subtract))
        P.dve(lambda e: e.tensor_scalar(hi, hi, float(CAP), float((NE - 1) * CAP), A.mult, A.add))
        P.dve(lambda e: e.tensor_scalar(lo, iotf[:, 0:32], float(CAP), None, A.mult))
        P.dve(lambda e: e.tensor_tensor(lo, lo, hi, A.subtract))
        tp = P.dve(lambda e, b=b: e.tensor_copy(pos, b[:, 0:128].rearrange("p (a b) -> p a b", b=32)))
        done(i, tp)
        P.dve(lambda e: e.tensor_scalar(c1, pos, float(CAP), None, A.is_lt))
        P.dve(lambda e: e.tensor_tensor(c1, c1, lo.unsqueeze(1).to_broadcast([128, NT, 32]), A.mult))
        P.dve(lambda e: e.tensor_tensor(pos, pos, c1, A.add))
        P.dve(lambda e: e.tensor_tensor(pos, pos, hi.unsqueeze(1).to_broadcast([128, NT, 32]), A.add))
        pk, pki = st(2 * NT).rearrange("p (a b) -> p a b", a=2), st(2 * NT).bitcast(I32).rearrange("p (a b) -> p a b", a=2)
        for k in range(2):
            P.dve(lambda e, k=k: e.tensor_tensor(OH[k], OH[k], pos, A.mult))
            P.dve(lambda e, k=k: e.tensor_reduce(pk[:, k, :], OH[k], AX, A.add))
        tpk = P.dve(lambda e: e.tensor_copy(pki, pk))
        exb, nov = st(NOV), st(NOV + 1).bitcast(I32)
        for j in range(NOV):
            P.dve(lambda e, j=j: e.tensor_scalar(ov, ove, float(j), None, A.is_le))
            P.dve(lambda e, j=j: e.tensor_reduce(exb[:, j:j + 1], ov, AX, A.add))
        P.dve(lambda e: e.tensor_scalar(exb, exb, float(NE - 1), None, A.min))
        P.dve(lambda e: e.tensor_copy(nov[:, 0:NOV], exb))
        tnov = P.dve(lambda e: e.tensor_copy(nov[:, NOV:NOV + 1], ove[:, 31:32]))
        NS = (NE + NOV) * CAP // 128
        fill = SC[:, 4, 0:128].bitcast(I32)
        t1 = P.pool(lambda e: e.memset(fill, 4 * T), fr)
        t1 = P.dma("pool", lambda e: e.dma_start(tab.rearrange("(a b) c -> a (b c)", b=128), fill[0:NS, :]), f"tf{bi}", t1)
        tsc = None
        for k in range(2):
            for tt in range(NT):
                tsc = P.dma("pool", lambda e, k=k, tt=tt: e.indirect_dma_start(tab, bass.IndirectOffsetOnAxis(ap=pki[:, k, tt:tt + 1], axis=0), ival[:, k, tt:tt + 1], None), f"ts{bi}", t1, tpk, cst)
        tb, tbf = SC[:, 4, 128:256].bitcast(I32), SC[:, 4, 256:384]
        t2 = P.dma("pool", lambda e: e.dma_start(tb[0:NS, :], tab.rearrange("(a b) c -> a (b c)", b=128)), f"tr{bi}", tsc)
        t2 = P.dve(lambda e: e.tensor_copy(tbf[0:NS, :], tb[0:NS, :]), t2, fr)
        i, b, frb = bank()
        tk = P.pe([tr(b[:, 0:NS], tbf[0:NS, :], ident[0:NS, 0:NS])], t2, frb)
        sidx, gidx = SC[:, 4, 384:384 + NS].bitcast(I32), SC[:, 4, 448:448 + NS].bitcast(I32)
        t3 = P.dve(lambda e, b=b: e.tensor_copy(sidx, b[:, 0:NS]), tk)
        done(i, t3)
        tix = P.dve(lambda e: e.tensor_scalar(gidx, sidx, 1, None, A.arith_shift_right))

        XG, YS, XE, HD, HT = scv(5, 2), scv(6, 2), scv(7, 2), scv(8, 4), scv(9, 4)
        tz = P.pool(lambda e: e.memset(SC[:, 5, :], 0.0), fr)
        HALF = (slice(0, 64), slice(64, 128))

        def gather(Q, p, rdy, fr_):
            s = p % 2
            return Q.dma("pool", lambda e: e.indirect_dma_start(XG[:, s, :], None, xrows, bass.IndirectOffsetOnAxis(ap=gidx[:, p:p + 1], axis=0), bounds_check=T - 1, oob_is_err=False), f"g{s}", rdy, fr_.get("xg"))

        def turn(Q, p, tg_, fr_):
            s = p % 2
            ts = []
            for hf in range(2):
                i, b, fb = bank()
                t2 = Q.pe([tr(b[:, j * 128:(j + 1) * 128], XG[:, s, (4 * hf + j) * 128:(4 * hf + j + 1) * 128], ident[:, :]) for j in range(4)], tg_, fb)
                dst = XE[:, s, hf * 512:(hf + 1) * 512]
                if hf == 0:
                    t3 = Q.act(lambda e, dst=dst, b=b: e.activation(dst, b[:, :], AF.Copy), t2, fr_.get("xe"))
                else:
                    t3 = Q.dve(lambda e, dst=dst, b=b: e.tensor_copy(dst, b[:, :]), t2, fr_.get("xe"))
                done(i, t3)
                ts.append(t3)
            return t2, ts

        def up(Q, p, tx_, w1, w3, fr_):
            s = p % 2
            hd = HD[:, s, :]
            ks = []
            for w_ in (w1, w3):
                i, b, fb = bank()
                ks.append((i, b, Q.pe([mm(b[HALF[x], :], XE[:, s, k * 128 + 64 * x:k * 128 + 64 * x + 64], w_[x][1][:, k, :], k == 0, k == 7) for k in range(8) for x in range(2)], tx_, fb, [u[2] for u in w_])))
            (i1, b1, k1), (i3, b3, k3) = ks
            ta = Q.act(lambda e: e.activation(hd, b1[:, :], AF.Silu), k1, fr_.get("hd"))
            done(i1, ta)
            th = Q.dve(lambda e: e.tensor_tensor(hd, hd, b3[:, :], A.mult), ta, k3)
            done(i3, th)
            return k1, k3, th

        def down(Q, p, th, w2, fr_):
            s = p % 2
            hd, ht, ys = HD[:, s, :], HT[:, s, :], YS[:, s, :]
            i, b, fb = bank()
            t2 = Q.pe([tr(b[:, j * 128:(j + 1) * 128], hd[:, j * 128:(j + 1) * 128], ident[:, :]) for j in range(4)], th, fb)
            t3 = Q.act(lambda e, b=b: e.activation(ht, b[:, :], AF.Copy), t2, fr_.get("ht"))
            done(i, t3)
            tys = []
            for hf in range(2):
                i, b, fb = bank()
                k2 = Q.pe([mm(b[HALF[x], :], ht[:, k * 128 + 64 * x:k * 128 + 64 * x + 64], w2[x][1][:, k, hf * 512:(hf + 1) * 512], k == 0, k == 3) for k in range(4) for x in range(2)], t3, fb, [u[2] for u in w2])
                dst = ys[:, hf * 512:(hf + 1) * 512]
                if hf:
                    ty = Q.act(lambda e, dst=dst, b=b: e.activation(dst, b[:, :], AF.Copy), k2, fr_.get("ys"))
                else:
                    ty = Q.dve(lambda e, dst=dst, b=b: e.tensor_copy(dst, b[:, :]), k2, fr_.get("ys"))
                done(i, ty)
                tys.append(ty)
            return t2, k2, tys

        def scatter(Q, p, tys):
            s = p % 2
            return Q.dma("pool", lambda e: e.indirect_dma_start(ytab, bass.IndirectOffsetOnAxis(ap=sidx[:, p:p + 1], axis=0), YS[:, s, :], None, bounds_check=2 * T - 1, oob_is_err=False), f"y{s}", tys)

        def pairs(Q, n, first, rdy, fr0_, weights, used, end_of=None):
            fr_ = [dict(fr0_), dict(fr0_)]
            tg_ = gather(Q, first, rdy, fr_[first % 2])
            t2, tx_ = turn(Q, first, tg_, fr_[first % 2])
            fr_[first % 2]["xg"] = t2
            ty = [None, None]
            for p in range(first, first + n):
                s = p % 2
                more = p + 1 < first + n
                w1 = weights(p, 0)
                w3 = weights(p, 1)
                if more and end_of is None:
                    tg_ = gather(Q, p + 1, rdy, fr_[1 - s])
                k1, k3, th = up(Q, p, tx_, w1, w3, fr_[s])
                fr_[s]["xe"] = k3
                used(w1, k1)
                used(w3, k3)
                if more and end_of is None:
                    t2, tx_ = turn(Q, p + 1, tg_, fr_[1 - s])
                    fr_[1 - s]["xg"] = t2
                w2 = weights(p, 2)
                t2, k2, tys = down(Q, p, th, w2, fr_[s])
                fr_[s]["hd"], fr_[s]["ht"] = t2, k2
                used(w2, k2)
                fr_[s]["ys"] = ty[s] = scatter(Q, p, tys)
                if end_of is not None:
                    end_of(p)
                    if more:
                        tg_ = gather(Q, p + 1, rdy, fr_[1 - s])
                        t2, tx_ = turn(Q, p + 1, tg_, fr_[1 - s])
                        fr_[1 - s]["xg"] = t2
            return ty

        def view(slot, j):
            return slot.rearrange("p (k n) -> p k n", k=4 if j == 2 else 8)

        def src(w_, e_):
            return w_[e_].rearrange("(k p) n -> p k n", p=128)

        def weights(p, j):
            us = [unit([(lambda sl, j=j: view(sl, j), src((W1, W3, W2)[j], 2 * p + x))]) for x in range(2)]
            return [(u_[0], view(u_[1], j), u_[2]) for u_ in us]

        def used(us, tok):
            for u_ in us:
                unit_done(u_[0], tok)

        spare = [SC[:, 10:12, :], SC[:, 2:4, :]]
        slots.extend(x.rearrange("p a b -> p (a b)") for x in spare)
        ring_free.extend([tx] + P.now() for _ in spare)
        while ring_no[0] % len(slots) != NRING:
            ring_no[0] += 1
        frx = {k: fr for k in ("xe", "hd", "ht", "ys")}
        ty = pairs(P, NE // 2, 0, [tix, txr, tz], frx, weights, used)
        O = Prog(nc, ctx, f"o{bi}")
        saved = list(bank_free), bank_no[0]
        for i in range(8):
            bank_free[i] = []
        segs = []
        wfree = [None] * 3

        def oweights(p, j):
            res = []
            for x in range(2):
                slot = slots[2 * j + x]

                def load(e, slot=slot, x=x):
                    o_ = 2 * (p - NE // 2) + x
                    v = e.value_load(nov[0:1, o_:o_ + 1], min_val=0, max_val=NE - 1)
                    return e.dma_start(view(slot, j), (W1, W3, W2)[j][bass.ds(v, 1)].rearrange("a (k p) n -> p (a k) n", p=128))

                tok = O.dma("sp", load, f"w{2 * j + x}", wfree[j])
                res.append((j, view(slot, j), tok))
            return res

        def oused(us, tok):
            wfree[us[0][0]] = tok

        pairs(O, NOV // 2, NE // 2, None, {}, oweights, oused,
              lambda p: segs.append(({g: len(O.q[g]) for g in ENG}, list(O.n.items()))))
        bank_free[:] = saved[0]
        bank_no[0] = saved[1]
        barrier = P.now() + ty + [tnov] + [(f"ring{i}", P.n[f"ring{i}"]) for i in range(len(slots))]

        def branch(eng):
            def run(e):
                v = e.value_load(nov[0:1, NOV:NOV + 1], min_val=0, max_val=NOV)
                seen, at = {}, 0
                for j, (to, ends) in enumerate(segs):
                    with e.If(v > 2 * j):
                        O.emit(eng, e, at, to[eng], seen)
                        for name, val in ends:
                            e.wait_ge(O.sems[name], val)
                    at = to[eng]
            return run

        toks = []
        if "join" not in P.sems:
            P.sems["join"] = ctx.enter_context(nc.semaphore("m_join"))
        for eng in ENG:
            P.raw(eng, branch(eng), barrier)
            tok = P.count("join", 1)
            P.raw(eng, lambda e: e.sem_inc(P.sems["join"], 1))
        del slots[NRING:], ring_free[NRING:]
        while ring_no[0] % NRING:
            ring_no[0] += 1
        for i in range(NRING):
            unit_done(i, tok)
        YB = [scv(0, 1, 1)[:, 0, :], scv(1, 1, 1)[:, 0, :]]
        fy = [tok, tok]
        for tt in range(NT):
            s = tt % 2
            ty = P.dma("act", lambda e, tt=tt, s=s: e.dma_start(YB[s], ytab.rearrange("(t p c) n -> t p (c n)", p=128, c=2)[tt]), f"yb{s}", tok, fy[s])
            for k, gk in ((0, g1), (1, g2)):
                fy[s] = P.dve(lambda e, k=k, gk=gk, tt=tt, s=s: e.scalar_tensor_tensor(X[:, tt, :], YB[s][:, k * D:(k + 1) * D], gk[:, tt:tt + 1], X[:, tt, :], A.mult, A.add), ty)
        keep["x"] = fy

    def block2_mix():
        stn[0] = 0
        w_in = t["w_in_2"][0]
        m0_ = P.now()
        rs, rt = rms(X, NT, D, m0_)
        xtt = to_xt(X, NT, rs, rt, pcols("norm_mix_2", 8), XT, scv(4, 4, 2), m0_)
        fr = P.now()
        QT, Y0, GH, BV, GT = scv(0, 4), scv(1, 4), SC[:, 2:4, :].rearrange("p s n -> p (s n)"), scv(4, 4), scv(5, 4)
        GTm = GH[:, 0:2048].rearrange("p (a n) -> p a n", a=4)
        Hm = GH[:, 2048:4096].rearrange("p (a n) -> p a n", a=4)
        tmp = [SC[:, 6 + i // 4, (i % 4) * 512:(i % 4 + 1) * 512] for i in range(22)]
        mu = pcols("shift_mu_2", 14)
        omu = st(14)
        P.dve(lambda e: e.tensor_scalar(omu, mu, -1.0, 1.0, A.mult, A.add))
        nw0, na0 = st(4), st(4)
        P.dve(lambda e: e.tensor_scalar(nw0, pcols("rw_w0_2", 4), -1.0, None, A.mult))
        tom = P.dve(lambda e: e.tensor_scalar(na0, pcols("rw_a0_2", 4), -1.0, None, A.mult))

        def shifted(wv, c, j, dst, wt, free=None):
            i, b, tk = proj_f(wv, c, 128, XT, 8, wt, xtt)
            ta = P.act(lambda e: e.activation(dst, b[:, :], AF.Identity, scale=omu[:, j:j + 1]), tk, tom, free)
            tv = P.dve(lambda e: e.scalar_tensor_tensor(dst[:, 1:512], b[:, 0:511], mu[:, j:j + 1], dst[:, 1:512], A.mult, A.add), ta)
            done(i, tv)
            return tk, tv

        wq = w_in.rearrange("(k p) n -> p k n", p=128)

        def part(o, n, c):
            return (lambda s: s[:, 0:3104].rearrange("p (k n) -> p k n", k=8)[:, :, o:o + n], wq[:, :, c:c + n])

        C_RW, C_Q, C_KV, C_QI, C_KI, C_WI = 0, 1792, 2304, 2432, 2688, 2752
        ul, sl, tl = unit([part(0, 256, 1536), part(256, 64, C_KI), part(320, 64, C_KI), part(384, 4, C_WI)])
        wl = sl[:, 0:3104].rearrange("p (k n) -> p k n", k=8)
        KI, WI = sb("KI", [128, T]), st(NT * 4).rearrange("p (a b) -> p a b", b=4)
        LW = tmp[18]
        XW, XG = tmp[20], tmp[21]
        tlw = P.dma("act", lambda e: e.dma_start(LW[0:64, :], t["rw_w2_2"][0]), "lw", fr)
        tlw = P.dma("act", lambda e: e.dma_start(LW[64:128, :], t["rw_a2_2"][0]), "lw")
        G2 = tmp[19]
        tlw = P.dma("act", lambda e: e.dma_start(G2, t["rw_g2_2"][0]), "lw")
        _, tv = shifted(wl, 0, 12, XW, tl, fr)
        txw = P.act(lambda e: e.activation(XW[0:64, :], XW[0:64, :], AF.Tanh), tv)
        _, tv = shifted(wl, 128, 13, XG, tl, fr)
        ta = P.act(lambda e: e.activation(XG, XG, AF.Exp, scale=-1.0), tv)
        P.dve(lambda e: e.tensor_scalar(XG, XG, 1.0, None, A.add), ta)
        txg = P.dve(lambda e: e.reciprocal(XG, XG))
        i, b, tk = proj_f(wl, 256, 128, XT, 8, tl, xtt)
        tki = P.act(lambda e, b=b: e.activation(KI[:, :], b[:, :], AF.Copy), tk)
        done(i, tki)
        for tt in range(NT):
            i, b, tk = proj_t(wl, 384, 4, XT, tt, 8, tl, xtt)
            twi = P.dve(lambda e, b=b, tt=tt: e.tensor_scalar(WI[:, tt, :], b[:, 0:4], 1.0 / 16.0, None, A.mult), tk)
            done(i, twi)
        unit_done(ul, tk)
        for j in range(4):
            i, b, fb = bank()
            tk = P.pe([mm(b[:, :], G2[:, j * 128:(j + 1) * 128], XG, True, True)], txg, tlw, fb)
            tg = evac(GT[:, j, :], b[:, :], tk, fr)
            done(i, tg)
        units = [wcols(w_in, 512 * j, 512) for j in range(3)]
        wvs = [u[1].rearrange("p (k n) -> p k n", k=8) for u in units]
        ESC = math.exp(-0.5)
        eref = st(32).rearrange("p (a c) -> p a c", a=4)
        eend = st(32).rearrange("p (a c) -> p a c", a=4)
        yT = P.now()
        fams = [None]

        def pair(pt):
            pf = P.now()
            r, k, v, a, b_, kk, t6, t7, al, be, kR, rR = tmp[0:12]
            aT, bT, kT, vT = (x.rearrange("p (t n) -> p t n", t=4) for x in tmp[12:16])
            for n, dst in enumerate((r, k, v)):
                tk, tv = shifted(wvs[n], pt * 128, 4 * n + pt, dst, units[n][2], pf)
                if pt == 3:
                    unit_done(units[n][0], tk)
            for src, c0, bias, dst in ((LW, 64, na0, a), (LW, 0, nw0, t6)):
                i, b, fb = bank()
                tk = P.pe([mm(b[:, :], LW[c0:c0 + 64, pt * 128:(pt + 1) * 128], XW[c0:c0 + 64, :], True, True)], fb, txw, tlw, tom)
                ta = P.act(lambda e, b=b, dst=dst, bias=bias: e.activation(dst, b[:, :], AF.Exp, scale=-1.0, bias=bias[:, pt:pt + 1]), tk, pf)
                done(i, ta)
                P.dve(lambda e, dst=dst: e.tensor_scalar(dst, dst, 1.0, None, A.add), ta)
                tv = P.dve(lambda e, dst=dst: e.reciprocal(dst, dst))
            P.dve(lambda e: e.tensor_scalar(t6, t6, -ESC, None, A.mult))
            P.dve(lambda e: e.tensor_tensor_scan(b_, CH[:, :], t6, 0.0, A.mult, A.add))
            P.dve(lambda e: e.tensor_tensor(t6, b_, t6, A.subtract))
            P.dve(lambda e, pt=pt: e.tensor_scalar(kk, k, pcol("rw_k_k_2", pt), None, A.mult))
            tv = P.dve(lambda e: e.tensor_tensor(t7, kk, kk, A.mult))
            i, b, fb = bank()
            tk = P.pe([mm(b[:, :], BO[:, :], t7, True, True)], tv, fb)
            t1 = P.dve(lambda e, b=b: e.tensor_scalar(t7, b[:, :], 1e-24, 2.0 ** 20, A.max, A.mult), tk)
            done(i, t1)
            P.act(lambda e: e.activation(al, t7, AF.Ln), t1)
            t1 = P.act(lambda e: e.activation(al, al, AF.Exp, scale=-0.5))
            P.dve(lambda e: e.scalar_tensor_tensor(be, al, -0.5, al, A.mult, A.mult), t1)
            P.dve(lambda e: e.tensor_tensor(be, be, t7, A.mult))
            P.dve(lambda e: e.scalar_tensor_tensor(al, be, 1.5, al, A.add, A.mult))
            P.dve(lambda e: e.scalar_tensor_tensor(kk, kk, 2.0 ** 10, al, A.mult, A.mult))
            P.dve(lambda e, pt=pt: e.tensor_scalar(t7, a, 1.0, pcol("rw_k_a_2", pt), A.subtract, A.mult))
            P.dve(lambda e: e.scalar_tensor_tensor(k, t7, 1.0, k, A.add, A.mult))
            P.dve(lambda e, pt=pt: e.tensor_scalar(t7, r, pcol("rw_r_k_2", pt), None, A.mult))
            tv = P.dve(lambda e: e.tensor_tensor(t7, t7, k, A.mult))
            i, b, fb = bank()
            tk = P.pe([mm(b[:, :], BO[:, :], t7, True, True)], tv, fb)
            tb = P.dve(lambda e, b=b, pt=pt: e.tensor_tensor(BV[:, pt, :], v, b[:, :], A.mult), tk, fr)
            done(i, tb)
            P.dve(lambda e: e.tensor_tensor(be, kk, a, A.mult))
            bc, pc3, t73 = (x.rearrange("p (c j) -> p c j", j=64) for x in (b_, t6, t7))
            mid = bc[:, :, 31:32].to_broadcast([128, 8, 64])
            t1 = P.dve(lambda e, pt=pt, bc=bc: e.tensor_tensor(eend[:, pt, :], bc[:, :, 63], bc[:, :, 31], A.subtract))
            P.act(lambda e, pt=pt: e.activation(eend[:, pt, :], eend[:, pt, :], AF.Exp), t1)
            te = P.act(lambda e, pt=pt, bc=bc: e.activation(eref[:, pt, :], bc[:, :, 31], AF.Exp))
            P.dve(lambda e, pc3=pc3, mid=mid: e.tensor_tensor(pc3, pc3, mid, A.subtract))
            t1 = P.dve(lambda e, t73=t73, bc=bc, mid=mid: e.tensor_tensor(t73, bc, mid, A.subtract), te)
            P.act(lambda e: e.activation(t6, t6, AF.Exp), t1)
            P.act(lambda e: e.activation(rR, t7, AF.Exp), pf)
            t1 = P.act(lambda e: e.activation(t7, t7, AF.Exp, scale=-1.0))
            P.dve(lambda e: e.scalar_tensor_tensor(al, kk, -1.0, t6, A.mult, A.mult), t1)
            P.dve(lambda e: e.tensor_tensor(be, be, t7, A.mult))
            P.dve(lambda e: e.tensor_tensor(kR, k, t7, A.mult))
            tf = P.dve(lambda e: e.tensor_tensor(rR, rR, r, A.mult))
            for src, dst in ((al, aT), (be, bT), (kR, kT), (v, vT)):
                i, b, fb = bank()
                tk = P.pe([tr(b[:, j * 128:(j + 1) * 128], src[:, j * 128:(j + 1) * 128], ident[:, :]) for j in range(NT)], tf, fb)
                td = evac(dst.rearrange("p t n -> p (t n)"), b[:, :], tk)
                done(i, td)
            tT = P.now("act", "dve", "pe")
            def head(par_):
                h = 2 * pt + par_
                q0 = par_ * 64
                hs = slice(q0, q0 + 64)
                N16, L16, N32, L32, L64, Pm, Qm, N2 = tmp[0:8]
                L2, AkT, RbT, RkT = tmp[16], tmp[17], SC[:, 11, 1024:1536], SC[:, 11, 1536:2048]
                X1, X2 = tmp[19], tmp[21]
                fz = [tT, fams[0]]
                tz = None
                for buf in (N16, L16, N32, L32, L64, AkT, RbT, RkT):
                    tz = P.pool(lambda e, buf=buf: e.memset(buf, 0.0), fz)

                def scores(l, rr, outs):
                    i, b, fb = bank()
                    tk = P.pe([mm(b[:, j * 128:(j + 1) * 128], l[hs, j * 128:(j + 1) * 128], rr[hs, j * 128:(j + 1) * 128], True, True) for j in range(NT)], fb, tT)
                    for dst, mask in outs:
                        tv = P.dve(lambda e, dst=dst, mask=mask, b=b: e.copy_predicated(dst.rearrange("p (t n) -> p t n", t=4), mask.unsqueeze(1).to_broadcast([128, 4, 128]), b[:, :].rearrange("p (t n) -> p t n", t=4)), tk, tz)
                    done(i, tv)
                    return tv

                mb = lambda j: mband[:, j, :]
                scores(be, al, ((N16, mb(0)), (N32, mb(2))))
                scores(al, be, ((L16, mb(1)), (L32, mb(3)), (L64, mb(4))))
                scores(kR, al, ((AkT, mb(5)),))
                scores(be, rR, ((RbT, mk[:, 0, :]),))
                tsc = scores(kR, rR, ((RkT, mk[:, 0, :]),))

                def mul(l, rr, *deps):
                    i, b, fb = bank()
                    return i, b, P.pe([mm(b[:, j * 128:(j + 1) * 128], l[:, j * 128:(j + 1) * 128], rr[:, j * 128:(j + 1) * 128], True, True) for j in range(NT)], fb, *deps)

                def cp(dst, ibk, *deps):
                    i, b, tk = ibk
                    tv = P.act(lambda e: e.activation(dst, b[:, :], AF.Copy), tk, *deps)
                    done(i, tv)
                    return tv

                def addto(dst, src, ibk, *deps):
                    i, b, tk = ibk
                    tv = P.dve(lambda e: e.tensor_tensor(dst, src, b[:, :], A.add), tk, *deps)
                    done(i, tv)
                    return tv

                idb = ident[:, :].unsqueeze(1).to_broadcast([128, 4, 128])
                v4 = lambda x: x.rearrange("p (t n) -> p t n", t=4)
                P.dve(lambda e: e.tensor_tensor(v4(Pm), v4(N16), idb, A.add))
                tpq = P.dve(lambda e: e.tensor_tensor(v4(Qm), v4(L16), idb, A.add))
                na, la, nb, lb_ = N16, L16, N2, L2
                for lev in range(3):
                    m1 = mul(la, na, tpq)
                    m2 = mul(na, la)
                    c1 = cp(nb, m1, fz)
                    c2 = cp(lb_, m2)
                    p1 = mul(lb_, Pm, c2, tpq)
                    p2 = mul(nb, Qm, c1)
                    addto(Pm, Pm, p1)
                    tpq = addto(Qm, Qm, p2)
                    na, la, nb, lb_ = nb, lb_, (X1, N2)[lev % 2], (X2, L2)[lev % 2]
                a1 = cp(N16, mul(L32, Pm, tpq), P.now("pe"))
                a2 = cp(L16, mul(N32, Qm))
                p1 = mul(Qm, N16, a1)
                p2 = mul(Pm, L16, a2)
                addto(Pm, Pm, p1, p2[2])
                tpq = addto(Qm, Qm, p2)
                a1 = cp(N16, mul(L64, Pm, tpq))
                tP = addto(Pm, Pm, mul(Qm, N16, a1))
                hc = slice(q0, q0 + 64)
                i, b, fb = bank()
                tk = P.pe([mm(b[:, j * 64:(j + 1) * 64], AkT[:, j * 128:(j + 1) * 128], vT[:, j, hc], True, True) for j in range(NT)], fb, tsc)
                Z, W1, UV = N2[:, 0:256], L2[:, 0:256], L2[:, 256:512]
                tz_ = P.act(lambda e, b=b: e.activation(Z, b[:, 0:256], AF.Copy), tk, tP)
                done(i, tz_)
                i, b, fb = bank()
                tk = P.pe([mm(b[:, j * 64:(j + 1) * 64], Pm[:, j * 128:(j + 1) * 128], aT[:, j, hc], True, True) for j in range(NT)]
                          + [mm(b[:, 256 + j * 64:256 + (j + 1) * 64], Pm[:, j * 128:(j + 1) * 128], Z[:, j * 64:(j + 1) * 64], True, True) for j in range(NT)], fb, tz_, tP)
                tw = P.act(lambda e, b=b: e.activation(L2, b[:, :], AF.Copy), tk)
                done(i, tw)
                i, b, fb = bank()
                tk = P.pe([mm(b[hs, j * 128:(j + 1) * 128], W1[:, j * 64:(j + 1) * 64], RbT[:, j * 128:(j + 1) * 128], True, True) for j in range(NT)], fb, tw, tsc)
                tq = P.dve(lambda e, b=b: e.tensor_tensor(QT[hs, pt, :], b[hs, :], rR[hs, :], A.add), tk, fr)
                done(i, tq)
                i, b, fb = bank()
                tk = P.pe([f for j in range(NT) for f in (mm(b[:, j * 64:(j + 1) * 64], RbT[:, j * 128:(j + 1) * 128], UV[:, j * 64:(j + 1) * 64], True, False),
                                                         mm(b[:, j * 64:(j + 1) * 64], RkT[:, j * 128:(j + 1) * 128], vT[:, j, hc], False, True))], fb)
                ty = P.act(lambda e, b=b, h=h: e.activation(Y0[:, :, h * 64:(h + 1) * 64], b[:, 0:256].rearrange("p (t n) -> p t n", t=4), AF.Copy), tk, fr)
                done(i, ty)
                for ev in range(2):
                    i, b, fb = bank()
                    i2, b2, fb2 = bank()
                    ps_ = slice(ev * 64, ev * 64 + 64)
                    fs = []
                    for tt in range(NT):
                        o_ = slice(tt * 64, tt * 64 + 64)
                        fs += [mm(b[hs, o_], W1[ps_, tt * 64:(tt + 1) * 64], bT[ps_, tt, hc], True, True),
                               mm(b2[hs, o_], bT[ps_, tt, hc], UV[ps_, tt * 64:(tt + 1) * 64], True, False),
                               mm(b2[hs, o_], kT[ps_, tt, hc], vT[ps_, tt, hc], False, True)]
                    tk = P.pe(fs, fb, fb2)
                    c4 = lambda x: x.rearrange("p (t c n) -> p t c n", c=2, n=64)[:, :, ev, :]
                    tg = P.act(lambda e, d=c4(GTm[hs, pt, :]), s_=b[hs, 0:256].rearrange("p (t n) -> p t n", n=64): e.activation(d, s_, AF.Copy), tk, fr)
                    done(i, tg)
                    th = P.dve(lambda e, d=c4(Hm[hs, pt, :]), s_=b2[hs, 0:256].rearrange("p (t n) -> p t n", n=64): e.tensor_copy(d, s_), tk, fr)
                    done(i2, th)
                fams[0] = P.now("pe", "act", "dve")

            head(0)
            head(1)

        for pt in range(4):
            pair(pt)
        fam_free = fams[0]
        P.dve(lambda e: e.tensor_tensor(eend[:, :, 0:7], eend[:, :, 0:7], eref[:, :, 1:8], A.mult), P.now())
        MB = [tmp[i] for i in range(8)]
        M4 = [m[:, 0:256].rearrange("p (a n) -> p a n", a=4) for m in MB]
        H5 = Hm.rearrange("p a (c n) -> p a c n", c=8)
        tm = None
        for c in range(7):
            dst = M4[c + 1]
            ec = eend[:, :, c:c + 1].to_broadcast([128, 4, 64])
            if c == 0:
                P.dve(lambda e, dst=dst: e.tensor_copy(dst, H5[:, :, 0, :]), fam_free)
            else:
                i, b, fb = bank()
                i2, b2, fb2 = bank()
                fs = []
                for pt in range(4):
                    for hs, bb in ((slice(0, 64), b), (slice(64, 128), b2)):
                        fs.append(mm(bb[hs, pt * 64:(pt + 1) * 64], GTm[hs, pt, c * 64:(c + 1) * 64], M4[c][hs, pt, :], True, True))
                tk = P.pe(fs, fb, fb2, tm, fam_free)
                P.dve(lambda e, dst=dst, c=c: e.tensor_tensor(dst, M4[c], H5[:, :, c, :], A.add))
                P.dve(lambda e, dst=dst, b=b: e.tensor_tensor(dst[0:64], dst[0:64], b[0:64, 0:256].rearrange("p (a n) -> p a n", a=4), A.add), tk)
                t2 = P.dve(lambda e, dst=dst, b2=b2: e.tensor_tensor(dst[64:128], dst[64:128], b2[64:128, 0:256].rearrange("p (a n) -> p a n", a=4), A.add), tk)
                done(i, t2)
                done(i2, t2)
            tm = P.dve(lambda e, dst=dst, ec=ec: e.tensor_tensor(dst, dst, ec, A.mult))
        for c in range(1, 8):
            tt, pp = c // 2, (c % 2) * 64
            for ev in range(2):
                hs = slice(ev * 64, ev * 64 + 64)
                i, b, fb = bank()
                tk = P.pe([mm(b[pp:pp + 64, pt * 64:(pt + 1) * 64], QT[hs, pt, c * 64:(c + 1) * 64], M4[c][hs, pt, :], True, True) for pt in range(4)], fb, tm)
                yh = Y0[pp:pp + 64, tt, :].rearrange("p (a e n) -> p a e n", e=2, n=64)[:, :, ev, :]
                ty = P.dve(lambda e, b=b, yh=yh, pp=pp: e.tensor_tensor(yh, yh, b[pp:pp + 64, 0:256].rearrange("p (a n) -> p a n", n=64), A.add), tk)
                done(i, ty)
        yv = Y0.rearrange("p t (h n) -> p (t h) n", n=64)
        junk = SC[:, NSC - 1, :]
        jv = junk.rearrange("p (a n) -> p a n", n=64)
        mean, var = st(32), st(32)
        P.dve(lambda e: e.tensor_reduce(mean, yv, AX, A.add))
        P.dve(lambda e: e.tensor_scalar(mean, mean, 1.0 / 64, None, A.mult))
        t1 = P.dve(lambda e: e.tensor_tensor(yv, yv, mean.unsqueeze(2).to_broadcast([128, 32, 64]), A.subtract))
        t1 = P.act(lambda e: e.activation(jv, yv, AF.Square), t1)
        t1 = P.dve(lambda e: e.tensor_reduce(var, jv, AX, A.add), t1)
        rs2, t1 = rsq(var, 32, 1.0 / 64, 64e-5, t1)
        t1 = P.dve(lambda e: e.tensor_tensor(yv, yv, rs2.unsqueeze(2).to_broadcast([128, 32, 64]), A.mult))
        YA = QT
        for j in range(4):
            i, b, fb = bank()
            tk = P.pe([tr(b[:, n * 128:(n + 1) * 128], Y0[:, n, j * 128:(j + 1) * 128], ident[:, :]) for n in range(NT)], t1, fb)
            t2 = P.dve(lambda e, b=b, j=j: e.tensor_scalar(YA[:, j, :], b[:, :], pcol("rw_ln_w_2", j), pcol("rw_ln_b_2", j), A.mult, A.add), tk)
            done(i, t2)
            P.dve(lambda e, j=j: e.tensor_tensor(YA[:, j, :], YA[:, j, :], BV[:, j, :], A.add))
            tya = P.dve(lambda e, j=j: e.tensor_tensor(YA[:, j, :], YA[:, j, :], GT[:, j, :], A.mult))
        keep["ya"] = tya
        if dbg.get('cut') != 1:
            dsa(xtt, tya, KI, WI, w_in)

    def dsa(xtt, tya, KI, WI, w_in):
        fr = P.now()
        YA, qF, YB = scv(0, 4), scv(1, 4), scv(10, 4)
        ct, cT = SC[:, 2, 0:512].rearrange("p (t n) -> p t n", t=4), SC[:, 2, 512:1024]
        QI = SC[:, 2, 1024:2048].rearrange("p (a n) -> p a n", a=2)
        wukT, wuv, wuk = SC[:, 3, 0:512].rearrange("p (a n) -> p a n", a=4), SC[:, 3, 512:1024], SC[:, 3, 1024:1536]
        BM = scv(4, 4)
        acc, work, eq, cum = (SC[:, 5, 512 * i:512 * (i + 1)] for i in range(4))
        rel = [SC[:, 6, 512 * i:512 * (i + 1)] for i in range(4)]
        ql = [SC[:, 7, 0:512], SC[:, 7, 512:1024]]
        pb = [SC[:, 8, 512 * i:512 * (i + 1)] for i in range(4)]
        pT = [SC[:, 9, 512 * i:512 * (i + 1)] for i in range(2)]
        oT = [SC[:, 9, 1024:1536], SC[:, 9, 1536:2048]]
        tw = P.dma("act", lambda e: e.dma_start(wuk, t["w_uk_2"].rearrange("l r h n -> (l r) (h n)")), "dsw", fr)
        tw = P.dma("act", lambda e: e.dma_start(wuv, t["w_uv_2"].rearrange("l r h n -> (l r) (h n)")), "dsw", fr)
        uq, sq, tq_ = wcols(w_in, 1792, 512)
        wq = sq.rearrange("p (k n) -> p k n", k=8)
        ud, sd, td_ = wcols(w_in, 2304, 384)
        wd = sd[:, 0:3072].rearrange("p (k n) -> p k n", k=8)
        for j in range(2):
            i, b, tk = proj_f(wd, 128 + 128 * j, 128, XT, 8, td_, xtt)
            t1 = evac(QI[:, j, :], b[:, :], tk, fr)
            done(i, t1)
        ss = st(NT)
        for tt in range(NT):
            i, b, tk = proj_t(wd, 0, 128, XT, tt, 8, td_, xtt)
            tc = P.act(lambda e, b=b, tt=tt: e.activation(ct[:, tt, :], b[:, 0:128], AF.Copy), tk, fr)
            done(i, tc)
            tc = P.act(lambda e, tt=tt: e.activation(rel[0][:, 0:128], ct[:, tt, :], AF.Square, accum_out=ss[:, tt:tt + 1]), fr)
        unit_done(ud, tk)
        for j in range(4):
            i, b, tk = proj_f(wq, 128 * j, 128, XT, 8, tq_, xtt)
            t1 = evac(qF[:, j, :], b[:, :], tk, fr)
            done(i, t1)
        unit_done(uq, tk)
        i, b, fb = bank()
        tk = P.pe([tr(b[:, j * 128:(j + 1) * 128], wuk[:, j * 128:(j + 1) * 128], ident[:, :]) for j in range(4)], tw, fb)
        t1 = evac(wukT.rearrange("p a n -> p (a n)"), b[:, :], tk, fr)
        done(i, t1)
        rs, rt = rsq(ss, NT, 1.0 / 128, 1e-6, tc)
        for tt in range(NT):
            tc = P.dve(lambda e, tt=tt: e.tensor_scalar(ct[:, tt, :], ct[:, tt, :], rs[:, tt:tt + 1], None, A.mult), rt)
        i, b, fb = bank()
        tk = P.pe([tr(b[:, j * 128:(j + 1) * 128], ct[:, j, :], ident[:, :]) for j in range(4)], tc, fb)
        tcT = evac(cT, b[:, :], tk, fr, scale=pcol("kv_norm_2"))
        done(i, tcT)
        ready = P.now("act", "dve")
        relf = [fr] * 4
        n = 0
        tbm = {0: None}
        for qt in range(1, NT):
            nk = 128 * (qt + 1)
            for h in range(4):
                s = n % 4
                n += 1
                hs = slice((h % 2) * 64, (h % 2) * 64 + 64)
                i, b, fb = bank()
                tk = P.pe([mm(b[:, 0:nk], QI[hs, h // 2, qt * 128:(qt + 1) * 128], KI[hs, 0:nk], True, True)], ready, fb)
                ta = P.act(lambda e, b=b, s=s, nk=nk: e.activation(rel[s][:, 0:nk], b[:, 0:nk], AF.Relu), tk, relf[s])
                done(i, ta)
                if h == 0:
                    tv = P.dve(lambda e, s=s, nk=nk, w=WI[:, qt, 0:1]: e.tensor_scalar(acc[:, 0:nk], rel[s][:, 0:nk], w, None, A.mult), ta, fr)
                else:
                    tv = P.dve(lambda e, s=s, nk=nk, w=WI[:, qt, h:h + 1]: e.scalar_tensor_tensor(acc[:, 0:nk], rel[s][:, 0:nk], w, acc[:, 0:nk], A.mult, A.add), ta)
                relf[s] = tv
            av, wv_, ev, cv = acc[:, 0:nk], work[:, 0:nk], eq[:, 0:nk], cum[:, 0:nk]
            P.dve(lambda e, nk=nk: e.tensor_tensor(acc[:, nk - 128:nk], acc[:, nk - 128:nk], diagm[:, :], A.add))
            m8 = st(8)
            for r_ in range(16):
                src = av if r_ == 0 else wv_
                P.dve(lambda e, src=src, m8=m8: e.max(m8, src))
                if r_ < 15:
                    P.dve(lambda e, src=src, m8=m8, wv_=wv_: e.match_replace(wv_, m8, src, -3.0e38))
            thr = m8[:, 7:8]
            need = st(1)
            P.dve(lambda e, a=av, o=wv_, thr=thr: e.tensor_scalar(o, a, thr, None, A.is_gt))
            P.dve(lambda e, o=wv_, need=need: e.tensor_reduce(need, o, AX, A.add))
            P.dve(lambda e, need=need: e.tensor_scalar(need, need, -1.0, 128.0, A.mult, A.add))
            P.dve(lambda e, a=av, o=ev, thr=thr: e.tensor_scalar(o, a, thr, None, A.is_equal))
            P.dve(lambda e, a=ev, o=cv: e.tensor_tensor_scan(o, a, a, 0.0, A.add, A.max))
            P.dve(lambda e, a=cv, o=ev, need=need: e.scalar_tensor_tensor(o, a, need, o, A.is_le, A.mult))
            P.dve(lambda e, a=wv_, o=ev: e.tensor_tensor(o, a, o, A.add))
            tbm[qt] = P.dve(lambda e, a=ev, o=BM[:, qt, 0:nk]: e.tensor_scalar(o, a, 1.0, -NEG, A.subtract, A.mult), fr)
        qlf, pbf, pTf, oTf = [fr] * 2, [fr] * 4, [fr] * 2, [fr] * 2
        n = 0
        for h in range(8):
            pt, q0 = h // 2, (h % 2) * 64
            hs = slice(q0, q0 + 64)
            s2 = h % 2
            i, b, fb = bank()
            tk = P.pe([mm(b[:, :], wukT[hs, pt, :], qF[hs, pt, :], True, True)], ready, fb)
            tql = evac(ql[s2], b[:, :], tk, qlf[s2])
            done(i, tql)
            io, bo, fo = bank()
            for qt in range(NT):
                nk = 128 * (qt + 1)
                s = n % 4
                sp = n % 2
                n += 1
                stt = st(3)
                p_ = pb[s][:, 0:nk]
                i, b, fb = bank()
                tk = P.pe([mm(b[:, 0:nk], ql[s2][:, qt * 128:(qt + 1) * 128], cT[:, 0:nk], True, True)], tql, tcT, fb)
                bias = diagm[:, :] if qt == 0 else BM[:, qt, 0:nk]
                t1 = P.dve(lambda e, p_=p_, b=b, nk=nk, bias=bias, m=stt[:, 0:1]: e.tensor_tensor_reduce(p_, b[:, 0:nk], bias, 1.0, -3.0e38, A.add, A.max, m), tk, pbf[s])
                done(i, t1)
                t1 = P.dve(lambda e, m=stt[:, 0:1]: e.tensor_scalar(m, m, -0.125, None, A.mult))
                t2 = P.act(lambda e, p_=p_, m=stt: e.activation(p_, p_, AF.Exp, bias=m[:, 0:1], scale=0.125, accum_out=m[:, 1:2]), t1)
                P.dve(lambda e, m=stt: e.reciprocal(m[:, 2:3], m[:, 1:2]), t2)
                t3 = P.dve(lambda e, p_=p_, m=stt: e.tensor_scalar(p_, p_, m[:, 2:3], None, A.mult))
                i, b, fb = bank()
                tk = P.pe([tr(b[:, j * 128:(j + 1) * 128], p_[:, j * 128:(j + 1) * 128], ident[:, :]) for j in range(qt + 1)], t3, fb)
                pbf[s] = tk
                t4 = P.act(lambda e, b=b, nk=nk, d=pT[sp][:, 0:nk]: e.activation(d, b[:, 0:nk], AF.Copy), tk, pTf[sp])
                done(i, t4)
                tk = P.pe([mm(bo[:, qt * 128:(qt + 1) * 128], ct[:, j, :], pT[sp][:, j * 128:(j + 1) * 128], j == 0, j == qt) for j in range(qt + 1)], t4, fo)
                pTf[sp] = tk
            qlf[s2] = tk
            t5 = P.act(lambda e, bo=bo, s2=s2: e.activation(oT[s2], bo[:, :], AF.Identity, scale=pcol("kv_norm_2")), tk, oTf[s2])
            done(io, t5)
            i, b, fb = bank()
            tk = P.pe([mm(b[hs, :], wuv[:, h * 64:(h + 1) * 64], oT[s2], True, True)], t5, fb, tw)
            oTf[s2] = tk
            t6 = P.act(lambda e, b=b, hs=hs, pt=pt: e.activation(YB[hs, pt, :], b[hs, :], AF.Copy), tk, fr)
            done(i, t6)
        nbg = st(16)
        tyb = [t6, P.dve(lambda e: e.tensor_scalar(nbg, pcols("b_gate_2", 16), -1.0, None, A.mult))]
        fr1 = P.now()
        E4, Y4 = scv(4, 4), scv(5, 4)
        tx = gated(w_in, 2756, t["w_proj_a_2"][0], YA, tya, t["w_proj_b_2"][0], YB, tyb, nbg,
                   t["w_out_2"][0], xtt, scv(2, 8, 2), ([E4[:, 0, :], E4[:, 1, :]], [Y4[:, 0, :], Y4[:, 1, :]]), fr1)
        keep['x'] = tx
        if dbg.get('cut') != 2:
            cross(tx)

    def cross(tx):
        fr = P.now()
        MEM, MN, MT = scv(0, 2), scv(1, 2), scv(2, 8)
        qF, kT, V = scv(3, 8, 2), scv(5, 8), scv(6, 2)
        pb = [SC[:, 7, 256 * i:256 * (i + 1)] for i in range(4)]
        PT = [SC[:, 8, 1024 * i:1024 * (i + 1)].rearrange("p (a n) -> p a n", a=2) for i in range(2)]
        oT = scv(9, 8, 2)
        tm = P.dma("act", lambda e: e.dma_start(MEM, t["mem_2"][0].rearrange("(t p) n -> p t n", p=128)), "mem", fr)
        rm, rmt = rms(MEM, 2, D, tm)
        tmt = to_xt(MEM, 2, rm, rmt, pcols("norm_mem_2", 8), MT, MN, fr)
        rs, rt = rms(X, NT, D, tx)
        xtt = to_xt(X, NT, rs, rt, pcols("norm_cross_2", 8), XT, scv(9, 4, 2), fr)
        for half in range(2):
            u_, s_, ut = wcols(t["w_ckv_2"][0], half * 512, 512)
            wv = s_.rearrange("p (k n) -> p k n", k=8)
            for j in range(4):
                i, b, tk = proj_f(wv, j * 128, 128, MT, 8, ut, tmt)
                t1 = evac(kT[:, half * 4 + j, :], b[:, 0:256], tk, fr)
                done(i, t1)
            unit_done(u_, tk)
        for half in range(2):
            u_, s_, ut = wcols(t["w_ckv_2"][0], 1024 + half * 512, 512)
            wv = s_.rearrange("p (k n) -> p k n", k=8)
            for j in range(2):
                i, b, tk = proj_t(wv, 0, 512, MT, j, 8, ut, tmt)
                t1 = evac(V[:, j, half * 512:(half + 1) * 512], b[:, :], tk, fr)
                done(i, t1)
            unit_done(u_, tk)
        for half in range(2):
            u_, s_, ut = wcols(t["w_cq_2"][0], half * 512, 512)
            wv = s_.rearrange("p (k n) -> p k n", k=8)
            for j in range(4):
                i, b, tk = proj_f(wv, j * 128, 128, XT, 8, ut, xtt)
                t1 = evac(qF[:, half * 4 + j, :], b[:, :], tk, fr)
                done(i, t1)
            unit_done(u_, tk)
        ready = P.now("act", "dve", "pe")
        pbf, PTf = [fr] * 4, [fr] * 2
        n = 0
        for h in range(4):
            s2 = h % 2
            for qt in range(NT):
                s = n % 4
                n += 1
                stt = st(3)
                i, b, fb = bank()
                tk = P.pe([mm(b[:, 0:256], qF[:, 2 * h + c, qt * 128:(qt + 1) * 128], kT[:, 2 * h + c, :], c == 0, c == 1) for c in range(2)], ready, fb)
                P.dve(lambda e, b=b, m=stt[:, 0:1]: e.tensor_reduce(m, b[:, 0:256], AX, A.max), tk)
                t1 = P.dve(lambda e, m=stt[:, 0:1]: e.tensor_scalar(m, m, -0.0625, None, A.mult))
                t2 = P.act(lambda e, p_=pb[s], b=b, m=stt: e.activation(p_, b[:, 0:256], AF.Exp, bias=m[:, 0:1], scale=0.0625, accum_out=m[:, 1:2]), t1, pbf[s])
                done(i, t2)
                P.dve(lambda e, m=stt: e.reciprocal(m[:, 2:3], m[:, 1:2]), t2)
                t3 = P.dve(lambda e, p_=pb[s], m=stt: e.tensor_scalar(p_, p_, m[:, 2:3], None, A.mult))
                i, b, fb = bank()
                tk = P.pe([tr(b[:, j * 128:(j + 1) * 128], pb[s][:, j * 128:(j + 1) * 128], ident[:, :]) for j in range(2)], t3, fb)
                pbf[s] = tk
                tp = P.act(lambda e, b=b, d=PT[s2][:, :, qt * 128:(qt + 1) * 128]: e.activation(d, b[:, 0:256].rearrange("p (a n) -> p a n", a=2), AF.Copy), tk, PTf[s2])
                done(i, tp)
            for c in range(2):
                i, b, fb = bank()
                tk = P.pe([mm(b[:, :], V[:, m, h * 256 + c * 128:h * 256 + (c + 1) * 128], PT[s2][:, m, :], m == 0, m == 1) for m in range(2)], tp, fb)
                to = evac(oT[:, 2 * h + c, :], b[:, :], tk, ready)
                done(i, to)
            PTf[s2] = tk
        keep["x"] = [add_proj(t["w_co_2"][0], oT, P.now("act", "dve"))]

    def finish():
        stn[0] = 0
        fr = P.now()
        gr = scv(0, 2)[:, 0, :]
        Y = scv(1, 4, 2)
        tg = P.dma("act", lambda e: e.dma_start(gr, t["norm_final_2"].rearrange("(a n) -> a n", a=1).to_broadcast([128, D])), "fg", fr)
        rs, rt = rms(X, NT, D, fr)
        for i in range(NT):
            t1 = P.dve(lambda e, i=i: e.scalar_tensor_tensor(Y[:, i, :], X[:, i, :], rs[:, i:i + 1], gr, A.mult, A.mult), rt, tg)
            P.dma("sp", lambda e, i=i: e.dma_start(out[0, i * 128:(i + 1) * 128, :], Y[:, i, :]), "out", t1)


    keep = {}
    ST_KEEP = 0
    phases = [block1_mix, lambda: moe(0), block2_mix, lambda: moe(1), finish]
    for n, ph in enumerate(phases):
        if dbg.get("start", 0) <= n < dbg.get("stop", 9):
            ph()
    for f in dbg.get("dumps", []):
        P.dma("act", (lambda f: lambda e: f(e, X, SC, XT))(f), "dump", P.now())
    block = ctx.enter_context(nc.Block())
    for nm, deco in (("sp", block.sync), ("act", block.scalar), ("dve", block.vector), ("pool", block.gpsimd), ("pe", block.tensor)):
        @deco
        def _(e, nm=nm):
            P.emit(nm, e)
            if nm == "act" and "dump" in P.sems:
                e.wait_ge(P.sems["dump"], P.n["dump"])
            if nm == "sp" and "out" in P.sems:
                e.wait_ge(P.sems["out"], P.n["out"])


_INS = ["x", "norm_mix", "w_in", "hg_lb", "hg_out_norm", "da_q_norm", "da_k_norm", "da_lambda", "da_out_norm",
        "w_branch_hg", "w_branch_da", "w_out", "norm_moe", "w_router_group", "b_router_group", "w_router_expert",
        "b_router_expert", "w1", "w3", "w2", "mem_2", "norm_mix_2", "w_in_2", "shift_mu_2", "rw_w0_2", "rw_w2_2",
        "rw_a0_2", "rw_a2_2", "rw_g2_2", "rw_k_k_2", "rw_k_a_2", "rw_r_k_2", "rw_ln_w_2", "rw_ln_b_2", "kv_norm_2",
        "w_uk_2", "w_uv_2", "w_proj_a_2", "w_proj_b_2", "b_gate_2", "w_out_2", "norm_cross_2", "norm_mem_2", "w_cq_2",
        "w_ckv_2", "w_co_2", "norm_ffn_2", "w_router_g_2", "b_router_g_2", "w_router_e_2", "b_router_e_2",
        "w_e_gate_2", "w_e_up_2", "w_e_down_2", "norm_final_2"]


def rope_tables():
    half = 32
    inv = np.float32(10000.0) ** (-np.arange(half, dtype=np.float32) / np.float32(half))
    ang = np.arange(T, dtype=np.float32)[:, None] * inv.astype(np.float32)[None, :]
    return np.cos(ang).astype(np.float32), np.sin(ang).astype(np.float32)


def kernel(**inputs):
    import concourse.bacc as _bacc
    from concourse.bass_utils import run_bass_kernel_spmd as _run

    nc = _bacc.Bacc("TRN2", target_bir_lowering=False, num_devices=1, dynamic_dma_scratch_size=8192)
    arrays, t = {}, {}
    cos, sin = rope_tables()
    for name, a in [(n, np.ascontiguousarray(inputs[n])) for n in _INS] + [("rope_cos", cos), ("rope_sin", sin)]:
        arrays[f"in_{name}"] = a
        t[name] = nc.dram_tensor(f"in_{name}", a.shape, F, kind="ExternalInput").ap()
    out = nc.dram_tensor("out_0", (1, T, D), F, kind="ExternalOutput").ap()
    program(nc, t, out, {})
    r = _run(nc, [arrays], core_ids=[0])
    return r.results[0]["out_0"]
```

```python
import math
from contextlib import ExitStack

import numpy as np
import concourse.bass as bass
from concourse import mybir

F = mybir.dt.float32
I32 = mybir.dt.int32
U32 = mybir.dt.uint32
A = mybir.AluOpType
AF = mybir.ActivationFunctionType
AX = mybir.AxisListType.X
ENG = ("sp", "act", "dve", "pool", "pe")

T = 512
NT = 4
D = 1024
NEG = -1.0e30
CAP = 64
NE = 32
NOV = 16
NRING = 4
NSC = 12
LAM_INIT = 0.8 - 0.6 * math.exp(0.0)


class Prog:

    def __init__(self, nc, ctx, tag):
        self.nc = nc
        self.q = {e: [] for e in ENG}
        self.sem = {e: ctx.enter_context(nc.semaphore(f"{tag}_{e}")) for e in ENG if e != "sp"}
        self.sems = dict(self.sem)
        self.n = {}
        self.tag = tag
        self.ctx = ctx
        self.fin = {}
        self.clk = {}
        self.end = 0
        self.marks = None

    def flat(self, deps, out):
        for d in deps:
            if d is None:
                continue
            if isinstance(d, list):
                self.flat(d, out)
            else:
                out.append(d)
        return out

    def count(self, name, by):
        self.n[name] = self.n.get(name, 0) + by
        if self.marks is not None and name in ENG:
            self.marks[name] = self.n[name]
        return (name, self.n[name])

    def now(self, *engs):
        n = self.n if self.marks is None else self.marks
        return [(e, n[e]) for e in (engs or ("act", "dve", "pool", "pe")) if n.get(e)]

    def guess(self, eng, tok, deps, ns):
        t = max([self.clk.get(eng, 0)] + [self.fin.get(d, 0) for d in deps]) + ns
        self.clk[eng] = t
        self.fin[tok] = t + 500
        self.end = max(self.end, t + 500)

    def weave(self, *gens):
        base = dict(self.n)
        t0 = max(self.clk.values())
        live = [[t0, n, g, dict(base)] for n, g in enumerate(gens)]
        while live:
            s = min(live, key=lambda s: (s[0], s[1]))
            self.marks = s[3]
            self.end = 0
            try:
                next(s[2])
            except StopIteration:
                live.remove(s)
                continue
            if self.end:
                s[0] = self.end
            else:
                s[0] = min([o[0] for o in live if o is not s] or [s[0]]) + 1
        self.marks = None

    def op(self, eng, fn, *deps, ns=400):
        deps = self.flat(deps, [])
        if eng != "pe" and self.n.get(eng):
            deps.append((eng, self.n[eng]))
        tok = self.count(eng, 1)
        self.guess(eng, tok, deps, ns)
        self.q[eng].append((deps, fn, eng, 1))
        return tok

    def dve(self, fn, *deps):
        return self.op("dve", fn, *deps)

    def act(self, fn, *deps):
        return self.op("act", fn, *deps)

    def pool(self, fn, *deps):
        return self.op("pool", fn, *deps)

    def pe(self, fns, *deps):
        def run(e):
            for f in fns:
                last = f(e)
            return last
        return self.op("pe", run, *deps, ns=sum(f.ns for f in fns))

    def dma(self, eng, fn, sem, *deps):
        if sem not in self.sems:
            self.sems[sem] = self.ctx.enter_context(self.nc.semaphore(f"{self.tag}_{sem}"))
        tok = self.count(sem, 16)
        self.fin[tok] = max([self.fin.get(d, 0) for d in self.flat(deps, [])] + [self.clk.get("pe", 0)]) + 4000
        self.q[eng].append((self.flat(deps, []), fn, sem, 16))
        return tok

    def raw(self, eng, fn, *deps):
        self.q[eng].append((self.flat(deps, []), fn, None, 0))

    def emit(self, eng, e, start=0, end=None, seen=None):
        seen = {} if seen is None else seen
        for deps, fn, sem, by in self.q[eng][start:end]:
            for name, val in deps:
                if seen.get(name, 0) < val:
                    e.wait_ge(self.sems[name], val)
                    seen[name] = val
            ins = fn(e)
            if sem is not None:
                ins.then_inc(self.sems[sem], by)


def mm(out, l, r, st, sp):
    def f(e):
        return e.matmul(out, l, r, start=st, stop=sp, skip_group_check=True)
    f.ns = 60 + 1.7 * math.prod(out.shape[1:])
    return f


def tr(out, in_, ident):
    def f(e):
        return e.transpose(out, in_, ident)
    f.ns = 60 + 1.7 * math.prod(out.shape[1:])
    return f


PARAMS = [("norm_mix", 8), ("hg_lb", 8), ("hg_out_norm", 1), ("da_out_norm", 1), ("norm_mix_2", 8),
          ("shift_mu_2", 14), ("rw_w0_2", 4), ("rw_a0_2", 4), ("rw_k_k_2", 4), ("rw_k_a_2", 4),
          ("rw_r_k_2", 4), ("rw_ln_w_2", 4), ("rw_ln_b_2", 4), ("b_gate_2", 16),
          ("norm_cross_2", 8), ("norm_mem_2", 8), ("kv_norm_2", 1)]


def program(nc, t, out, dbg):
    with ExitStack() as ctx:
        build(nc, ctx, t, out, dbg)


def build(nc, ctx, t, out, dbg):
    P = Prog(nc, ctx, "m")

    def sb(name, shape, dt=F):
        return ctx.enter_context(nc.sbuf_tensor(name, shape, dt))

    X = sb("X", [128, NT, D])
    XT = sb("XT", [128, 8, T])
    RING = sb("RING", [128, NRING, 4096])
    SC = sb("SC", [128, NSC, 2048])
    ST = sb("ST", [128, 1400])
    PR = SC[:, NSC - 1, 0:128]
    PC = sb("PC", [128, 128])
    ident = sb("ident", [128, 128])
    CH = sb("CH", [128, T])
    mk = sb("mk", [128, 4, 128], mybir.dt.int8)
    mband = sb("mband", [128, 6, 128], mybir.dt.int8)
    diagm = sb("diagm", [128, 128])
    PS = [ctx.enter_context(nc.psum_tensor(f"ps{i}", [128, 512], F)) for i in range(8)]
    ytab = nc.dram_tensor("ytab", [2 * T, D], F, kind="Internal").ap()
    xkeep = nc.dram_tensor("xkeep", [T, D], F, kind="Internal").ap()
    xrows = nc.dram_tensor("xrows", [T, D], F, kind="Internal").ap()
    tabs = [nc.dram_tensor(f"tab{i}", [(NE + NOV) * CAP, 1], I32, kind="Internal").ap() for i in range(2)]

    stn = [0]

    def st(n):
        a = ST[:, stn[0]:stn[0] + n]
        stn[0] += n
        assert stn[0] <= 1400, stn
        return a

    bank_no = [0]
    bank_free = [[] for _ in range(8)]

    def bank():
        assert any(f is not None for f in bank_free)
        while bank_free[bank_no[0] % 8] is None:
            bank_no[0] += 1
        i = bank_no[0] % 8
        bank_no[0] += 1
        free = bank_free[i]
        bank_free[i] = None
        return i, PS[i], free

    def done(i, *toks):
        bank_free[i] = list(toks)

    ring_no = [0]
    slots = [RING[:, i, :] for i in range(NRING)]
    ring_free = [[] for _ in range(NRING)]

    def unit(srcs):
        i = ring_no[0] % len(slots)
        ring_no[0] += 1
        slot = slots[i]
        free = ring_free[i]
        assert free is not None
        ring_free[i] = None
        tok = None
        for dst, src in srcs:
            tok = P.dma("sp", (lambda d, s: lambda e: e.dma_start(d, s))(dst(slot), src), f"ring{i}", free)
        return i, slot, tok

    def unit_done(i, *toks):
        ring_free[i] = list(toks)

    def wcols(w, c0, n):
        return unit([(lambda s: s[:, 0:8 * n].rearrange("p (k n) -> p k n", k=8),
                      w.rearrange("(k p) n -> p k n", p=128)[:, :, c0:c0 + n])])

    flip = [0]

    def evac(dst, src, *deps, scale=None):
        flip[0] += 1
        if flip[0] % 2:
            if scale is None:
                return P.act(lambda e: e.activation(dst, src, AF.Copy), *deps)
            return P.act(lambda e: e.activation(dst, src, AF.Identity, scale=scale), *deps)
        if scale is None:
            return P.dve(lambda e: e.tensor_copy(dst, src), *deps)
        return P.dve(lambda e: e.tensor_scalar(dst, src, scale, None, A.mult), *deps)

    def rsq(src, n, scale, eps, *deps):
        a, y, u = st(n), st(n), st(n)
        t0 = P.dve(lambda e: e.tensor_scalar(a, src, scale, eps, A.mult, A.add), *deps)
        t1 = P.act(lambda e: e.activation(y, a, AF.Ln), t0)
        t1 = P.act(lambda e: e.activation(y, y, AF.Exp, scale=-0.5), t1)
        P.dve(lambda e: e.scalar_tensor_tensor(u, y, -0.5, y, A.mult, A.mult), t1)
        P.dve(lambda e: e.tensor_tensor(u, u, a, A.mult))
        return y, P.dve(lambda e: e.scalar_tensor_tensor(y, u, 1.5, y, A.add, A.mult))

    ld = []
    for tt in range(NT):
        ld.append(P.dma("act", (lambda tt: lambda e: e.dma_start(X[:, tt, :], t["x"][0, tt * 128:(tt + 1) * 128, :]))(tt), "x"))
    x_in = ld[-1]
    col = {}
    row = 0
    for name, n in PARAMS:
        v = t[name]
        if name == "rw_r_k_2":
            v = v.rearrange("l h n -> l (h n)")
        v = v.rearrange("l n -> (l n)") if len(v.shape) == 2 else v
        tok = P.dma("act", (lambda v, row, n: lambda e: e.dma_start(PR[row:row + n, :], v.rearrange("(a b) -> a b", b=128)))(v, row, n), "par")
        col[name] = row
        row += n
    NPR = row
    G64 = sb("G64", [128, 2, 64])
    LAMP = sb("LAMP", [128, 256])
    ROPE = sb("ROPE", [128, 2, NT, 32])
    RB = sb("RB", [128, 2, 36])
    WR = sb("WR", [128, 2, 8, 36])
    tok = P.dma("act", lambda e: e.dma_start(G64[:, 0, :], t["da_q_norm"].to_broadcast([128, 64])), "par")
    tok = P.dma("act", lambda e: e.dma_start(G64[:, 1, :], t["da_k_norm"].to_broadcast([128, 64])), "par")
    tok = P.dma("act", lambda e: e.dma_start(LAMP[:, :], t["da_lambda"].rearrange("l a b -> l (a b)").to_broadcast([128, 256])), "par")
    tok = P.dma("act", lambda e: e.dma_start(ROPE[:, 0, :, :], t["rope_cos"].rearrange("(t p) n -> p t n", p=128)), "par")
    tok = P.dma("act", lambda e: e.dma_start(ROPE[:, 1, :, :], t["rope_sin"].rearrange("(t p) n -> p t n", p=128)), "par")
    for b, (g, e_) in enumerate((("router_group", "router_expert"), ("router_g_2", "router_e_2"))):
        tok = P.dma("act", (lambda b, g: lambda e: e.dma_start(RB[:, b, 0:4], t["b_" + g].to_broadcast([128, 4])))(b, g), "par")
        tok = P.dma("act", (lambda b, g: lambda e: e.dma_start(RB[:, b, 4:36], t["b_" + g].to_broadcast([128, 32])))(b, e_), "par")
        tok = P.dma("act", (lambda b, g: lambda e: e.dma_start(WR[:, b, :, 0:4], t["w_" + g][0].rearrange("(k p) n -> p k n", p=128)))(b, g), "par")
        tok = P.dma("act", (lambda b, g: lambda e: e.dma_start(WR[:, b, :, 4:36], t["w_" + g][0].rearrange("(k p) n -> p k n", p=128)))(b, e_), "par")
    par = tok

    ones = sb("ones", [128, 128])
    upper = sb("upper", [128, 128])
    BO = sb("BO", [128, 128])
    iotf = sb("iotf", [128, 40])
    iotm = sb("iotm", [128, 8])
    ival = sb("ival", [128, 2, NT], I32)
    tmpm = SC[:, NSC - 2, 0:1024]
    P.pool(lambda e: e.memset(ones[:, :], 1.0))

    def sel(dst, src, pattern, op, fill, base, cm):
        return P.pool(lambda e: e.affine_select(out=dst, in_=src, pattern=pattern, compare_op=op, fill=fill, base=base, channel_multiplier=cm))

    P.pool(lambda e: e.memset(ident[:, :], 0.0))
    sel(ident[:, :], ident[:, :], [[-1, 128]], A.not_equal, 1.0, 0, 1)
    sel(upper[:, :], ones[:, :], [[1, 128]], A.is_gt, 0.0, 0, -1)
    P.pool(lambda e: e.memset(diagm[:, :], 0.0))
    sel(diagm[:, :], diagm[:, :], [[-1, 128]], A.is_ge, NEG, 0, 1)
    P.pool(lambda e: e.memset(BO[:, :], 0.0))
    P.pool(lambda e: e.memset(BO[0:64, 0:64], 1.0))
    P.pool(lambda e: e.memset(BO[64:128, 64:128], 1.0))
    P.pool(lambda e: e.memset(CH[:, :], 1.0))
    P.pool(lambda e: e.memset(CH[:, :].rearrange("p (c j) -> p c j", j=64)[:, :, 0], 0.0))
    P.pool(lambda e: e.iota(iotf[:, :], [[1, 40]], base=0, channel_multiplier=0, allow_small_or_imprecise_dtypes=True))
    P.pool(lambda e: e.iota(iotm[:, :], [[1, 8]], base=-8, channel_multiplier=0, allow_small_or_imprecise_dtypes=True))
    for k in range(2):
        P.pool((lambda k: lambda e: e.iota(ival[:, k, :], [[256, NT]], base=k, channel_multiplier=2))(k))
    m0, m1, m16, m32 = (tmpm[:, 128 * i:128 * (i + 1)] for i in range(4))
    BOv = BO[:, :]

    def blocks(dst, size):
        v = dst.rearrange("p (a b) -> p a b", b=size)
        sel(v, ones[:, :].rearrange("p (a b) -> p a b", b=size), [[-size, 128 // size], [0, size]], A.is_ge, 0.0, 0, 1)
        sel(v, v, [[size, 128 // size], [0, size]], A.is_ge, 0.0, size - 1, -1)

    blocks(m16, 16)
    blocks(m32, 32)
    u = tmpm[:, 512:640]
    w = tmpm[:, 640:768]
    lower = tmpm[:, 768:896]
    sel(lower, ones[:, :], [[-1, 128]], A.is_gt, 0.0, 0, 1)
    sel(m0, BOv, [[1, 128]], A.is_ge, 0.0, 0, -1)
    tk = P.pool(lambda e: e.tensor_copy(mk[:, 0, :], m0))

    def band(i, tri, hi, lo):
        P.pool(lambda e: e.tensor_tensor(u, tri, hi, A.mult))
        if lo is not None:
            P.pool(lambda e: e.tensor_tensor(w, u, lo, A.mult))
            P.pool(lambda e: e.tensor_tensor(u, u, w, A.subtract))
        return P.pool(lambda e: e.tensor_copy(mband[:, i, :], u))

    band(0, upper[:, :], m16, None)
    band(1, lower, m16, None)
    band(2, upper[:, :], m32, m16)
    band(3, lower, m32, m16)
    band(4, lower, BOv, m32)
    cst = band(5, upper[:, :], BOv, None)

    i, b, fr = bank()
    tk = P.pe([tr(b[:, 0:NPR], PR[0:NPR, :], ident[0:NPR, 0:NPR])], cst, par)
    pc = P.dve(lambda e: e.tensor_copy(PC[:, 0:NPR], b[:, 0:NPR]), tk)
    done(i, pc)

    def pcol(name, j=0):
        c = col[name] + j
        return PC[:, c:c + 1]

    def pcols(name, n):
        return PC[:, col[name]:col[name] + n]

    def scv(i, a, n=1):
        v = SC[:, i:i + n, :].rearrange("p s b -> p (s b)")
        return v.rearrange("p (a b) -> p a b", a=a)

    def rms(src, nt, n, *deps):
        ss = st(nt)
        junk = SC[:, NSC - 1, 0:n]
        for i in range(nt):
            tk = P.act((lambda i: lambda e: e.activation(junk, src[:, i, :], AF.Square, accum_out=ss[:, i:i + 1]))(i), *deps)
        return rsq(ss, nt, 1.0 / n, 1e-6, tk)

    def to_xt(src, nt, rs, rtok, gain, dst, xn, free):
        tk = None
        for i in range(nt):
            tk = P.dve((lambda i: lambda e: e.tensor_scalar(xn[:, i, :], src[:, i, :], rs[:, i:i + 1], None, A.mult))(i), rtok, free)
        return transposed(xn, nt, gain, dst, tk, free)

    def transposed(xn, nt, gain, dst, tk, free):
        out_ = []
        for k in range(8):
            i, b, fr = bank()
            t1 = P.pe([tr(b[:, j * 128:(j + 1) * 128], xn[:, j, k * 128:(k + 1) * 128], ident[:, :]) for j in range(nt)], tk, fr, cst)
            t2 = evac(dst[:, k, :], b[:, 0:nt * 128], t1, free, pc, scale=None if gain is None else gain[:, k:k + 1])
            done(i, t2)
            out_.append(t2)
        return out_[-2:]

    def proj_f(wv, c, n, rhs, nk, *deps, at=0, bk=None):
        if bk is None:
            bk = bank()
        i, b, fr = bk
        N = rhs.shape[-1]
        tk = P.pe([mm(b[at:at + n, 0:N], wv[:, k, c:c + n], rhs[:, k, :], k == 0, k == nk - 1) for k in range(nk)], fr, *deps)
        return i, b, tk

    def proj_t(wv, c, n, lhs, tt, nk, *deps):
        i, b, fr = bank()
        tk = P.pe([mm(b[:, 0:n], lhs[:, k, tt * 128:(tt + 1) * 128], wv[:, k, c:c + n], k == 0, k == nk - 1) for k in range(nk)], fr, *deps)
        return i, b, tk

    def gated(wgate, gcol0, wa, ya, ya_t, wb, yb, yb_t, bias, wout, xtt, mbuf, tmp, free, tx=None):
        E, Y = tmp
        last = [free] * 2
        for br, (w_, y, yt) in enumerate(((wa, ya, ya_t), (wb, yb, yb_t))):
            wu, ws, wt = unit([(lambda s: s.rearrange("p (k n) -> p k n", k=4), w_.rearrange("(k p) n -> p k n", p=128))])
            wv = ws.rearrange("p (k n) -> p k n", k=4)
            for half in range(2):
                gu, gs, gt = wcols(wgate, gcol0 + br * 1024 + half * 512, 512)
                gv = gs.rearrange("p (k n) -> p k n", k=8)
                for j in range(4):
                    dt_ = half * 4 + j
                    s_ = dt_ % 2
                    e_, y_ = E[s_], Y[s_]
                    i, b, tk = proj_f(gv, j * 128, 128, XT, 8, gt, xtt)
                    nb = None if bias is None else bias[:, br * 8 + dt_:br * 8 + dt_ + 1]
                    ta = P.act((lambda e_, b, nb: lambda e: e.activation(e_, b[:, :], AF.Exp, scale=-1.0, **({} if nb is None else {"bias": nb})))(e_, b, nb), tk, last[s_])
                    done(i, ta)
                    P.dve((lambda e_: lambda e: e.tensor_scalar(e_, e_, 1.0, None, A.add))(e_), ta)
                    P.dve((lambda e_: lambda e: e.reciprocal(e_, e_))(e_))
                    i2, b2, tk2 = proj_f(wv, dt_ * 128, 128, y, 4, wt, yt)
                    dst = mbuf[:, dt_, :] if br == 0 else y_
                    tv = P.dve((lambda dst, e_, b2: lambda e: e.tensor_tensor(dst, e_, b2[:, :], A.mult))(dst, e_, b2), tk2, free)
                    done(i2, tv)
                    last[s_] = tv
                    if br == 1:
                        tv = last[s_] = P.dve((lambda m, y_: lambda e: e.tensor_tensor(m, m, y_, A.add))(mbuf[:, dt_, :], y_))
                unit_done(gu, tk)
            unit_done(wu, tk2)
        return add_proj(wout, mbuf, [tv, tx])

    def add_proj(wout, src, tv):
        for half in range(2):
            u_, s_, wt = wcols(wout, half * 512, 512)
            v = s_.rearrange("p (k n) -> p k n", k=8)
            for tt in range(NT):
                i, b, tk = proj_t(v, 0, 512, src, tt, 8, wt, tv)
                xs = X[:, tt, half * 512:(half + 1) * 512]
                tx = P.dve((lambda xs, b: lambda e: e.tensor_tensor(xs, xs, b[:, :], A.add))(xs, b), tk)
                done(i, tx)
            unit_done(u_, tk)
        return tx


    def heads_out(o, tok, n, gain, dst, const, free, mul=None, bias=None):
        ss = st(16)
        junk = SC[:, NSC - 1, 0:2048]
        t1 = P.act(lambda e: e.activation(junk, o.rearrange("p a b -> p (a b)"), AF.Square), tok)
        t2 = P.dve(lambda e: e.tensor_reduce(ss, junk.rearrange("p (a b) -> p a b", b=128), AX, A.add), t1)
        rs, t3 = rsq(ss, 16, 1.0 / 128, 1e-6, t2)
        ov = o.rearrange("p a (h b) -> p (a h) b", b=128)
        t4 = P.dve(lambda e: e.tensor_tensor(ov, ov, rs.unsqueeze(2).to_broadcast([128, 16, 128]), A.mult), t3)
        if mul is not None:
            t4 = P.dve(lambda e: e.tensor_tensor(o, o, mul, A.mult))
        g = st(1)
        t5 = P.dve(lambda e: e.tensor_scalar(g, gain, const, None, A.mult), pc)
        outs = []
        for h in range(4):
            i, b, fr = bank()
            t6 = P.pe([tr(b[:, j * 128:(j + 1) * 128], o[:, j, h * 128:(h + 1) * 128], ident[:, :]) for j in range(NT)], t4, fr)
            t7 = evac(dst[:, h, :], b[:, :], t6, t5, free, scale=g)
            done(i, t7)
            outs.append(t7)
        return outs[-2:]

    def block1_mix():
        rs, rt = rms(X, NT, D, x_in, pc)
        xn = scv(8, 4, 2)
        xtt = to_xt(X, NT, rs, rt, pcols("norm_mix", 8), XT, xn, cst)
        keep["xt1"] = xtt
        w_in = t["w_in"][0]
        q, k, b_, qr, kr, v, og, kt, o, E = (scv(i, 4) for i in (0, 1, 2, 3, 4, 5, 6, 7, 8, 9))
        SB = scv(10, 4)
        lb, oml, l1, l2 = st(4), st(4), st(4), st(4)
        a0, a1 = pcols("hg_lb", 8)[:, 0:4], pcols("hg_lb", 8)[:, 4:8]
        P.dve(lambda e: e.tensor_tensor(lb, a0, a1, A.max))
        P.dve(lambda e: e.tensor_tensor(l1, a0, lb, A.subtract))
        t1 = P.dve(lambda e: e.tensor_tensor(l2, a1, lb, A.subtract))
        P.act(lambda e: e.activation(l1, l1, AF.Exp), t1)
        t1 = P.act(lambda e: e.activation(l2, l2, AF.Exp))
        P.dve(lambda e: e.tensor_tensor(l2, l1, l2, A.add), t1)
        P.dve(lambda e: e.reciprocal(l2, l2))
        P.dve(lambda e: e.tensor_tensor(lb, l1, l2, A.mult))
        P.dve(lambda e: e.tensor_scalar(oml, lb, -1.0, 1.0, A.mult, A.add))

        u_, s_, ut = wcols(w_in, 0, 512)
        wv = s_.rearrange("p (k n) -> p k n", k=8)
        for h in range(4):
            i, b, tk = proj_f(wv, h * 128, 128, XT, 8, ut, xtt)
            tq = evac(q[:, h, :], b[:, :], tk)
            done(i, tq)
        unit_done(u_, tk)
        qdone = P.now("act", "dve")
        u_, s_, ut = wcols(w_in, 512, 512)
        wv2 = s_.rearrange("p (k n) -> p k n", k=8)
        for h in range(4):
            i, b, tk = proj_f(wv2, h * 128, 128, XT, 8, ut, xtt)
            kh, lh, bh = k[:, h, :], qr[:, h, :], b_[:, h, :]
            ta = P.act(lambda e, kh=kh, b=b: e.activation(kh, b[:, :], AF.Exp, scale=-1.0), tk)
            done(i, ta)
            P.dve(lambda e, kh=kh: e.tensor_scalar(kh, kh, 1.0, None, A.add), ta)
            P.dve(lambda e, kh=kh: e.reciprocal(kh, kh))
            tf = P.dve(lambda e, kh=kh, h=h: e.tensor_scalar(kh, kh, oml[:, h:h + 1], lb[:, h:h + 1], A.mult, A.add))
            tl = P.act(lambda e, kh=kh, lh=lh: e.activation(lh, kh, AF.Ln), tf)
            P.dve(lambda e, kh=kh: e.tensor_scalar(kh, kh, -1.0, 1.0, A.mult, A.add), tl)
            P.dve(lambda e, bh=bh, lh=lh: e.tensor_tensor_scan(bh, CH[:, :], lh, 0.0, A.mult, A.add), tl, cst)
        unit_done(u_, tk)

        def ch(x):
            return x.rearrange("p h (c j) -> p (h c) j", j=64)

        bc = ch(b_)
        eref, eend = st(32), st(32)
        P.dve(lambda e: e.tensor_tensor(ch(qr), bc, bc[:, :, 31:32].to_broadcast([128, 32, 64]), A.subtract))
        t1 = P.dve(lambda e: e.tensor_tensor(eend, bc[:, :, 63], bc[:, :, 31], A.subtract))
        P.act(lambda e: e.activation(eend, eend, AF.Exp), t1)
        P.act(lambda e: e.activation(eref, bc[:, :, 31], AF.Exp))
        P.act(lambda e: e.activation(kr, qr, AF.Exp, scale=-1.0))
        t1 = P.act(lambda e: e.activation(qr, qr, AF.Exp))
        P.dve(lambda e: e.tensor_tensor(kr, kr, k, A.mult), t1)
        tqk = P.dve(lambda e: e.tensor_tensor(qr, qr, q, A.mult), qdone)
        er, ee = (x.rearrange("p (h c) -> p h c", h=4) for x in (eref, eend))
        tes = P.dve(lambda e: e.tensor_tensor(ee[:, :, 0:7], ee[:, :, 0:7], er[:, :, 1:8], A.mult))

        u_, s_, ut = wcols(w_in, 1024, 512)
        wv3 = s_.rearrange("p (k n) -> p k n", k=8)
        for tt in range(NT):
            i, b, tk = proj_t(wv3, 0, 512, XT, tt, 8, ut, xtt)
            tv = evac(v[:, tt, :], b[:, :], tk)
            done(i, tv)
        unit_done(u_, tk)
        vdone = P.now("act", "dve")
        u_, s_, ut = wcols(w_in, 1536, 512)
        wv4 = s_.rearrange("p (k n) -> p k n", k=8)
        for tt in range(NT):
            i, b, tk = proj_t(wv4, 0, 512, XT, tt, 8, ut, xtt)
            e_ = E[:, tt, :]
            ta = P.act(lambda e, e_=e_, b=b: e.activation(e_, b[:, :], AF.Exp, scale=-1.0), tk, xtt)
            P.dve(lambda e, e_=e_: e.tensor_scalar(e_, e_, 1.0, None, A.add), ta)
            P.dve(lambda e, e_=e_: e.reciprocal(e_, e_))
            tv = P.dve(lambda e, e_=e_, b=b, tt=tt: e.tensor_tensor(og[:, tt, :], e_, b[:, :], A.mult))
            done(i, tv)
        unit_done(u_, tk)
        for tt in range(NT):
            i, b, fr = bank()
            t2 = P.pe([tr(b[:, h * 128:(h + 1) * 128], kr[:, h, tt * 128:(tt + 1) * 128], ident[:, :]) for h in range(4)], tqk, fr)
            tkt = evac(kt[:, tt, :], b[:, :], t2)
            done(i, tkt)
        ktdone = P.now("act", "dve")
        tz = P.dve(lambda e: e.memset(SC[:, 10, :], 0.0), cst)
        free_sc = [tz, tz]
        mfree = [tz, tz]
        tm = tz
        mask = mk[:, 0, :].unsqueeze(1).to_broadcast([128, 4, 128])
        for tt in range(NT):
            i, b, fr = bank()
            cs = slice(tt * 128, (tt + 1) * 128)
            t2 = P.pe([mm(b[:, h * 128:(h + 1) * 128], kr[:, h, cs], qr[:, h, cs], True, True) for h in range(4)], tqk, fr)
            scm = SB[:, tt % 2, :]
            t3 = P.dve(lambda e, scm=scm, b=b: e.copy_predicated(scm.rearrange("p (h n) -> p h n", h=4), mask, b[:, :].rearrange("p (h n) -> p h n", h=4)), t2, free_sc[tt % 2])
            done(i, t3)
            i, b, fr = bank()
            t4 = P.pe([mm(b[:, h * 128:(h + 1) * 128], scm[:, h * 128:(h + 1) * 128], v[:, tt, h * 128:(h + 1) * 128], h == 0, tt == 0) for h in range(4)], t3, fr, vdone)
            free_sc[tt % 2] = t4
            for hb in range(2):
                c = 2 * tt + hb
                c0 = c * 64
                p0 = hb * 64
                M = SB[:, 2 + c % 2, :]
                Mn = SB[:, 2 + (c + 1) % 2, :]
                if c:
                    t4 = P.pe([mm(b[p0:p0 + 64, h * 128:(h + 1) * 128], qr[:, h, c0:c0 + 64], M[:, h * 128:(h + 1) * 128], False, True) for h in range(4)], tm)
                    mfree[c % 2] = t4
                if c < 7:
                    i2, b2, fr2 = bank()
                    t5 = P.pe([mm(b2[:, h * 128:(h + 1) * 128], kt[p0:p0 + 64, tt, h * 128:(h + 1) * 128], v[p0:p0 + 64, tt, h * 128:(h + 1) * 128], True, True) for h in range(4)], fr2, ktdone)
                    t6 = P.dve(lambda e, M=M, Mn=Mn, b2=b2: e.tensor_tensor(Mn, M, b2[:, :], A.add), t5, mfree[(c + 1) % 2])
                    done(i2, t6)
                    tm = P.dve(lambda e, Mn=Mn, c=c: e.tensor_tensor(Mn.rearrange("p (h n) -> p h n", h=4), Mn.rearrange("p (h n) -> p h n", h=4), ee[:, :, c:c + 1].to_broadcast([128, 4, 128]), A.mult), tes)
            t7 = evac(o[:, tt, :], b[:, :], t4)
            done(i, t7)
        ohg = scv(1, 4)
        toh = heads_out(o, P.now("act", "dve"), 128, pcol("hg_out_norm"), ohg, 1.0, P.now(), mul=og)

        fr0 = P.now()
        dq, dk, dv, E1, E2, qT, kT, o2, odT = (scv(i, 4) for i in (0, 2, 3, 4, 5, 6, 8, 0, 7))
        raws = {}
        for n, dst in ((0, dq), (1, dk), (2, dv)):
            u_, s_, ut = wcols(w_in, 2048 + 512 * n, 512)
            wn = s_.rearrange("p (k n) -> p k n", k=8)
            for tt in range(NT):
                i, b, tk = proj_t(wn, 0, 512, XT, tt, 8, ut, xtt)
                tv = evac(dst[:, tt, :], b[:, :], tk, fr0)
                done(i, tv)
            unit_done(u_, tk)
        dvdone = P.now("act", "dve")
        for n, (src, dstT) in enumerate(((dq, qT), (dk, kT))):
            ss = st(32)
            t1 = P.act(lambda e, src=src: e.activation(E1, src, AF.Square), dvdone, P.now("pe"))
            t2 = P.dve(lambda e, ss=ss: e.tensor_reduce(ss, E1.rearrange("p a (j b) -> p (a j) b", b=64), AX, A.add), t1)
            rs_, t3 = rsq(ss, 32, 1.0 / 64, 1e-6, t2)
            sv = src.rearrange("p a (j b) -> p (a j) b", b=64)
            P.dve(lambda e, sv=sv, rs_=rs_: e.tensor_tensor(sv, sv, rs_.unsqueeze(2).to_broadcast([128, 32, 64]), A.mult), t3)
            P.dve(lambda e, sv=sv, n=n: e.tensor_tensor(sv, sv, G64[:, n:n + 1, :].to_broadcast([128, 32, 64]), A.mult), par)
            for tt in range(NT):
                s3 = src[:, tt, :].rearrange("p (j b) -> p j b", b=64)
                x1, x2 = s3[:, :, 0:32], s3[:, :, 32:64]
                e1 = E1[:, tt, :].rearrange("p (j b) -> p j b", b=64)
                e2 = E2[:, tt, :].rearrange("p (j b) -> p j b", b=64)
                cb = ROPE[:, 0, tt:tt + 1, :].to_broadcast([128, 8, 32])
                sb_ = ROPE[:, 1, tt:tt + 1, :].to_broadcast([128, 8, 32])
                P.dve(lambda e, a=e1[:, :, 0:32], x=x1, c=cb: e.tensor_tensor(a, x, c, A.mult), t1)
                P.dve(lambda e, a=e1[:, :, 32:64], x=x2, c=cb: e.tensor_tensor(a, x, c, A.mult))
                P.dve(lambda e, a=e2[:, :, 0:32], x=x2, c=sb_: e.tensor_tensor(a, x, c, A.mult))
                P.dve(lambda e, a=e2[:, :, 32:64], x=x1, c=sb_: e.tensor_tensor(a, x, c, A.mult))
                P.dve(lambda e, a=x1, x=e1[:, :, 0:32], y=e2[:, :, 0:32]: e.tensor_tensor(a, x, y, A.subtract))
                tx = P.dve(lambda e, a=x2, x=e1[:, :, 32:64], y=e2[:, :, 32:64]: e.tensor_tensor(a, x, y, A.add))
            for h in range(4):
                i, b, fr = bank()
                t6 = P.pe([tr(b[:, j * 128:(j + 1) * 128], src[:, j, h * 128:(h + 1) * 128], ident[:, :]) for j in range(NT)], tx, fr)
                t7 = evac(dstT[:, h, :], b[:, :], t6, fr0)
                done(i, t7)
        tqk = P.now("act", "dve", "pe")
        l = st(4)
        P.dve(lambda e: e.tensor_tensor_reduce(LAMP[:, 0:64], LAMP[:, 0:64], LAMP[:, 64:128], 1.0, 0.0, A.mult, A.add, l[:, 0:1]), par)
        t1 = P.dve(lambda e: e.tensor_tensor_reduce(LAMP[:, 128:192], LAMP[:, 128:192], LAMP[:, 192:256], 1.0, 0.0, A.mult, A.add, l[:, 1:2]))
        t1 = P.act(lambda e: e.activation(l[:, 0:2], l[:, 0:2], AF.Exp), t1)
        P.dve(lambda e: e.tensor_tensor(l[:, 2:3], l[:, 1:2], l[:, 0:1], A.subtract), t1)
        P.dve(lambda e: e.tensor_scalar(l[:, 3:4], l[:, 2:3], -LAM_INIT, None, A.add))
        nlam = l[:, 3:4]
        pfree = [tqk, tqk]
        afree = [tqk, tqk]
        n = 0
        for qt in range(NT):
            nk = 128 * (qt + 1)
            io, bo, fro = bank()
            for h in range(4):
                s = n % 2
                n += 1
                sts = st(8)
                ps = []
                for c in range(2):
                    i, b, fr = bank()
                    t2 = P.pe([mm(b[:, 0:nk], qT[64 * c:64 * c + 64, h, qt * 128:(qt + 1) * 128], kT[64 * c:64 * c + 64, h, 0:nk], True, True)], tqk, fr)
                    P.dve(lambda e, b=b, nk=nk: e.tensor_tensor(b[:, nk - 128:nk], b[:, nk - 128:nk], diagm[:, :], A.add), t2, cst)
                    P.dve(lambda e, b=b, nk=nk, m=sts[:, c:c + 1]: e.tensor_reduce(m, b[:, 0:nk], AX, A.max))
                    t3 = P.dve(lambda e, m=sts[:, c:c + 1]: e.tensor_scalar(m, m, -0.125, None, A.mult))
                    p_ = E1[:, 2 * s + c, 0:nk]
                    t4 = P.act(lambda e, p_=p_, b=b, nk=nk, m=sts[:, c:c + 1], z=sts[:, 2 + c:3 + c]: e.activation(p_, b[:, 0:nk], AF.Exp, bias=m, scale=0.125, accum_out=z), t3, pfree[s])
                    done(i, t4)
                    ps.append(p_)
                P.dve(lambda e, a=sts: e.reciprocal(a[:, 4:6], a[:, 2:4]), t4)
                P.dve(lambda e, a=sts: e.tensor_tensor(a[:, 5:6], a[:, 5:6], nlam, A.mult))
                P.dve(lambda e, a=sts, p=ps[1]: e.tensor_scalar(p, p, a[:, 5:6], None, A.mult))
                t5 = P.dve(lambda e, a=sts, p=ps[0], p1=ps[1]: e.scalar_tensor_tensor(p, p, a[:, 4:5], p1, A.mult, A.add))
                i, b, fr = bank()
                t6 = P.pe([tr(b[:, j * 128:(j + 1) * 128], ps[0][:, j * 128:(j + 1) * 128], ident[:, :]) for j in range(qt + 1)], t5, fr)
                pfree[s] = t6
                aT = E2[:, s, 0:nk]
                t7 = evac(aT, b[:, 0:nk], t6, afree[s])
                done(i, t7)
                t8 = P.pe([mm(bo[:, h * 128:(h + 1) * 128], aT[:, j * 128:(j + 1) * 128], dv[:, j, h * 128:(h + 1) * 128], j == 0, j == qt) for j in range(qt + 1)], t7, fro)
                afree[s] = t8
            t9 = evac(o2[:, qt, :], bo[:, :], t8, tqk)
            done(io, t9)
        tod = heads_out(o2, P.now("act", "dve"), 128, pcol("da_out_norm"), odT, 1.0 - LAM_INIT, P.now())
        fr1 = P.now()
        mb = scv(2, 8, 2)
        E4, Y4 = scv(4, 4), scv(5, 4)
        keep["x1"] = gated(w_in, 3584, t["w_branch_hg"][0], ohg, toh, t["w_branch_da"][0], odT, tod, None,
                           t["w_out"][0], xtt, mb, ([E4[:, 0, :], E4[:, 1, :]], [Y4[:, 0, :], Y4[:, 1, :]]), fr1)

    def first_hot(dst, vals, mx, n, *deps):
        tmp, m = st(NT * n).rearrange("p (a b) -> p a b", b=n), st(NT)
        io = iotm[:, 0:n].unsqueeze(1).to_broadcast([128, NT, n])
        P.dve(lambda e: e.tensor_tensor(dst, vals, mx.unsqueeze(2).to_broadcast([128, NT, n]), A.is_equal), *deps)
        P.dve(lambda e: e.tensor_tensor(tmp, dst, io, A.mult))
        P.dve(lambda e: e.tensor_reduce(m, tmp, AX, A.min))
        return P.dve(lambda e: e.tensor_tensor(dst, io, m.unsqueeze(2).to_broadcast([128, NT, n]), A.is_equal))

    def moe(bi):
        stn[0] = ST_KEEP
        wa, wb, wc, gname = ((("w1", "w3", "w2", "norm_moe"), ("w_e_gate_2", "w_e_up_2", "w_e_down_2", "norm_ffn_2"))[bi])
        W1, W3, W2 = t[wa][0], t[wb][0], t[wc][0]
        tab = tabs[bi]
        fr = P.now()
        xn = scv(0, 4, 2)
        gr = scv(2, 2)[:, 0, :]
        tg = P.dma("act", lambda e: e.dma_start(gr, t[gname].to_broadcast([128, D])), f"moeg{bi}", fr)
        rs, rt = rms(X, NT, D, fr)
        for i in range(NT):
            P.dve(lambda e, i=i: e.tensor_scalar(xn[:, i, :], X[:, i, :], rs[:, i:i + 1], None, A.mult), rt)
            tx = P.dve(lambda e, i=i: e.tensor_tensor(xn[:, i, :], xn[:, i, :], gr, A.mult), tg)
        txr = P.dma("act", lambda e: e.dma_start(xrows.rearrange("(t p) n -> p t n", p=128), xn), f"moex{bi}", tx)
        xtt = transposed(xn, NT, None, XT, tx, fr)
        i, b, frb = bank()
        for tt in range(NT):
            tk = P.pe([mm(b[:, tt * 64:tt * 64 + 36], XT[:, k, tt * 128:(tt + 1) * 128], WR[:, bi, k, :], k == 0, k == 7) for k in range(8)], frb, xtt, par)
        L = st(NT * 36).rearrange("p (a b) -> p a b", b=36)
        tl = P.dve(lambda e, b=b: e.tensor_tensor(L, b[:, 0:256].rearrange("p (a b) -> p a b", b=64)[:, :, 0:36], RB[:, bi:bi + 1, :].to_broadcast([128, NT, 36]), A.add), tk)
        done(i, tl)
        gl = L[:, :, 0:4]

        def s3(n):
            return st(NT * n).rearrange("p (a b) -> p a b", b=n)

        gm, gs, goh, ge, ein, tmp8, oh1, oh2 = st(NT), st(NT), s3(4), s3(4), s3(8), s3(8), s3(8), s3(8)
        P.dve(lambda e: e.tensor_reduce(gm, gl, AX, A.max))
        t1 = P.dve(lambda e: e.tensor_tensor(ge, gl, gm.unsqueeze(2).to_broadcast([128, NT, 4]), A.subtract))
        t1 = P.act(lambda e: e.activation(ge, ge, AF.Exp), t1)
        P.dve(lambda e: e.tensor_reduce(gs, ge, AX, A.add), t1)
        P.dve(lambda e: e.reciprocal(gs, gs))
        first_hot(goh, gl, gm, 4)
        for g in range(4):
            dst = ein if g == 0 else tmp8
            P.dve(lambda e, g=g, dst=dst: e.tensor_tensor(dst, L[:, :, 4 + 8 * g:12 + 8 * g], goh[:, :, g:g + 1].to_broadcast([128, NT, 8]), A.mult))
            if g:
                P.dve(lambda e: e.tensor_tensor(ein, ein, tmp8, A.add))
        v1, v2, g1, g2 = st(NT), st(NT), st(NT), st(NT)
        P.dve(lambda e: e.tensor_reduce(v1, ein, AX, A.max))
        first_hot(oh1, ein, v1, 8)
        P.dve(lambda e: e.scalar_tensor_tensor(tmp8, oh1, NEG, ein, A.mult, A.add))
        P.dve(lambda e: e.tensor_reduce(v2, tmp8, AX, A.max))
        first_hot(oh2, tmp8, v2, 8)
        t1 = P.dve(lambda e: e.tensor_tensor(v2, v2, v1, A.subtract))
        t1 = P.act(lambda e: e.activation(v2, v2, AF.Exp), t1)
        P.dve(lambda e: e.tensor_scalar(v1, v2, 1.0, None, A.add), t1)
        P.dve(lambda e: e.reciprocal(v1, v1))
        P.dve(lambda e: e.tensor_tensor(g1, v1, gs, A.mult))
        P.dve(lambda e: e.tensor_tensor(g2, g1, v2, A.mult))
        OH = [s3(32), s3(32)]
        M = s3(32)
        for k, oh in ((0, oh1), (1, oh2)):
            for g in range(4):
                P.dve(lambda e, k=k, g=g, oh=oh: e.tensor_tensor(OH[k][:, :, 8 * g:8 * g + 8], oh, goh[:, :, g:g + 1].to_broadcast([128, NT, 8]), A.mult))
        tM = P.dve(lambda e: e.tensor_tensor(M, OH[0], OH[1], A.add))
        i, b, frb = bank()
        for tt in range(NT):
            o_ = b[:, 32 * tt:32 * tt + 32]
            tk = P.pe([mm(o_, ones[:, :], M[:, j, :], j == 0, False) for j in range(tt)] + [mm(o_, upper[:, :], M[:, tt, :], tt == 0, True)], frb, tM, cst)
        tk = P.pe([mm(b[:, 128:160], ones[:, :], M[:, j, :], j == 0, j == 3) for j in range(NT)])
        tot, ov, ove, hi, lo = st(32), st(32), st(32), st(32), st(32)
        pos, c1 = s3(32), s3(32)
        P.dve(lambda e, b=b: e.tensor_copy(tot, b[:, 128:160]), tk)
        P.dve(lambda e: e.tensor_scalar(ov, tot, float(CAP), None, A.is_gt))
        for m in range(2, T // CAP):
            P.dve(lambda e, m=m: e.tensor_scalar(ove, tot, float(CAP * m), None, A.is_gt))
            P.dve(lambda e: e.tensor_tensor(ov, ov, ove, A.add))
        P.dve(lambda e: e.tensor_tensor_scan(ove, ones[:, 0:32], ov, 0.0, A.mult, A.add), cst)
        P.dve(lambda e: e.tensor_tensor(hi, ove, ov, A.subtract))
        P.dve(lambda e: e.tensor_scalar(hi, hi, float(CAP), float((NE - 1) * CAP), A.mult, A.add))
        P.dve(lambda e: e.tensor_scalar(lo, iotf[:, 0:32], float(CAP), None, A.mult))
        P.dve(lambda e: e.tensor_tensor(lo, lo, hi, A.subtract))
        tp = P.dve(lambda e, b=b: e.tensor_copy(pos, b[:, 0:128].rearrange("p (a b) -> p a b", b=32)))
        done(i, tp)
        P.dve(lambda e: e.tensor_scalar(c1, pos, float(CAP), None, A.is_lt))
        P.dve(lambda e: e.tensor_tensor(c1, c1, lo.unsqueeze(1).to_broadcast([128, NT, 32]), A.mult))
        P.dve(lambda e: e.tensor_tensor(pos, pos, c1, A.add))
        P.dve(lambda e: e.tensor_tensor(pos, pos, hi.unsqueeze(1).to_broadcast([128, NT, 32]), A.add))
        pk, pki = st(2 * NT).rearrange("p (a b) -> p a b", a=2), st(2 * NT).bitcast(I32).rearrange("p (a b) -> p a b", a=2)
        for k in range(2):
            P.dve(lambda e, k=k: e.tensor_tensor(OH[k], OH[k], pos, A.mult))
            P.dve(lambda e, k=k: e.tensor_reduce(pk[:, k, :], OH[k], AX, A.add))
        tpk = P.dve(lambda e: e.tensor_copy(pki, pk))
        exb, nov = st(NOV), st(NOV + 1).bitcast(I32)
        for j in range(NOV):
            P.dve(lambda e, j=j: e.tensor_scalar(ov, ove, float(j), None, A.is_le))
            P.dve(lambda e, j=j: e.tensor_reduce(exb[:, j:j + 1], ov, AX, A.add))
        P.dve(lambda e: e.tensor_scalar(exb, exb, float(NE - 1), None, A.min))
        P.dve(lambda e: e.tensor_copy(nov[:, 0:NOV], exb))
        tnov = P.dve(lambda e: e.tensor_copy(nov[:, NOV:NOV + 1], ove[:, 31:32]))
        NS = (NE + NOV) * CAP // 128
        fill = SC[:, 4, 0:128].bitcast(I32)
        t1 = P.pool(lambda e: e.memset(fill, 4 * T), fr)
        t1 = P.dma("pool", lambda e: e.dma_start(tab.rearrange("(a b) c -> a (b c)", b=128), fill[0:NS, :]), f"tf{bi}", t1)
        tsc = None
        for k in range(2):
            for tt in range(NT):
                tsc = P.dma("pool", lambda e, k=k, tt=tt: e.indirect_dma_start(tab, bass.IndirectOffsetOnAxis(ap=pki[:, k, tt:tt + 1], axis=0), ival[:, k, tt:tt + 1], None), f"ts{bi}", t1, tpk, cst)
        tb, tbf = SC[:, 4, 128:256].bitcast(I32), SC[:, 4, 256:384]
        t2 = P.dma("pool", lambda e: e.dma_start(tb[0:NS, :], tab.rearrange("(a b) c -> a (b c)", b=128)), f"tr{bi}", tsc)
        t2 = P.dve(lambda e: e.tensor_copy(tbf[0:NS, :], tb[0:NS, :]), t2, fr)
        i, b, frb = bank()
        tk = P.pe([tr(b[:, 0:NS], tbf[0:NS, :], ident[0:NS, 0:NS])], t2, frb)
        sidx, gidx = SC[:, 4, 384:384 + NS].bitcast(I32), SC[:, 4, 448:448 + NS].bitcast(I32)
        t3 = P.dve(lambda e, b=b: e.tensor_copy(sidx, b[:, 0:NS]), tk)
        done(i, t3)
        tix = P.dve(lambda e: e.tensor_scalar(gidx, sidx, 1, None, A.arith_shift_right))

        XG, YS, XE, HD, HT = scv(5, 2), scv(6, 2), scv(7, 2), scv(8, 4), scv(9, 4)
        tz = P.pool(lambda e: e.memset(SC[:, 5, :], 0.0), fr)
        HALF = (slice(0, 64), slice(64, 128))

        def gather(Q, p, rdy, fr_):
            s = p % 2
            return Q.dma("pool", lambda e: e.indirect_dma_start(XG[:, s, :], None, xrows, bass.IndirectOffsetOnAxis(ap=gidx[:, p:p + 1], axis=0), bounds_check=T - 1, oob_is_err=False), f"g{s}", rdy, fr_.get("xg"))

        def turn(Q, p, tg_, fr_):
            s = p % 2
            ts = []
            for hf in range(2):
                i, b, fb = bank()
                t2 = Q.pe([tr(b[:, j * 128:(j + 1) * 128], XG[:, s, (4 * hf + j) * 128:(4 * hf + j + 1) * 128], ident[:, :]) for j in range(4)], tg_, fb)
                dst = XE[:, s, hf * 512:(hf + 1) * 512]
                if hf == 0:
                    t3 = Q.act(lambda e, dst=dst, b=b: e.activation(dst, b[:, :], AF.Copy), t2, fr_.get("xe"))
                else:
                    t3 = Q.dve(lambda e, dst=dst, b=b: e.tensor_copy(dst, b[:, :]), t2, fr_.get("xe"))
                done(i, t3)
                ts.append(t3)
            return t2, ts

        def up(Q, p, tx_, w1, w3, fr_):
            s = p % 2
            hd = HD[:, s, :]
            ks = []
            for w_ in (w1, w3):
                i, b, fb = bank()
                ks.append((i, b, Q.pe([mm(b[HALF[x], :], XE[:, s, k * 128 + 64 * x:k * 128 + 64 * x + 64], w_[x][1][:, k, :], k == 0, k == 7) for k in range(8) for x in range(2)], tx_, fb, [u[2] for u in w_])))
            (i1, b1, k1), (i3, b3, k3) = ks
            ta = Q.act(lambda e: e.activation(hd, b1[:, :], AF.Silu), k1, fr_.get("hd"))
            done(i1, ta)
            th = Q.dve(lambda e: e.tensor_tensor(hd, hd, b3[:, :], A.mult), ta, k3)
            done(i3, th)
            return k1, k3, th

        def down(Q, p, th, w2, fr_):
            s = p % 2
            hd, ht, ys = HD[:, s, :], HT[:, s, :], YS[:, s, :]
            i, b, fb = bank()
            t2 = Q.pe([tr(b[:, j * 128:(j + 1) * 128], hd[:, j * 128:(j + 1) * 128], ident[:, :]) for j in range(4)], th, fb)
            t3 = Q.act(lambda e, b=b: e.activation(ht, b[:, :], AF.Copy), t2, fr_.get("ht"))
            done(i, t3)
            tys = []
            for hf in range(2):
                i, b, fb = bank()
                k2 = Q.pe([mm(b[HALF[x], :], ht[:, k * 128 + 64 * x:k * 128 + 64 * x + 64], w2[x][1][:, k, hf * 512:(hf + 1) * 512], k == 0, k == 3) for k in range(4) for x in range(2)], t3, fb, [u[2] for u in w2])
                dst = ys[:, hf * 512:(hf + 1) * 512]
                if hf:
                    ty = Q.act(lambda e, dst=dst, b=b: e.activation(dst, b[:, :], AF.Copy), k2, fr_.get("ys"))
                else:
                    ty = Q.dve(lambda e, dst=dst, b=b: e.tensor_copy(dst, b[:, :]), k2, fr_.get("ys"))
                done(i, ty)
                tys.append(ty)
            return t2, k2, tys

        def scatter(Q, p, tys):
            s = p % 2
            return Q.dma("pool", lambda e: e.indirect_dma_start(ytab, bass.IndirectOffsetOnAxis(ap=sidx[:, p:p + 1], axis=0), YS[:, s, :], None, bounds_check=2 * T - 1, oob_is_err=False), f"y{s}", tys)

        def pairs(Q, n, first, rdy, fr0_, weights, used, end_of=None):
            fr_ = [dict(fr0_), dict(fr0_)]
            tg_ = gather(Q, first, rdy, fr_[first % 2])
            t2, tx_ = turn(Q, first, tg_, fr_[first % 2])
            fr_[first % 2]["xg"] = t2
            ty = [None, None]
            for p in range(first, first + n):
                s = p % 2
                more = p + 1 < first + n
                w1 = weights(p, 0)
                w3 = weights(p, 1)
                if more and end_of is None:
                    tg_ = gather(Q, p + 1, rdy, fr_[1 - s])
                k1, k3, th = up(Q, p, tx_, w1, w3, fr_[s])
                fr_[s]["xe"] = k3
                used(w1, k1)
                used(w3, k3)
                if more and end_of is None:
                    t2, tx_ = turn(Q, p + 1, tg_, fr_[1 - s])
                    fr_[1 - s]["xg"] = t2
                w2 = weights(p, 2)
                t2, k2, tys = down(Q, p, th, w2, fr_[s])
                fr_[s]["hd"], fr_[s]["ht"] = t2, k2
                used(w2, k2)
                fr_[s]["ys"] = ty[s] = scatter(Q, p, tys)
                if end_of is not None:
                    end_of(p)
                    if more:
                        tg_ = gather(Q, p + 1, rdy, fr_[1 - s])
                        t2, tx_ = turn(Q, p + 1, tg_, fr_[1 - s])
                        fr_[1 - s]["xg"] = t2
            return ty

        def view(slot, j):
            return slot.rearrange("p (k n) -> p k n", k=4 if j == 2 else 8)

        def src(w_, e_):
            return w_[e_].rearrange("(k p) n -> p k n", p=128)

        def weights(p, j):
            us = [unit([(lambda sl, j=j: view(sl, j), src((W1, W3, W2)[j], 2 * p + x))]) for x in range(2)]
            return [(u_[0], view(u_[1], j), u_[2]) for u_ in us]

        def used(us, tok):
            for u_ in us:
                unit_done(u_[0], tok)

        spare = [SC[:, 10:12, :], SC[:, 2:4, :]]
        slots.extend(x.rearrange("p a b -> p (a b)") for x in spare)
        ring_free.extend([tx] + P.now() for _ in spare)
        while ring_no[0] % len(slots) != NRING:
            ring_no[0] += 1
        frx = {k: fr for k in ("xe", "hd", "ht", "ys")}
        ty = pairs(P, NE // 2, 0, [tix, txr, tz], frx, weights, used)
        O = Prog(nc, ctx, f"o{bi}")
        saved = list(bank_free), bank_no[0]
        for i in range(8):
            bank_free[i] = []
        segs = []
        wfree = [None] * 3

        def oweights(p, j):
            res = []
            for x in range(2):
                slot = slots[2 * j + x]

                def load(e, slot=slot, x=x):
                    o_ = 2 * (p - NE // 2) + x
                    v = e.value_load(nov[0:1, o_:o_ + 1], min_val=0, max_val=NE - 1)
                    return e.dma_start(view(slot, j), (W1, W3, W2)[j][bass.ds(v, 1)].rearrange("a (k p) n -> p (a k) n", p=128))

                tok = O.dma("sp", load, f"w{2 * j + x}", wfree[j])
                res.append((j, view(slot, j), tok))
            return res

        def oused(us, tok):
            wfree[us[0][0]] = tok

        pairs(O, NOV // 2, NE // 2, None, {}, oweights, oused,
              lambda p: segs.append(({g: len(O.q[g]) for g in ENG}, list(O.n.items()))))
        bank_free[:] = saved[0]
        bank_no[0] = saved[1]
        barrier = P.now() + ty + [tnov] + [(f"ring{i}", P.n[f"ring{i}"]) for i in range(len(slots))]

        def branch(eng):
            def run(e):
                v = e.value_load(nov[0:1, NOV:NOV + 1], min_val=0, max_val=NOV)
                seen, at = {}, 0
                for j, (to, ends) in enumerate(segs):
                    with e.If(v > 2 * j):
                        O.emit(eng, e, at, to[eng], seen)
                        for name, val in ends:
                            e.wait_ge(O.sems[name], val)
                    at = to[eng]
            return run

        toks = []
        if "join" not in P.sems:
            P.sems["join"] = ctx.enter_context(nc.semaphore("m_join"))
        for eng in ENG:
            P.raw(eng, branch(eng), barrier)
            tok = P.count("join", 1)
            P.raw(eng, lambda e: e.sem_inc(P.sems["join"], 1))
        del slots[NRING:], ring_free[NRING:]
        while ring_no[0] % NRING:
            ring_no[0] += 1
        for i in range(NRING):
            unit_done(i, tok)
        YB = [scv(0, 1, 1)[:, 0, :], scv(1, 1, 1)[:, 0, :]]
        fy = [tok, tok]
        for tt in range(NT):
            s = tt % 2
            ty = P.dma("act", lambda e, tt=tt, s=s: e.dma_start(YB[s], ytab.rearrange("(t p c) n -> t p (c n)", p=128, c=2)[tt]), f"yb{s}", tok, fy[s])
            for k, gk in ((0, g1), (1, g2)):
                fy[s] = P.dve(lambda e, k=k, gk=gk, tt=tt, s=s: e.scalar_tensor_tensor(X[:, tt, :], YB[s][:, k * D:(k + 1) * D], gk[:, tt:tt + 1], X[:, tt, :], A.mult, A.add), ty)
        keep["x"] = fy

    def block2_mix():
        stn[0] = 0
        w_in = t["w_in_2"][0]
        m0_ = P.now()
        rs, rt = rms(X, NT, D, m0_)
        xtt = to_xt(X, NT, rs, rt, pcols("norm_mix_2", 8), XT, scv(4, 4, 2), m0_)
        fr = P.now()
        QT, Y0, GH, BV, GT = scv(0, 4), scv(1, 4), SC[:, 2:4, :].rearrange("p s n -> p (s n)"), scv(4, 4), scv(5, 4)
        GTm = GH[:, 0:2048].rearrange("p (a n) -> p a n", a=4)
        Hm = GH[:, 2048:4096].rearrange("p (a n) -> p a n", a=4)
        tmp = [SC[:, 6 + i // 4, (i % 4) * 512:(i % 4 + 1) * 512] for i in range(22)]
        mu = pcols("shift_mu_2", 14)
        omu = st(14)
        P.dve(lambda e: e.tensor_scalar(omu, mu, -1.0, 1.0, A.mult, A.add))
        nw0, na0 = st(4), st(4)
        P.dve(lambda e: e.tensor_scalar(nw0, pcols("rw_w0_2", 4), -1.0, None, A.mult))
        tom = P.dve(lambda e: e.tensor_scalar(na0, pcols("rw_a0_2", 4), -1.0, None, A.mult))

        def shifted(wv, c, j, dst, wt, free=None):
            i, b, tk = proj_f(wv, c, 128, XT, 8, wt, xtt)
            ta = P.act(lambda e: e.activation(dst, b[:, :], AF.Identity, scale=omu[:, j:j + 1]), tk, tom, free)
            tv = P.dve(lambda e: e.scalar_tensor_tensor(dst[:, 1:512], b[:, 0:511], mu[:, j:j + 1], dst[:, 1:512], A.mult, A.add), ta)
            done(i, tv)
            return tk, tv

        wq = w_in.rearrange("(k p) n -> p k n", p=128)

        def part(o, n, c):
            return (lambda s: s[:, 0:3104].rearrange("p (k n) -> p k n", k=8)[:, :, o:o + n], wq[:, :, c:c + n])

        C_RW, C_Q, C_KV, C_QI, C_KI, C_WI = 0, 1792, 2304, 2432, 2688, 2752
        ul, sl, tl = unit([part(0, 256, 1536), part(256, 64, C_KI), part(320, 64, C_KI), part(384, 4, C_WI)])
        wl = sl[:, 0:3104].rearrange("p (k n) -> p k n", k=8)
        KI, WI = sb("KI", [128, T]), st(NT * 4).rearrange("p (a b) -> p a b", b=4)
        LW = tmp[18]
        XW, XG = tmp[20], tmp[21]
        tlw = P.dma("act", lambda e: e.dma_start(LW[0:64, :], t["rw_w2_2"][0]), "lw", fr)
        tlw = P.dma("act", lambda e: e.dma_start(LW[64:128, :], t["rw_a2_2"][0]), "lw")
        G2 = tmp[19]
        tlw = P.dma("act", lambda e: e.dma_start(G2, t["rw_g2_2"][0]), "lw")
        _, tv = shifted(wl, 0, 12, XW, tl, fr)
        txw = P.act(lambda e: e.activation(XW[0:64, :], XW[0:64, :], AF.Tanh), tv)
        _, tv = shifted(wl, 128, 13, XG, tl, fr)
        ta = P.act(lambda e: e.activation(XG, XG, AF.Exp, scale=-1.0), tv)
        P.dve(lambda e: e.tensor_scalar(XG, XG, 1.0, None, A.add), ta)
        txg = P.dve(lambda e: e.reciprocal(XG, XG))
        i, b, tk = proj_f(wl, 256, 128, XT, 8, tl, xtt)
        tki = P.act(lambda e, b=b: e.activation(KI[:, :], b[:, :], AF.Copy), tk)
        done(i, tki)
        for tt in range(NT):
            i, b, tk = proj_t(wl, 384, 4, XT, tt, 8, tl, xtt)
            twi = P.dve(lambda e, b=b, tt=tt: e.tensor_scalar(WI[:, tt, :], b[:, 0:4], 1.0 / 16.0, None, A.mult), tk)
            done(i, twi)
        unit_done(ul, tk)
        for j in range(4):
            i, b, fb = bank()
            tk = P.pe([mm(b[:, :], G2[:, j * 128:(j + 1) * 128], XG, True, True)], txg, tlw, fb)
            tg = evac(GT[:, j, :], b[:, :], tk, fr)
            done(i, tg)
        xs = P.dma("act", lambda e: e.dma_start(xkeep.rearrange("(t p) n -> p t n", p=128), X[:, :, :]), "xs", m0_)
        ESC = math.exp(-0.5)
        eref = st(32).rearrange("p (a c) -> p a c", a=4)
        eend = st(32).rearrange("p (a c) -> p a c", a=4)
        bufs = [tmp[0:11], tmp[11:18] + [tmp[19], tmp[21], SC[:, 11, 1024:1536], SC[:, 11, 1536:2048]]]
        rkv = {}
        lead = []
        used = {}

        def rkv_load(pt):
            slot = pt % 2
            sl = RING[:, slot, :]
            wv = sl[:, 0:3072].rearrange("p (k n) -> p k n", k=8)
            for n in range(3):
                tok = P.dma("sp", lambda e, n=n: e.dma_start(wv[:, :, 128 * n:128 * n + 128], wq[:, :, 512 * n + 128 * pt:512 * n + 128 * pt + 128]), f"rkv{slot}", ring_free[slot])
            rkv[pt] = (wv, tok)
            used[pt] = []

        def half(hf):
            t0 = hf * 256
            ts = slice(t0, t0 + 256)
            U = bufs[hf]
            H2 = [u[:, 256 * n:256 * n + 256] for u in U for n in range(2)]
            r, k, v, a, b_, kk, t6, t7, al, be, kR, rR = H2[0:12]
            fam = [fr]
            v2 = lambda x: x.rearrange("p (t n) -> p t n", n=128)
            aT, bT, kT, vT = (v2(x) for x in H2[12:16])
            n0 = 1 if hf else 0
            while hf and not lead:
                yield
            for pt in range(4):
                while pt not in rkv:
                    yield
                wv, wt = rkv[pt]
                pf = fam[0]
                for n, dst in enumerate((r, k, v)):
                    j = 4 * n + pt
                    i, b, fb = bank()
                    tk = P.pe([mm(b[:, 0:256 + n0], wv[:, kc, 128 * n:128 * n + 128], XT[:, kc, t0 - n0:t0 + 256], kc == 0, kc == 7) for kc in range(8)], fb, wt, xtt)
                    ta = P.act(lambda e, b=b, dst=dst, j=j: e.activation(dst, b[:, n0:256 + n0], AF.Identity, scale=omu[:, j:j + 1]), tk, tom, pf)
                    tv = P.dve(lambda e, b=b, dst=dst, j=j: e.scalar_tensor_tensor(dst[:, 1 - n0:256], b[:, 0:255 + n0], mu[:, j:j + 1], dst[:, 1 - n0:256], A.mult, A.add), ta)
                    done(i, tv)
                    yield
                used[pt].append(tk)
                if len(used[pt]) == 2:
                    ring_free[pt % 2] = list(used[pt])
                    if pt + 2 < 4:
                        rkv_load(pt + 2)
                for c0, bias, dst in ((64, na0, a), (0, nw0, t6)):
                    i, b, fb = bank()
                    tk = P.pe([mm(b[:, 0:256], LW[c0:c0 + 64, pt * 128:(pt + 1) * 128], XW[c0:c0 + 64, ts], True, True)], fb, txw, tlw, tom)
                    ta = P.act(lambda e, b=b, dst=dst, bias=bias, pt=pt: e.activation(dst, b[:, 0:256], AF.Exp, scale=-1.0, bias=bias[:, pt:pt + 1]), tk, pf)
                    done(i, ta)
                    yield
                for dst in (a, t6):
                    P.dve(lambda e, dst=dst: e.tensor_scalar(dst, dst, 1.0, None, A.add), ta)
                    P.dve(lambda e, dst=dst: e.reciprocal(dst, dst))
                    yield
                P.dve(lambda e: e.tensor_scalar(t6, t6, -ESC, None, A.mult))
                P.dve(lambda e: e.tensor_tensor_scan(b_, CH[:, 0:256], t6, 0.0, A.mult, A.add), pf)
                P.dve(lambda e: e.tensor_tensor(t6, b_, t6, A.subtract))
                yield
                P.dve(lambda e, pt=pt: e.tensor_scalar(kk, k, pcol("rw_k_k_2", pt), None, A.mult))
                tv = P.dve(lambda e: e.tensor_tensor(t7, kk, kk, A.mult))
                i, b, fb = bank()
                tk = P.pe([mm(b[:, 0:256], BO[:, :], t7, True, True)], tv, fb)
                yield
                t1 = P.dve(lambda e, b=b: e.tensor_scalar(t7, b[:, 0:256], 1e-24, 2.0 ** 20, A.max, A.mult), tk)
                done(i, t1)
                P.act(lambda e: e.activation(al, t7, AF.Ln), t1)
                t1 = P.act(lambda e: e.activation(al, al, AF.Exp, scale=-0.5))
                yield
                P.dve(lambda e, pt=pt: e.tensor_scalar(kR, a, 1.0, pcol("rw_k_a_2", pt), A.subtract, A.mult), pf)
                P.dve(lambda e: e.scalar_tensor_tensor(k, kR, 1.0, k, A.add, A.mult))
                P.dve(lambda e, pt=pt: e.tensor_scalar(kR, r, pcol("rw_r_k_2", pt), None, A.mult))
                tv = P.dve(lambda e: e.tensor_tensor(kR, kR, k, A.mult))
                i, b, fb = bank()
                tk = P.pe([mm(b[:, 0:256], BO[:, :], kR, True, True)], tv, fb)
                yield
                P.dve(lambda e: e.scalar_tensor_tensor(be, al, -0.5, al, A.mult, A.mult), t1, pf)
                P.dve(lambda e: e.tensor_tensor(be, be, t7, A.mult))
                P.dve(lambda e: e.scalar_tensor_tensor(al, be, 1.5, al, A.add, A.mult))
                P.dve(lambda e: e.scalar_tensor_tensor(kk, kk, 2.0 ** 10, al, A.mult, A.mult))
                yield
                tb = P.dve(lambda e, b=b, pt=pt: e.tensor_tensor(BV[:, pt, ts], v, b[:, 0:256], A.mult), tk, fr)
                done(i, tb)
                P.dve(lambda e: e.tensor_tensor(be, kk, a, A.mult))
                c3 = lambda x: x.rearrange("p (c j) -> p c j", j=64)
                bc, p3, s3_ = c3(b_), c3(t6), c3(t7)
                mid = bc[:, :, 31:32].to_broadcast([128, 4, 64])
                cr = slice(4 * hf, 4 * hf + 4)
                yield
                t1 = P.dve(lambda e, pt=pt: e.tensor_tensor(eend[:, pt, cr], bc[:, :, 63], bc[:, :, 31], A.subtract))
                P.dve(lambda e: e.tensor_tensor(p3, p3, mid, A.subtract))
                P.act(lambda e, pt=pt: e.activation(eend[:, pt, cr], eend[:, pt, cr], AF.Exp), t1)
                P.act(lambda e, pt=pt: e.activation(eref[:, pt, cr], bc[:, :, 31], AF.Exp))
                t1 = P.dve(lambda e: e.tensor_tensor(s3_, bc, mid, A.subtract))
                yield
                P.act(lambda e: e.activation(t6, t6, AF.Exp), t1)
                ta = P.act(lambda e: e.activation(rR, t7, AF.Exp), pf)
                t1 = P.act(lambda e: e.activation(t7, t7, AF.Exp, scale=-1.0))
                P.dve(lambda e: e.scalar_tensor_tensor(al, kk, -1.0, t6, A.mult, A.mult), ta)
                P.dve(lambda e: e.tensor_tensor(rR, rR, r, A.mult))
                P.dve(lambda e: e.tensor_tensor(be, be, t7, A.mult), t1)
                tf = P.dve(lambda e: e.tensor_tensor(kR, k, t7, A.mult))
                yield
                for (s0, s1), dst in (((al, be), U[6]), ((kR, v), U[7])):
                    i, b, fb = bank()
                    tk = P.pe([tr(b[:, 256 * n + j * 128:256 * n + (j + 1) * 128], src[:, j * 128:(j + 1) * 128], ident[:, :]) for n, src in enumerate((s0, s1)) for j in range(2)], tf, fb)
                    td = evac(dst, b[:, :], tk)
                    done(i, td)
                    yield
                tT = P.now("act", "dve", "pe")
                lead.append(pt)
                for par_ in range(2):
                    yield from head(par_, hf, pt, U, H2, aT, bT, kT, vT, tT, fam)
            halves[hf] = P.now()

        halves = {}

        def head(par_, hf, pt, U, H2, aT, bT, kT, vT, tT, fam):
            h = 2 * pt + par_
            q0 = par_ * 64
            hs = slice(q0, q0 + 64)
            tl0 = 2 * hf
            al, be, kR, rR = H2[8:12]
            N16, L16, N32, L32, Pm, Qm, N2, L2 = H2[0:8]
            L64, AkT, RbT, RkT, X1, X2 = H2[16:22]
            fz = [tT, fam[0]]
            for n in (0, 1, 8, 9):
                tz = P.pool(lambda e, u=U[n]: e.memset(u, 0.0), fz)
            yield

            def scores(prs, outs):
                i, b, fb = bank()
                tk = P.pe([mm(b[:, 256 * n + j * 128:256 * n + (j + 1) * 128], l[hs, j * 128:(j + 1) * 128], rr[hs, j * 128:(j + 1) * 128], True, True) for n, (l, rr) in enumerate(prs) for j in range(2)], fb, tT)
                for dst, mask, o, w_ in outs:
                    m = mask.unsqueeze(2).to_broadcast([128, w_, 2, 128])
                    tv = P.dve(lambda e, dst=dst, m=m, b=b, o=o, w_=w_: e.copy_predicated(dst.rearrange("p (a t n) -> p a t n", a=w_, n=128), m, b[:, 256 * o:256 * (o + w_)].rearrange("p (a t n) -> p a t n", a=w_, n=128)), tk, tz)
                done(i, tv)
                return tv

            tsc0 = scores([(be, al), (al, be)], [(U[0], mband[:, 0:2, :], 0, 2), (U[1], mband[:, 2:4, :], 0, 2), (L64, mband[:, 4:5, :], 1, 1)])
            yield

            def mul2(x, y, *deps, n=2):
                i, b, fb = bank()
                return i, b[:, 0:256 * n], P.pe([mm(b[:, 256 * m + j * 128:256 * m + (j + 1) * 128], x[m][:, j * 128:(j + 1) * 128], y[m][:, j * 128:(j + 1) * 128], True, True) for m in range(n) for j in range(2)], fb, *deps)

            def cp(dst, ibk, *deps):
                i, b, tk = ibk
                tv = P.act(lambda e: e.activation(dst, b, AF.Copy), tk, *deps)
                done(i, tv)
                return tv

            def addto(dst, ibk, *deps):
                i, b, tk = ibk
                tv = P.dve(lambda e: e.tensor_tensor(dst, dst, b, A.add), tk, *deps)
                done(i, tv)
                return tv

            v4 = lambda x: x.rearrange("p (t n) -> p t n", n=128)
            PQ = (Pm, Qm)
            tpq = P.dve(lambda e: e.tensor_tensor(v4(U[2]), v4(U[0]), ident[:, :].unsqueeze(1).to_broadcast([128, 4, 128]), A.add))
            cur, new = U[0], U[3]
            for lev in range(3):
                n_, l_ = cur[:, 0:256], cur[:, 256:512]
                c1 = cp(new, mul2((l_, n_), (n_, l_), tsc0 if lev == 0 else c1), fz)
                yield
                if lev == 0:
                    scores([(kR, al)], [(AkT, mband[:, 5:6, :], 0, 1)])
                if lev == 1:
                    tsc = scores([(be, rR), (kR, rR)], [(RbT, mk[:, 0:1, :], 0, 1), (RkT, mk[:, 0:1, :], 1, 1)])
                n_, l_ = new[:, 0:256], new[:, 256:512]
                tpq = addto(U[2], mul2((l_, n_), PQ, c1, tpq))
                yield
                cur, new = new, (U[10], U[3])[lev % 2]
            a1 = cp(U[0], mul2((L32, N32), PQ, tpq), P.now("pe"))
            yield
            tpq = addto(U[2], mul2((Qm, Pm), (N16, L16), a1))
            yield
            hc = slice(q0, q0 + 64)
            a1 = cp(N16, mul2((L64,), (Pm,), tpq, n=1))
            i, b, fb = bank()
            tk = P.pe([mm(b[:, j * 64:(j + 1) * 64], AkT[:, j * 128:(j + 1) * 128], vT[:, j, hc], True, True) for j in range(2)], fb, tsc)
            Z, W1, UV = N2[:, 0:128], L2[:, 0:128], L2[:, 128:256]
            tz_ = P.act(lambda e, b=b: e.activation(Z, b[:, 0:128], AF.Copy), tk, tpq)
            done(i, tz_)
            yield
            tP = addto(Pm, mul2((Qm,), (N16,), a1, n=1))
            yield
            i, b, fb = bank()
            tk = P.pe([mm(b[:, j * 64:(j + 1) * 64], Pm[:, j * 128:(j + 1) * 128], aT[:, j, hc], True, True) for j in range(2)]
                      + [mm(b[:, 128 + j * 64:128 + (j + 1) * 64], Pm[:, j * 128:(j + 1) * 128], Z[:, j * 64:(j + 1) * 64], True, True) for j in range(2)], fb, tz_, tP)
            tw = P.act(lambda e, b=b: e.activation(L2, b[:, 0:256], AF.Copy), tk)
            done(i, tw)
            yield
            i, b, fb = bank()
            tk = P.pe([mm(b[hs, j * 128:(j + 1) * 128], W1[:, j * 64:(j + 1) * 64], RbT[:, j * 128:(j + 1) * 128], True, True) for j in range(2)], fb, tw, tsc)
            tq = P.dve(lambda e, b=b: e.tensor_tensor(QT[hs, pt, 256 * hf:256 * hf + 256], b[hs, 0:256], rR[hs, :], A.add), tk, fr)
            done(i, tq)
            i, b, fb = bank()
            tk = P.pe([f for j in range(2) for f in (mm(b[:, j * 64:(j + 1) * 64], RbT[:, j * 128:(j + 1) * 128], UV[:, j * 64:(j + 1) * 64], True, False),
                                                     mm(b[:, j * 64:(j + 1) * 64], RkT[:, j * 128:(j + 1) * 128], vT[:, j, hc], False, True))], fb)
            ty = P.act(lambda e, b=b: e.activation(Y0[:, tl0:tl0 + 2, h * 64:(h + 1) * 64], b[:, 0:128].rearrange("p (t n) -> p t n", t=2), AF.Copy), tk, fr)
            done(i, ty)
            yield
            for ev in range(2):
                i, b, fb = bank()
                ps_ = slice(ev * 64, ev * 64 + 64)
                fs = []
                for tt in range(2):
                    o_, o2 = slice(tt * 64, tt * 64 + 64), slice(128 + tt * 64, 192 + tt * 64)
                    fs += [mm(b[hs, o_], W1[ps_, tt * 64:(tt + 1) * 64], bT[ps_, tt, hc], True, True),
                           mm(b[hs, o2], bT[ps_, tt, hc], UV[ps_, tt * 64:(tt + 1) * 64], True, False),
                           mm(b[hs, o2], kT[ps_, tt, hc], vT[ps_, tt, hc], False, True)]
                tk = P.pe(fs, fb)
                d = GH5[hs, :, pt, tl0:tl0 + 2, ev, :]
                s_ = b[hs, 0:256].rearrange("p (g t n) -> p g t n", g=2, n=64)
                if ev:
                    tg = P.act(lambda e, d=d, s_=s_: e.activation(d, s_, AF.Copy), tk, fr)
                else:
                    tg = P.dve(lambda e, d=d, s_=s_: e.tensor_copy(d, s_), tk, fr)
                done(i, tg)
            fam[0] = P.now("pe", "act", "dve")
            yield

        GH5 = GH.rearrange("p (g a t c n) -> p g a t c n", g=2, a=4, c=2, n=64)
        rkv_load(0)
        rkv_load(1)
        dsa_end = {}
        if dbg.get("cut") == 1:
            P.weave(half(0), half(1), tail(halves, QT, Y0, GTm, Hm, BV, GT, tmp, eref, eend))
            return
        P.weave(half(0), half(1), tail(halves, QT, Y0, GTm, Hm, BV, GT, tmp, eref, eend),
                dsa(dsa_end, xtt, KI, WI, w_in, P.now(), [xs]))
        gate2(w_in, xtt, keep["ya"], dsa_end)

    def tail(halves, QT, Y0, GTm, Hm, BV, GT, tmp, eref, eend):
        while len(halves) < 2:
            yield
        fam_free = list(halves.values())
        P.dve(lambda e: e.tensor_tensor(eend[:, :, 0:7], eend[:, :, 0:7], eref[:, :, 1:8], A.mult), fam_free)
        MB = [tmp[i] for i in range(8)]
        M4 = [m[:, 0:256].rearrange("p (a n) -> p a n", a=4) for m in MB]
        H5 = Hm.rearrange("p a (c n) -> p a c n", c=8)
        tm = None
        for c in range(7):
            dst = M4[c + 1]
            ec = eend[:, :, c:c + 1].to_broadcast([128, 4, 64])
            if c == 0:
                P.dve(lambda e, dst=dst: e.tensor_copy(dst, H5[:, :, 0, :]), fam_free)
            else:
                i, b, fb = bank()
                i2, b2, fb2 = bank()
                fs = []
                for pt in range(4):
                    for hs, bb in ((slice(0, 64), b), (slice(64, 128), b2)):
                        fs.append(mm(bb[hs, pt * 64:(pt + 1) * 64], GTm[hs, pt, c * 64:(c + 1) * 64], M4[c][hs, pt, :], True, True))
                tk = P.pe(fs, fb, fb2, tm, fam_free)
                P.dve(lambda e, dst=dst, c=c: e.tensor_tensor(dst, M4[c], H5[:, :, c, :], A.add))
                P.dve(lambda e, dst=dst, b=b: e.tensor_tensor(dst[0:64], dst[0:64], b[0:64, 0:256].rearrange("p (a n) -> p a n", a=4), A.add), tk)
                t2 = P.dve(lambda e, dst=dst, b2=b2: e.tensor_tensor(dst[64:128], dst[64:128], b2[64:128, 0:256].rearrange("p (a n) -> p a n", a=4), A.add), tk)
                done(i, t2)
                done(i2, t2)
            tm = P.dve(lambda e, dst=dst, ec=ec: e.tensor_tensor(dst, dst, ec, A.mult))
            yield
        for c in range(1, 8):
            tt, pp = c // 2, (c % 2) * 64
            for ev in range(2):
                hs = slice(ev * 64, ev * 64 + 64)
                i, b, fb = bank()
                tk = P.pe([mm(b[pp:pp + 64, pt * 64:(pt + 1) * 64], QT[hs, pt, c * 64:(c + 1) * 64], M4[c][hs, pt, :], True, True) for pt in range(4)], fb, tm)
                yield
                yh = Y0[pp:pp + 64, tt, :].rearrange("p (a e n) -> p a e n", e=2, n=64)[:, :, ev, :]
                ty = P.dve(lambda e, b=b, yh=yh, pp=pp: e.tensor_tensor(yh, yh, b[pp:pp + 64, 0:256].rearrange("p (a n) -> p a n", n=64), A.add), tk)
                done(i, ty)
        yield
        yv = Y0.rearrange("p t (h n) -> p (t h) n", n=64)
        junk = SC[:, NSC - 1, :]
        jv = junk.rearrange("p (a n) -> p a n", n=64)
        mean, var = st(32), st(32)
        P.dve(lambda e: e.tensor_reduce(mean, yv, AX, A.add))
        P.dve(lambda e: e.tensor_scalar(mean, mean, 1.0 / 64, None, A.mult))
        t1 = P.dve(lambda e: e.tensor_tensor(yv, yv, mean.unsqueeze(2).to_broadcast([128, 32, 64]), A.subtract))
        yield
        t1 = P.act(lambda e: e.activation(jv, yv, AF.Square), t1)
        t1 = P.dve(lambda e: e.tensor_reduce(var, jv, AX, A.add), t1)
        yield
        rs2, t1 = rsq(var, 32, 1.0 / 64, 64e-5, t1)
        t1 = P.dve(lambda e: e.tensor_tensor(yv, yv, rs2.unsqueeze(2).to_broadcast([128, 32, 64]), A.mult))
        YA = QT
        for j in range(4):
            i, b, fb = bank()
            tk = P.pe([tr(b[:, n * 128:(n + 1) * 128], Y0[:, n, j * 128:(j + 1) * 128], ident[:, :]) for n in range(NT)], t1, fb)
            t2 = P.dve(lambda e, b=b, j=j: e.tensor_scalar(YA[:, j, :], b[:, :], pcol("rw_ln_w_2", j), pcol("rw_ln_b_2", j), A.mult, A.add), tk)
            done(i, t2)
            P.dve(lambda e, j=j: e.tensor_tensor(YA[:, j, :], YA[:, j, :], BV[:, j, :], A.add))
            tya = P.dve(lambda e, j=j: e.tensor_tensor(YA[:, j, :], YA[:, j, :], GT[:, j, :], A.mult))
            yield
        keep["ya"] = tya

    def dsa(end, xtt, KI, WI, w_in, fr, xs):
        XX = X[:, :, :].rearrange("p t n -> p (t n)")
        R2, R3 = RING[:, 2, :], RING[:, 3, :]
        qF = XX[:, 0:2048].rearrange("p (a n) -> p a n", a=4)
        YB = qF
        ct, cT = XX[:, 2048:2560].rearrange("p (t n) -> p t n", t=4), XX[:, 2560:3072]
        QI = XX[:, 3072:4096].rearrange("p (a n) -> p a n", a=2)
        wuk, wuv = R3[:, 3072:3584], R3[:, 3584:4096]
        wq, wd = R2.rearrange("p (k n) -> p k n", k=8), R3[:, 0:3072].rearrange("p (k n) -> p k n", k=8)
        tw = P.dma("act", lambda e: e.dma_start(wuk, t["w_uk_2"].rearrange("l r h n -> (l r) (h n)")), "dsw", fr)
        tw = P.dma("act", lambda e: e.dma_start(wuv, t["w_uv_2"].rearrange("l r h n -> (l r) (h n)")), "dsw", fr)
        wi_ = w_in.rearrange("(k p) n -> p k n", p=128)
        td_ = P.dma("sp", lambda e: e.dma_start(wd, wi_[:, :, 2304:2688]), "dsd", fr)
        tq_ = P.dma("sp", lambda e: e.dma_start(wq, wi_[:, :, 1792:2304]), "dsq", fr)
        U2 = [R2[:, 512 * n:512 * n + 512] for n in range(8)]
        acc, work, eq, cum, junk, wukT_, rel0, rel1 = U2
        wukT = wukT_.rearrange("p (a n) -> p a n", a=4)
        rel = [rel0, rel1]
        BM = R3[:, 0:2048].rearrange("p (a n) -> p a n", a=4)
        ql = [R3[:, 2048:2560], R3[:, 2560:3072]]
        pb = [acc, work, eq]
        pT = [cum, junk]
        oT = [rel0, rel1]
        yield
        for j in range(2):
            i, b, tk = proj_f(wd, 128 + 128 * j, 128, XT, 8, td_, xtt)
            t1 = evac(QI[:, j, :], b[:, :], tk, xs)
            done(i, t1)
            yield
        ss = st(NT)
        for tt in range(NT):
            i, b, tk = proj_t(wd, 0, 128, XT, tt, 8, td_, xtt)
            tc = P.act(lambda e, b=b, tt=tt: e.activation(ct[:, tt, :], b[:, 0:128], AF.Copy), tk, xs)
            done(i, tc)
            tc = P.act(lambda e, tt=tt: e.activation(cT[:, 0:128], ct[:, tt, :], AF.Square, accum_out=ss[:, tt:tt + 1]))
            yield
        for j in range(4):
            i, b, tk = proj_f(wq, 128 * j, 128, XT, 8, tq_, xtt)
            t1 = evac(qF[:, j, :], b[:, :], tk, xs)
            done(i, t1)
            yield
        fr = P.now("pe")
        i, b, fb = bank()
        tk = P.pe([tr(b[:, j * 128:(j + 1) * 128], wuk[:, j * 128:(j + 1) * 128], ident[:, :]) for j in range(4)], tw, fb)
        t1 = evac(wukT.rearrange("p a n -> p (a n)"), b[:, :], tk, fr)
        done(i, t1)
        rs, rt = rsq(ss, NT, 1.0 / 128, 1e-6, tc)
        for tt in range(NT):
            tc = P.dve(lambda e, tt=tt: e.tensor_scalar(ct[:, tt, :], ct[:, tt, :], rs[:, tt:tt + 1], None, A.mult), rt)
        i, b, fb = bank()
        tk = P.pe([tr(b[:, j * 128:(j + 1) * 128], ct[:, j, :], ident[:, :]) for j in range(4)], tc, fb)
        tcT = evac(cT, b[:, :], tk, fr, scale=pcol("kv_norm_2"))
        done(i, tcT)
        ready = P.now("act", "dve")
        relf = [fr] * 2
        n = 0
        tbm = {0: None}
        for qt in range(1, NT):
            nk = 128 * (qt + 1)
            for h in range(4):
                s = n % 2
                n += 1
                hs = slice((h % 2) * 64, (h % 2) * 64 + 64)
                i, b, fb = bank()
                tk = P.pe([mm(b[:, 0:nk], QI[hs, h // 2, qt * 128:(qt + 1) * 128], KI[hs, 0:nk], True, True)], ready, fb)
                ta = P.act(lambda e, b=b, s=s, nk=nk: e.activation(rel[s][:, 0:nk], b[:, 0:nk], AF.Relu), tk, relf[s])
                done(i, ta)
                if h == 0:
                    tv = P.dve(lambda e, s=s, nk=nk, w=WI[:, qt, 0:1]: e.tensor_scalar(acc[:, 0:nk], rel[s][:, 0:nk], w, None, A.mult), ta, fr)
                else:
                    tv = P.dve(lambda e, s=s, nk=nk, w=WI[:, qt, h:h + 1]: e.scalar_tensor_tensor(acc[:, 0:nk], rel[s][:, 0:nk], w, acc[:, 0:nk], A.mult, A.add), ta)
                relf[s] = tv
                yield
            av, wv_, ev, cv = acc[:, 0:nk], work[:, 0:nk], eq[:, 0:nk], cum[:, 0:nk]
            P.dve(lambda e, nk=nk: e.tensor_tensor(acc[:, nk - 128:nk], acc[:, nk - 128:nk], diagm[:, :], A.add))
            yield
            m8 = st(8)
            for r_ in range(16):
                src = av if r_ == 0 else wv_
                P.dve(lambda e, src=src, m8=m8: e.max(m8, src))
                if r_ < 15:
                    P.dve(lambda e, src=src, m8=m8, wv_=wv_: e.match_replace(wv_, m8, src, -3.0e38))
                yield
            thr = m8[:, 7:8]
            need = st(1)
            P.dve(lambda e, a=av, o=wv_, thr=thr: e.tensor_scalar(o, a, thr, None, A.is_gt))
            yield
            P.dve(lambda e, o=wv_, need=need: e.tensor_reduce(need, o, AX, A.add))
            P.dve(lambda e, need=need: e.tensor_scalar(need, need, -1.0, 128.0, A.mult, A.add))
            P.dve(lambda e, a=av, o=ev, thr=thr: e.tensor_scalar(o, a, thr, None, A.is_equal))
            yield
            P.dve(lambda e, a=ev, o=cv: e.tensor_tensor_scan(o, a, a, 0.0, A.add, A.max))
            P.dve(lambda e, a=cv, o=ev, need=need: e.scalar_tensor_tensor(o, a, need, o, A.is_le, A.mult))
            yield
            P.dve(lambda e, a=wv_, o=ev: e.tensor_tensor(o, a, o, A.add))
            tbm[qt] = P.dve(lambda e, a=ev, o=BM[:, qt, 0:nk]: e.tensor_scalar(o, a, 1.0, -NEG, A.subtract, A.mult), fr)
        fr = P.now()
        qlf, pbf, pTf, oTf = [fr] * 2, [fr] * 3, [fr] * 2, [fr] * 2
        n = 0
        for h in range(8):
            pt, q0 = h // 2, (h % 2) * 64
            hs = slice(q0, q0 + 64)
            s2 = h % 2
            i, b, fb = bank()
            tk = P.pe([mm(b[:, :], wukT[hs, pt, :], qF[hs, pt, :], True, True)], ready, fb)
            tql = evac(ql[s2], b[:, :], tk, qlf[s2])
            done(i, tql)
            io, bo, fo = bank()
            for qt in range(NT):
                nk = 128 * (qt + 1)
                s = n % 3
                sp = n % 2
                n += 1
                stt = st(3)
                p_ = pb[s][:, 0:nk]
                i, b, fb = bank()
                tk = P.pe([mm(b[:, 0:nk], ql[s2][:, qt * 128:(qt + 1) * 128], cT[:, 0:nk], True, True)], tql, tcT, fb)
                bias = diagm[:, :] if qt == 0 else BM[:, qt, 0:nk]
                t1 = P.dve(lambda e, p_=p_, b=b, nk=nk, bias=bias, m=stt[:, 0:1]: e.tensor_tensor_reduce(p_, b[:, 0:nk], bias, 1.0, -3.0e38, A.add, A.max, m), tk, pbf[s])
                done(i, t1)
                t1 = P.dve(lambda e, m=stt[:, 0:1]: e.tensor_scalar(m, m, -0.125, None, A.mult))
                yield
                t2 = P.act(lambda e, p_=p_, m=stt: e.activation(p_, p_, AF.Exp, bias=m[:, 0:1], scale=0.125, accum_out=m[:, 1:2]), t1)
                P.dve(lambda e, m=stt: e.reciprocal(m[:, 2:3], m[:, 1:2]), t2)
                t3 = P.dve(lambda e, p_=p_, m=stt: e.tensor_scalar(p_, p_, m[:, 2:3], None, A.mult))
                yield
                i, b, fb = bank()
                tk = P.pe([tr(b[:, j * 128:(j + 1) * 128], p_[:, j * 128:(j + 1) * 128], ident[:, :]) for j in range(qt + 1)], t3, fb)
                pbf[s] = tk
                t4 = P.act(lambda e, b=b, nk=nk, d=pT[sp][:, 0:nk]: e.activation(d, b[:, 0:nk], AF.Copy), tk, pTf[sp])
                done(i, t4)
                tk = P.pe([mm(bo[:, qt * 128:(qt + 1) * 128], ct[:, j, :], pT[sp][:, j * 128:(j + 1) * 128], j == 0, j == qt) for j in range(qt + 1)], t4, fo)
                pTf[sp] = tk
                yield
            qlf[s2] = tk
            t5 = P.act(lambda e, bo=bo, s2=s2: e.activation(oT[s2], bo[:, :], AF.Identity, scale=pcol("kv_norm_2")), tk, oTf[s2])
            done(io, t5)
            i, b, fb = bank()
            tk = P.pe([mm(b[hs, :], wuv[:, h * 64:(h + 1) * 64], oT[s2], True, True)], t5, fb, tw)
            oTf[s2] = tk
            t6 = P.act(lambda e, b=b, hs=hs, pt=pt: e.activation(YB[hs, pt, :], b[hs, :], AF.Copy), tk, fr)
            done(i, t6)
            yield
        end["t"] = P.now()
        end["yb"] = qF

    def gate2(w_in, xtt, tya, end):
        fr = P.now()
        YA, YB = scv(0, 4), scv(10, 4)
        for i in range(NRING):
            ring_free[i] = list(fr)
        for j in range(4):
            tyb = P.act(lambda e, j=j: e.activation(YB[:, j, :], end["yb"][:, j, :], AF.Copy), fr)
        nbg = st(16)
        tn = P.dve(lambda e: e.tensor_scalar(nbg, pcols("b_gate_2", 16), -1.0, None, A.mult))
        tx = P.dma("act", lambda e: e.dma_start(X[:, :, :], xkeep.rearrange("(t p) n -> p t n", p=128)), "xl", fr, tyb)
        E4, Y4 = scv(4, 4), scv(5, 4)
        tx = gated(w_in, 2756, t["w_proj_a_2"][0], YA, tya, t["w_proj_b_2"][0], YB, [tyb], nbg,
                   t["w_out_2"][0], xtt, scv(2, 8, 2), ([E4[:, 0, :], E4[:, 1, :]], [Y4[:, 0, :], Y4[:, 1, :]]), [fr, tn], tx)
        keep['x'] = tx
        if dbg.get('cut') != 2:
            cross(tx)

    def cross(tx):
        fr = P.now()
        MEM, MN, MT = scv(0, 2), scv(1, 2), scv(2, 8)
        qF, kT, V = scv(3, 8, 2), scv(5, 8), scv(6, 2)
        pb = [SC[:, 7, 256 * i:256 * (i + 1)] for i in range(4)]
        PT = [SC[:, 8, 1024 * i:1024 * (i + 1)].rearrange("p (a n) -> p a n", a=2) for i in range(2)]
        oT = scv(9, 8, 2)
        tm = P.dma("act", lambda e: e.dma_start(MEM, t["mem_2"][0].rearrange("(t p) n -> p t n", p=128)), "mem", fr)
        rm, rmt = rms(MEM, 2, D, tm)
        tmt = to_xt(MEM, 2, rm, rmt, pcols("norm_mem_2", 8), MT, MN, fr)
        rs, rt = rms(X, NT, D, tx)
        xtt = to_xt(X, NT, rs, rt, pcols("norm_cross_2", 8), XT, scv(9, 4, 2), fr)
        for half in range(2):
            u_, s_, ut = wcols(t["w_ckv_2"][0], half * 512, 512)
            wv = s_.rearrange("p (k n) -> p k n", k=8)
            for j in range(4):
                i, b, tk = proj_f(wv, j * 128, 128, MT, 8, ut, tmt)
                t1 = evac(kT[:, half * 4 + j, :], b[:, 0:256], tk, fr)
                done(i, t1)
            unit_done(u_, tk)
        for half in range(2):
            u_, s_, ut = wcols(t["w_ckv_2"][0], 1024 + half * 512, 512)
            wv = s_.rearrange("p (k n) -> p k n", k=8)
            for j in range(2):
                i, b, tk = proj_t(wv, 0, 512, MT, j, 8, ut, tmt)
                t1 = evac(V[:, j, half * 512:(half + 1) * 512], b[:, :], tk, fr)
                done(i, t1)
            unit_done(u_, tk)
        for half in range(2):
            u_, s_, ut = wcols(t["w_cq_2"][0], half * 512, 512)
            wv = s_.rearrange("p (k n) -> p k n", k=8)
            for j in range(4):
                i, b, tk = proj_f(wv, j * 128, 128, XT, 8, ut, xtt)
                t1 = evac(qF[:, half * 4 + j, :], b[:, :], tk, fr)
                done(i, t1)
            unit_done(u_, tk)
        ready = P.now("act", "dve", "pe")
        pbf, PTf = [fr] * 4, [fr] * 2
        n = 0
        for h in range(4):
            s2 = h % 2
            for qt in range(NT):
                s = n % 4
                n += 1
                stt = st(3)
                i, b, fb = bank()
                tk = P.pe([mm(b[:, 0:256], qF[:, 2 * h + c, qt * 128:(qt + 1) * 128], kT[:, 2 * h + c, :], c == 0, c == 1) for c in range(2)], ready, fb)
                P.dve(lambda e, b=b, m=stt[:, 0:1]: e.tensor_reduce(m, b[:, 0:256], AX, A.max), tk)
                t1 = P.dve(lambda e, m=stt[:, 0:1]: e.tensor_scalar(m, m, -0.0625, None, A.mult))
                t2 = P.act(lambda e, p_=pb[s], b=b, m=stt: e.activation(p_, b[:, 0:256], AF.Exp, bias=m[:, 0:1], scale=0.0625, accum_out=m[:, 1:2]), t1, pbf[s])
                done(i, t2)
                P.dve(lambda e, m=stt: e.reciprocal(m[:, 2:3], m[:, 1:2]), t2)
                t3 = P.dve(lambda e, p_=pb[s], m=stt: e.tensor_scalar(p_, p_, m[:, 2:3], None, A.mult))
                i, b, fb = bank()
                tk = P.pe([tr(b[:, j * 128:(j + 1) * 128], pb[s][:, j * 128:(j + 1) * 128], ident[:, :]) for j in range(2)], t3, fb)
                pbf[s] = tk
                tp = P.act(lambda e, b=b, d=PT[s2][:, :, qt * 128:(qt + 1) * 128]: e.activation(d, b[:, 0:256].rearrange("p (a n) -> p a n", a=2), AF.Copy), tk, PTf[s2])
                done(i, tp)
            for c in range(2):
                i, b, fb = bank()
                tk = P.pe([mm(b[:, :], V[:, m, h * 256 + c * 128:h * 256 + (c + 1) * 128], PT[s2][:, m, :], m == 0, m == 1) for m in range(2)], tp, fb)
                to = evac(oT[:, 2 * h + c, :], b[:, :], tk, ready)
                done(i, to)
            PTf[s2] = tk
        keep["x"] = [add_proj(t["w_co_2"][0], oT, P.now("act", "dve"))]

    def finish():
        stn[0] = 0
        fr = P.now()
        gr = scv(0, 2)[:, 0, :]
        Y = scv(1, 4, 2)
        tg = P.dma("act", lambda e: e.dma_start(gr, t["norm_final_2"].rearrange("(a n) -> a n", a=1).to_broadcast([128, D])), "fg", fr)
        rs, rt = rms(X, NT, D, fr)
        for i in range(NT):
            t1 = P.dve(lambda e, i=i: e.scalar_tensor_tensor(Y[:, i, :], X[:, i, :], rs[:, i:i + 1], gr, A.mult, A.mult), rt, tg)
            P.dma("sp", lambda e, i=i: e.dma_start(out[0, i * 128:(i + 1) * 128, :], Y[:, i, :]), "out", t1)


    keep = {}
    ST_KEEP = 0
    phases = [block1_mix, lambda: moe(0), block2_mix, lambda: moe(1), finish]
    for n, ph in enumerate(phases):
        if dbg.get("start", 0) <= n < dbg.get("stop", 9):
            ph()
    for f in dbg.get("dumps", []):
        P.dma("act", (lambda f: lambda e: f(e, X, SC, XT))(f), "dump", P.now())
    block = ctx.enter_context(nc.Block())
    for nm, deco in (("sp", block.sync), ("act", block.scalar), ("dve", block.vector), ("pool", block.gpsimd), ("pe", block.tensor)):
        @deco
        def _(e, nm=nm):
            P.emit(nm, e)
            if nm == "act" and "dump" in P.sems:
                e.wait_ge(P.sems["dump"], P.n["dump"])
            if nm == "sp" and "out" in P.sems:
                e.wait_ge(P.sems["out"], P.n["out"])


_INS = ["x", "norm_mix", "w_in", "hg_lb", "hg_out_norm", "da_q_norm", "da_k_norm", "da_lambda", "da_out_norm",
        "w_branch_hg", "w_branch_da", "w_out", "norm_moe", "w_router_group", "b_router_group", "w_router_expert",
        "b_router_expert", "w1", "w3", "w2", "mem_2", "norm_mix_2", "w_in_2", "shift_mu_2", "rw_w0_2", "rw_w2_2",
        "rw_a0_2", "rw_a2_2", "rw_g2_2", "rw_k_k_2", "rw_k_a_2", "rw_r_k_2", "rw_ln_w_2", "rw_ln_b_2", "kv_norm_2",
        "w_uk_2", "w_uv_2", "w_proj_a_2", "w_proj_b_2", "b_gate_2", "w_out_2", "norm_cross_2", "norm_mem_2", "w_cq_2",
        "w_ckv_2", "w_co_2", "norm_ffn_2", "w_router_g_2", "b_router_g_2", "w_router_e_2", "b_router_e_2",
        "w_e_gate_2", "w_e_up_2", "w_e_down_2", "norm_final_2"]


def rope_tables():
    half = 32
    inv = np.float32(10000.0) ** (-np.arange(half, dtype=np.float32) / np.float32(half))
    ang = np.arange(T, dtype=np.float32)[:, None] * inv.astype(np.float32)[None, :]
    return np.cos(ang).astype(np.float32), np.sin(ang).astype(np.float32)


def kernel(**inputs):
    import concourse.bacc as _bacc
    from concourse.bass_utils import run_bass_kernel_spmd as _run

    nc = _bacc.Bacc("TRN2", target_bir_lowering=False, num_devices=1, dynamic_dma_scratch_size=8192)
    arrays, t = {}, {}
    cos, sin = rope_tables()
    for name, a in [(n, np.ascontiguousarray(inputs[n])) for n in _INS] + [("rope_cos", cos), ("rope_sin", sin)]:
        arrays[f"in_{name}"] = a
        t[name] = nc.dram_tensor(f"in_{name}", a.shape, F, kind="ExternalInput").ap()
    out = nc.dram_tensor("out_0", (1, T, D), F, kind="ExternalOutput").ap()
    program(nc, t, out, {})
    r = _run(nc, [arrays], core_ids=[0])
    return r.results[0]["out_0"]
```

```python
import math
from contextlib import ExitStack

import numpy as np
import concourse.bass as bass
from concourse import mybir

F = mybir.dt.float32
I32 = mybir.dt.int32
U32 = mybir.dt.uint32
A = mybir.AluOpType
AF = mybir.ActivationFunctionType
AX = mybir.AxisListType.X
ENG = ("sp", "act", "dve", "pool", "pe")

T = 512
NT = 4
D = 1024
NEG = -1.0e30
CAP = 64
NE = 32
NOV = 16
NRING = 4
NSC = 12
S1, S2 = 1.0, 1.5
SLOW1, SLOW2 = 1.0, 1.6
LAG = 500
LAM_INIT = 0.8 - 0.6 * math.exp(0.0)


class Prog:

    def __init__(self, nc, ctx, tag):
        self.nc = nc
        self.q = {e: [] for e in ENG}
        self.sem = {e: ctx.enter_context(nc.semaphore(f"{tag}_{e}")) for e in ENG if e != "sp"}
        self.sems = dict(self.sem)
        self.n = {}
        self.tag = tag
        self.ctx = ctx
        self.fin = {}
        self.clk = {}
        self.end = 0
        self.marks = None

    def flat(self, deps, out):
        for d in deps:
            if d is None:
                continue
            if isinstance(d, list):
                self.flat(d, out)
            else:
                out.append(d)
        return out

    def count(self, name, by):
        self.n[name] = self.n.get(name, 0) + by
        if self.marks is not None and name in ENG:
            self.marks[name] = self.n[name]
        return (name, self.n[name])

    def now(self, *engs):
        n = self.n if self.marks is None else self.marks
        return [(e, n[e]) for e in (engs or ("act", "dve", "pool", "pe")) if n.get(e)]

    def guess(self, eng, tok, deps, ns):
        t = max([self.clk.get(eng, 0)] + [self.fin.get(d, 0) for d in deps]) + ns
        self.clk[eng] = t
        self.fin[tok] = t + LAG
        self.end = max(self.end, t + LAG)

    def weave(self, *gens):
        base = dict(self.n)
        t0 = max(self.clk.values())
        live = []
        for n, g in enumerate(gens):
            g, slow = g if isinstance(g, tuple) else (g, 1.0)
            live.append([t0, n, g, dict(base), slow])
        while live:
            s = min(live, key=lambda s: (s[0], s[1]))
            self.marks = s[3]
            self.end = 0
            try:
                next(s[2])
            except StopIteration:
                live.remove(s)
                continue
            if self.end:
                s[0] += max(1, self.end - s[0]) * s[4]
            else:
                s[0] = min([o[0] for o in live if o is not s] or [s[0]]) + 1
        self.marks = None

    def op(self, eng, fn, *deps, ns=400):
        deps = self.flat(deps, [])
        if eng != "pe" and self.n.get(eng):
            deps.append((eng, self.n[eng]))
        tok = self.count(eng, 1)
        self.guess(eng, tok, deps, ns)
        self.q[eng].append((deps, fn, eng, 1))
        return tok

    def dve(self, fn, *deps, ns=400):
        return self.op("dve", fn, *deps, ns=ns)

    def act(self, fn, *deps, ns=400):
        return self.op("act", fn, *deps, ns=ns)

    def pool(self, fn, *deps, ns=400):
        return self.op("pool", fn, *deps, ns=ns)

    def pe(self, fns, *deps):
        def run(e):
            for f in fns:
                last = f(e)
            return last
        return self.op("pe", run, *deps, ns=sum(f.ns for f in fns))

    def dma(self, eng, fn, sem, *deps):
        if sem not in self.sems:
            self.sems[sem] = self.ctx.enter_context(self.nc.semaphore(f"{self.tag}_{sem}"))
        tok = self.count(sem, 16)
        self.fin[tok] = max([self.fin.get(d, 0) for d in self.flat(deps, [])] + [self.clk.get("pe", 0)]) + 4000
        self.q[eng].append((self.flat(deps, []), fn, sem, 16))
        return tok

    def raw(self, eng, fn, *deps):
        self.q[eng].append((self.flat(deps, []), fn, None, 0))

    def emit(self, eng, e, start=0, end=None, seen=None):
        seen = {} if seen is None else seen
        for deps, fn, sem, by in self.q[eng][start:end]:
            for name, val in deps:
                if seen.get(name, 0) < val:
                    e.wait_ge(self.sems[name], val)
                    seen[name] = val
            ins = fn(e)
            if sem is not None:
                ins.then_inc(self.sems[sem], by)


def mm(out, l, r, st, sp):
    def f(e):
        return e.matmul(out, l, r, start=st, stop=sp, skip_group_check=True)
    n = math.prod(out.shape[1:])
    f.ns = 215 if n <= 64 else max(430, 1.7 * n)
    return f


def tr(out, in_, ident):
    def f(e):
        return e.transpose(out, in_, ident)
    n = math.prod(out.shape[1:])
    f.ns = 215 if n <= 64 else max(430, 1.7 * n)
    return f


PARAMS = [("norm_mix", 8), ("hg_lb", 8), ("hg_out_norm", 1), ("da_out_norm", 1), ("norm_mix_2", 8),
          ("shift_mu_2", 14), ("rw_w0_2", 4), ("rw_a0_2", 4), ("rw_k_k_2", 4), ("rw_k_a_2", 4),
          ("rw_r_k_2", 4), ("rw_ln_w_2", 4), ("rw_ln_b_2", 4), ("b_gate_2", 16),
          ("norm_cross_2", 8), ("norm_mem_2", 8), ("kv_norm_2", 1),
          ("norm_moe", 8), ("norm_ffn_2", 8)]


def program(nc, t, out):
    with ExitStack() as ctx:
        build(nc, ctx, t, out)


def build(nc, ctx, t, out):
    P = Prog(nc, ctx, "m")

    def sb(name, shape, dt=F):
        return ctx.enter_context(nc.sbuf_tensor(name, shape, dt))

    X = sb("X", [128, NT, D])
    XT = sb("XT", [128, 8, T])
    RING = sb("RING", [128, NRING, 4096])
    SC = sb("SC", [128, NSC, 2048])
    ST = sb("ST", [128, 1400])
    PR = SC[:, NSC - 1, 1024:1152]
    PC = sb("PC", [128, 128])
    ident = sb("ident", [128, 128])
    CH = sb("CH", [128, T])
    mk = sb("mk", [128, 4, 128], mybir.dt.int8)
    mband = sb("mband", [128, 6, 128], mybir.dt.int8)
    diagm = sb("diagm", [128, 128])
    PS = [ctx.enter_context(nc.psum_tensor(f"ps{i}", [128, 512], F)) for i in range(8)]
    ytab = nc.dram_tensor("ytab", [2 * T, D], F, kind="Internal").ap()
    xkeep = nc.dram_tensor("xkeep", [T, D], F, kind="Internal").ap()
    xrows = nc.dram_tensor("xrows", [T, D], F, kind="Internal").ap()

    stn = [0]

    def st(n):
        a = ST[:, stn[0]:stn[0] + n]
        stn[0] += n
        assert stn[0] <= 1400, stn
        return a

    bank_no = [0]
    bank_free = [[] for _ in range(8)]

    def bank():
        assert any(f is not None for f in bank_free)
        while bank_free[bank_no[0] % 8] is None:
            bank_no[0] += 1
        i = bank_no[0] % 8
        bank_no[0] += 1
        free = bank_free[i]
        bank_free[i] = None
        return i, PS[i], free

    def done(i, *toks):
        bank_free[i] = list(toks)

    ring_order = list(range(NRING))
    slots = [RING[:, i, :] for i in range(NRING)]
    ring_free = [[] for _ in range(NRING)]

    def unit(srcs):
        i = ring_order.pop(0)
        slot = slots[i]
        free = ring_free[i]
        assert free is not None
        ring_free[i] = None
        tok = None
        for dst, src in srcs:
            tok = P.dma("sp", (lambda d, s: lambda e: e.dma_start(d, s))(dst(slot), src), f"ring{i}", free)
        return i, slot, tok

    def unit_done(i, *toks):
        ring_free[i] = list(toks)
        ring_order.append(i)

    def wcols(w, c0, n):
        return unit([(lambda s: s[:, 0:8 * n].rearrange("p (k n) -> p k n", k=8),
                      w.rearrange("(k p) n -> p k n", p=128)[:, :, c0:c0 + n])])

    flip = [0]

    def evac(dst, src, *deps, scale=None):
        flip[0] += 1
        if flip[0] % 2:
            if scale is None:
                return P.act(lambda e: e.activation(dst, src, AF.Copy), *deps)
            return P.act(lambda e: e.activation(dst, src, AF.Identity, scale=scale), *deps)
        if scale is None:
            return P.dve(lambda e: e.tensor_copy(dst, src), *deps)
        return P.dve(lambda e: e.tensor_scalar(dst, src, scale, None, A.mult), *deps)

    def rsq(src, n, scale, eps, *deps):
        a, y, u = st(n), st(n), st(n)
        t0 = P.dve(lambda e: e.tensor_scalar(a, src, scale, eps, A.mult, A.add), *deps)
        t1 = P.act(lambda e: e.activation(y, a, AF.Ln), t0)
        t1 = P.act(lambda e: e.activation(y, y, AF.Exp, scale=-0.5), t1)
        P.dve(lambda e: e.scalar_tensor_tensor(u, y, -0.5, y, A.mult, A.mult), t1)
        P.dve(lambda e: e.tensor_tensor(u, u, a, A.mult))
        return y, P.dve(lambda e: e.scalar_tensor_tensor(y, u, 1.5, y, A.add, A.mult))

    ld = []
    for tt in range(NT):
        ld.append(P.dma("sp", (lambda tt: lambda e: e.dma_start(X[:, tt, :], t["x"][0, tt * 128:(tt + 1) * 128, :]))(tt), "x"))
    x_in = ld[-1]
    col = {}
    row = 0
    for name, n in PARAMS:
        v = t[name]
        if name == "rw_r_k_2":
            v = v.rearrange("l h n -> l (h n)")
        v = v.rearrange("l n -> (l n)") if len(v.shape) == 2 else v
        tok = P.dma("act", (lambda v, row, n: lambda e: e.dma_start(PR[row:row + n, :], v.rearrange("(a b) -> a b", b=128)))(v, row, n), "rows")
        col[name] = row
        row += n
    NPR = row
    rows = tok
    G64 = sb("G64", [128, 2, 64])
    LAMP = sb("LAMP", [128, 256])
    ROPE = sb("ROPE", [128, 2, NT, 32])
    RB = sb("RB", [128, 2, 36])
    WR = sb("WR", [128, 2, 8, 36])
    tok = P.dma("act", lambda e: e.dma_start(G64[:, 0, :], t["da_q_norm"].to_broadcast([128, 64])), "par")
    tok = P.dma("act", lambda e: e.dma_start(G64[:, 1, :], t["da_k_norm"].to_broadcast([128, 64])), "par")
    tok = P.dma("act", lambda e: e.dma_start(LAMP[:, :], t["da_lambda"].rearrange("l a b -> l (a b)").to_broadcast([128, 256])), "par")
    tok = P.dma("act", lambda e: e.dma_start(ROPE[:, 0, :, :], t["rope_cos"].rearrange("(t p) n -> p t n", p=128)), "par")
    tok = P.dma("act", lambda e: e.dma_start(ROPE[:, 1, :, :], t["rope_sin"].rearrange("(t p) n -> p t n", p=128)), "par")
    for b, (g, e_) in enumerate((("router_group", "router_expert"), ("router_g_2", "router_e_2"))):
        tok = P.dma("act", (lambda b, g: lambda e: e.dma_start(RB[:, b, 0:4], t["b_" + g].to_broadcast([128, 4])))(b, g), "par")
        tok = P.dma("act", (lambda b, g: lambda e: e.dma_start(RB[:, b, 4:36], t["b_" + g].to_broadcast([128, 32])))(b, e_), "par")
        tok = P.dma("act", (lambda b, g: lambda e: e.dma_start(WR[:, b, :, 0:4], t["w_" + g][0].rearrange("(k p) n -> p k n", p=128)))(b, g), "par")
        tok = P.dma("act", (lambda b, g: lambda e: e.dma_start(WR[:, b, :, 4:36], t["w_" + g][0].rearrange("(k p) n -> p k n", p=128)))(b, e_), "par")
    par = tok

    ones = sb("ones", [128, 128])
    upper = sb("upper", [128, 128])
    BO = sb("BO", [128, 128])
    iotf = sb("iotf", [128, 128])
    iotm = sb("iotm", [128, 8])
    fval = sb("fval", [128, 2, NT])
    tmpm = SC[:, NSC - 2, 0:1024]
    P.pool(lambda e: e.memset(ones[:, :], 1.0))

    def sel(dst, src, pattern, op, fill, base, cm):
        return P.pool(lambda e: e.affine_select(out=dst, in_=src, pattern=pattern, compare_op=op, fill=fill, base=base, channel_multiplier=cm))

    P.pool(lambda e: e.memset(ident[:, :], 0.0))
    sel(ident[:, :], ident[:, :], [[-1, 128]], A.not_equal, 1.0, 0, 1)
    sel(upper[:, :], ones[:, :], [[1, 128]], A.is_gt, 0.0, 0, -1)
    P.pool(lambda e: e.memset(diagm[:, :], 0.0))
    sel(diagm[:, :], diagm[:, :], [[-1, 128]], A.is_ge, NEG, 0, 1)
    P.pool(lambda e: e.memset(BO[:, :], 0.0))
    P.pool(lambda e: e.memset(BO[0:64, 0:64], 1.0))
    P.pool(lambda e: e.memset(BO[64:128, 64:128], 1.0))
    P.pool(lambda e: e.memset(CH[:, :], 1.0))
    P.pool(lambda e: e.memset(CH[:, :].rearrange("p (c j) -> p c j", j=64)[:, :, 0], 0.0))
    P.pool(lambda e: e.iota(iotf[:, :], [[1, 128]], base=0, channel_multiplier=0, allow_small_or_imprecise_dtypes=True))
    P.pool(lambda e: e.iota(iotm[:, :], [[1, 8]], base=-8, channel_multiplier=0, allow_small_or_imprecise_dtypes=True))
    for k in range(2):
        P.pool((lambda k: lambda e: e.iota(fval[:, k, :], [[256, NT]], base=k - 4 * T, channel_multiplier=2, allow_small_or_imprecise_dtypes=True))(k))
    m0, m1, m16, m32 = (tmpm[:, 128 * i:128 * (i + 1)] for i in range(4))
    BOv = BO[:, :]

    def blocks(dst, size):
        v = dst.rearrange("p (a b) -> p a b", b=size)
        sel(v, ones[:, :].rearrange("p (a b) -> p a b", b=size), [[-size, 128 // size], [0, size]], A.is_ge, 0.0, 0, 1)
        sel(v, v, [[size, 128 // size], [0, size]], A.is_ge, 0.0, size - 1, -1)

    blocks(m16, 16)
    blocks(m32, 32)
    u = tmpm[:, 512:640]
    w = tmpm[:, 640:768]
    lower = tmpm[:, 768:896]
    sel(lower, ones[:, :], [[-1, 128]], A.is_gt, 0.0, 0, 1)
    sel(m0, BOv, [[1, 128]], A.is_ge, 0.0, 0, -1)
    tk = P.pool(lambda e: e.tensor_copy(mk[:, 0, :], m0))

    def band(i, tri, hi, lo):
        P.pool(lambda e: e.tensor_tensor(u, tri, hi, A.mult))
        if lo is not None:
            P.pool(lambda e: e.tensor_tensor(w, u, lo, A.mult))
            P.pool(lambda e: e.tensor_tensor(u, u, w, A.subtract))
        return P.pool(lambda e: e.tensor_copy(mband[:, i, :], u))

    band(0, upper[:, :], m16, None)
    band(1, lower, m16, None)
    band(2, upper[:, :], m32, m16)
    band(3, lower, m32, m16)
    band(4, lower, BOv, m32)
    cst = band(5, upper[:, :], BOv, None)

    i, b, fr = bank()
    tk = P.pe([tr(b[:, 0:NPR], PR[0:NPR, :], ident[0:NPR, 0:NPR])], cst, rows)
    pc = P.dve(lambda e: e.tensor_copy(PC[:, 0:NPR], b[:, 0:NPR]), tk)
    done(i, pc)

    def pcol(name, j=0):
        c = col[name] + j
        return PC[:, c:c + 1]

    def pcols(name, n):
        return PC[:, col[name]:col[name] + n]

    def scv(i, a, n=1):
        v = SC[:, i:i + n, :].rearrange("p s b -> p (s b)")
        return v.rearrange("p (a b) -> p a b", a=a)

    def rms(src, nt, n, *deps):
        ss = st(nt)
        junk = SC[:, NSC - 1, 0:n]
        for i in range(nt):
            tk = P.act((lambda i: lambda e: e.activation(junk, src[:, i, :], AF.Square, accum_out=ss[:, i:i + 1]))(i), *deps)
        return rsq(ss, nt, 1.0 / n, 1e-6, tk)

    def to_xt(src, nt, rs, rtok, gain, dst, xn, free):
        tk = None
        for i in range(nt):
            tk = P.dve((lambda i: lambda e: e.tensor_scalar(xn[:, i, :], src[:, i, :], rs[:, i:i + 1], None, A.mult))(i), rtok, free)
        return transposed(xn, nt, gain, dst, tk, free)

    def transposed(xn, nt, gain, dst, tk, free):
        out_ = []
        for k in range(8):
            i, b, fr = bank()
            t1 = P.pe([tr(b[:, j * 128:(j + 1) * 128], xn[:, j, k * 128:(k + 1) * 128], ident[:, :]) for j in range(nt)], tk, fr, cst)
            t2 = evac(dst[:, k, :], b[:, 0:nt * 128], t1, free, pc, scale=None if gain is None else gain[:, k:k + 1])
            done(i, t2)
            out_.append(t2)
        return out_[-2:]

    def proj_f(wv, c, n, rhs, nk, *deps, at=0, bk=None):
        if bk is None:
            bk = bank()
        i, b, fr = bk
        N = rhs.shape[-1]
        tk = P.pe([mm(b[at:at + n, 0:N], wv[:, k, c:c + n], rhs[:, k, :], k == 0, k == nk - 1) for k in range(nk)], fr, *deps)
        return i, b, tk

    def proj_t(wv, c, n, lhs, tt, nk, *deps):
        i, b, fr = bank()
        tk = P.pe([mm(b[:, 0:n], lhs[:, k, tt * 128:(tt + 1) * 128], wv[:, k, c:c + n], k == 0, k == nk - 1) for k in range(nk)], fr, *deps)
        return i, b, tk

    def gated(wgate, gcol0, branches, bias, wout, xtt, mbuf, tmp, free, end):
        E, Y = tmp
        last = [free] * 2
        for n, (br, w_, get) in enumerate(branches):
            wu, ws, wt = unit([(lambda s: s.rearrange("p (k n) -> p k n", k=4), w_.rearrange("(k p) n -> p k n", p=128))])
            wv = ws.rearrange("p (k n) -> p k n", k=4)
            for half in range(2):
                gu, gs, gt = wcols(wgate, gcol0 + br * 1024 + half * 512, 512)
                gv = gs.rearrange("p (k n) -> p k n", k=8)
                for j in range(4):
                    dt_ = half * 4 + j
                    s_ = dt_ % 2
                    e_, y_ = E[s_], Y[s_]
                    i, b, tk = proj_f(gv, j * 128, 128, XT, 8, gt, xtt)
                    nb = None if bias is None else bias[:, br * 8 + dt_:br * 8 + dt_ + 1]
                    ta = P.act((lambda e_, b, nb: lambda e: e.activation(e_, b[:, :], AF.Exp, scale=-1.0, **({} if nb is None else {"bias": nb})))(e_, b, nb), tk, last[s_])
                    done(i, ta)
                    yield
                    while get() is None:
                        yield
                    y, yt = get()
                    P.dve((lambda e_: lambda e: e.tensor_scalar(e_, e_, 1.0, None, A.add))(e_), ta)
                    P.dve((lambda e_: lambda e: e.reciprocal(e_, e_))(e_))
                    i2, b2, tk2 = proj_f(wv, dt_ * 128, 128, y, 4, wt, yt)
                    dst = mbuf[:, dt_, :] if n == 0 else y_
                    tv = P.dve((lambda dst, e_, b2: lambda e: e.tensor_tensor(dst, e_, b2[:, :], A.mult))(dst, e_, b2), tk2, free)
                    done(i2, tv)
                    last[s_] = tv
                    if n == 1:
                        tv = last[s_] = P.dve((lambda m, y_: lambda e: e.tensor_tensor(m, m, y_, A.add))(mbuf[:, dt_, :], y_))
                    yield
                unit_done(gu, tk)
            unit_done(wu, tk2)
            end.append(tk2)
        yield from add_proj(wout, mbuf, [tv], end)

    def add_proj(wout, src, tv, end):
        for half in range(2):
            u_, s_, wt = wcols(wout, half * 512, 512)
            v = s_.rearrange("p (k n) -> p k n", k=8)
            for tt in range(NT):
                i, b, tk = proj_t(v, 0, 512, src, tt, 8, wt, tv)
                xs = X[:, tt, half * 512:(half + 1) * 512]
                tx = P.dve((lambda xs, b: lambda e: e.tensor_tensor(xs, xs, b[:, :], A.add))(xs, b), tk, keep.get("xback"))
                done(i, tx)
                yield
            unit_done(u_, tk)
            keep["half", half] = tx
        end.append(tx)


    def heads_out(end, o, tok, n, gain, dst, const, free, junk, mul=None):
        ss = st(16)
        t1 = P.act(lambda e: e.activation(junk, o.rearrange("p a b -> p (a b)"), AF.Square), tok)
        t2 = P.dve(lambda e: e.tensor_reduce(ss, junk.rearrange("p (a b) -> p a b", b=128), AX, A.add), t1)
        yield
        rs, t3 = rsq(ss, 16, 1.0 / 128, 1e-6, t2)
        ov = o.rearrange("p a (h b) -> p (a h) b", b=128)
        t4 = P.dve(lambda e: e.tensor_tensor(ov, ov, rs.unsqueeze(2).to_broadcast([128, 16, 128]), A.mult), t3)
        if mul is not None:
            t4 = P.dve(lambda e: e.tensor_tensor(o, o, mul, A.mult))
        g = st(1)
        t5 = P.dve(lambda e: e.tensor_scalar(g, gain, const, None, A.mult), pc)
        outs = []
        for h in range(4):
            i, b, fr = bank()
            t6 = P.pe([tr(b[:, j * 128:(j + 1) * 128], o[:, j, h * 128:(h + 1) * 128], ident[:, :]) for j in range(NT)], t4, fr)
            t7 = evac(dst[:, h, :], b[:, :], t6, t5, free, scale=g)
            done(i, t7)
            outs.append(t7)
            yield
        end.append(outs[-2:])

    def block1_mix():
        rs, rt = rms(X, NT, D, x_in)
        xn = scv(8, 4, 2)
        xtt = to_xt(X, NT, rs, rt, pcols("norm_mix", 8), XT, xn, cst)
        keep["xt1"] = xtt
        w_in = t["w_in"][0]
        toh, tod, qk, att = [], [], [], []
        ohg, odT = scv(1, 4), scv(9, 4)
        P.weave(hgrn(toh, xtt, w_in, ohg), diff(tod, qk, att, xtt, w_in, odT), (diff_heads(0, qk, att), S1), (diff_heads(1, qk, att), S1),
                (gate1(toh, tod, att, xtt, w_in, ohg, odT), S2))

    def gate1(toh, tod, att, xtt, w_in, ohg, odT):
        while not toh:
            yield
        fr1 = toh[0]
        mb = scv(2, 8, 2)
        E4, Y4 = scv(4, 4), scv(5, 4)

        def da():
            if not tod:
                return None
            if not toh[1:]:
                toh.append(P.dma("act", lambda e: e.dma_start(X[:, :, :], t["x"][0].rearrange("(t p) n -> p t n", p=128)), "x1", att))
                keep["xback"] = toh[1]
            return odT, tod

        yield from gated(w_in, 3584, ((0, t["w_branch_hg"][0], lambda: (ohg, fr1)), (1, t["w_branch_da"][0], da)), None,
                         t["w_out"][0], xtt, mb, ([E4[:, 0, :], E4[:, 1, :]], [Y4[:, 0, :], Y4[:, 1, :]]), fr1, [])

    def hgrn(toh, xtt, w_in, ohg):
        q, k, b_, qr, kr, og = (scv(i, 4) for i in (0, 1, 2, 3, 4, 5))
        kt, v, o = k, b_, q
        E = SC[:, 6, 0:1024].rearrange("p (t n) -> p t n", t=2)
        SB = scv(7, 4)
        fr0 = P.now()
        lb, oml, l1, l2 = st(4), st(4), st(4), st(4)
        a0, a1 = pcols("hg_lb", 8)[:, 0:4], pcols("hg_lb", 8)[:, 4:8]
        P.dve(lambda e: e.tensor_tensor(lb, a0, a1, A.max))
        P.dve(lambda e: e.tensor_tensor(l1, a0, lb, A.subtract))
        t1 = P.dve(lambda e: e.tensor_tensor(l2, a1, lb, A.subtract))
        P.act(lambda e: e.activation(l1, l1, AF.Exp), t1)
        t1 = P.act(lambda e: e.activation(l2, l2, AF.Exp))
        P.dve(lambda e: e.tensor_tensor(l2, l1, l2, A.add), t1)
        P.dve(lambda e: e.reciprocal(l2, l2))
        P.dve(lambda e: e.tensor_tensor(lb, l1, l2, A.mult))
        P.dve(lambda e: e.tensor_scalar(oml, lb, -1.0, 1.0, A.mult, A.add))

        u_, s_, ut = wcols(w_in, 512, 512)
        wv2 = s_.rearrange("p (k n) -> p k n", k=8)
        for h in range(4):
            i, b, tk = proj_f(wv2, h * 128, 128, XT, 8, ut, xtt)
            kh, lh, bh = k[:, h, :], qr[:, h, :], b_[:, h, :]
            ta = P.act(lambda e, kh=kh, b=b: e.activation(kh, b[:, :], AF.Exp, scale=-1.0), tk)
            done(i, ta)
            yield
            P.dve(lambda e, kh=kh: e.tensor_scalar(kh, kh, 1.0, None, A.add), ta)
            P.dve(lambda e, kh=kh: e.reciprocal(kh, kh))
            tf = P.dve(lambda e, kh=kh, h=h: e.tensor_scalar(kh, kh, oml[:, h:h + 1], lb[:, h:h + 1], A.mult, A.add))
            tl = P.act(lambda e, kh=kh, lh=lh: e.activation(lh, kh, AF.Ln), tf)
            yield
            P.dve(lambda e, kh=kh: e.tensor_scalar(kh, kh, -1.0, 1.0, A.mult, A.add), tl)
            P.dve(lambda e, bh=bh, lh=lh: e.tensor_tensor_scan(bh, CH[:, :], lh, 0.0, A.mult, A.add), tl, cst)
            yield
        unit_done(u_, tk)

        u_, s_, ut = wcols(w_in, 0, 512)
        wv = s_.rearrange("p (k n) -> p k n", k=8)
        for h in range(4):
            i, b, tk = proj_f(wv, h * 128, 128, XT, 8, ut, xtt)
            tq = evac(q[:, h, :], b[:, :], tk)
            done(i, tq)
            yield
        unit_done(u_, tk)
        qdone = P.now("act", "dve")
        def ch(x):
            return x.rearrange("p h (c j) -> p (h c) j", j=64)

        bc = ch(b_)
        eref, eend = st(32), st(32)
        P.dve(lambda e: e.tensor_tensor(ch(qr), bc, bc[:, :, 31:32].to_broadcast([128, 32, 64]), A.subtract))
        t1 = P.dve(lambda e: e.tensor_tensor(eend, bc[:, :, 63], bc[:, :, 31], A.subtract))
        yield
        P.act(lambda e: e.activation(eend, eend, AF.Exp), t1)
        P.act(lambda e: e.activation(eref, bc[:, :, 31], AF.Exp))
        P.act(lambda e: e.activation(kr, qr, AF.Exp, scale=-1.0))
        t1 = P.act(lambda e: e.activation(qr, qr, AF.Exp))
        P.dve(lambda e: e.tensor_tensor(kr, kr, k, A.mult), t1)
        yield
        tqk = P.dve(lambda e: e.tensor_tensor(qr, qr, q, A.mult), qdone)
        er, ee = (x.rearrange("p (h c) -> p h c", h=4) for x in (eref, eend))
        tes = P.dve(lambda e: e.tensor_tensor(ee[:, :, 0:7], ee[:, :, 0:7], er[:, :, 1:8], A.mult))

        u_, s_, ut = wcols(w_in, 1024, 512)
        wv3 = s_.rearrange("p (k n) -> p k n", k=8)
        for tt in range(NT):
            i, b, tk = proj_t(wv3, 0, 512, XT, tt, 8, ut, xtt)
            tv = evac(v[:, tt, :], b[:, :], tk, tes, P.now("act"))
            done(i, tv)
            yield
        unit_done(u_, tk)
        vdone = P.now("act", "dve")
        u_, s_, ut = wcols(w_in, 1536, 512)
        efree = [[], []]
        wv4 = s_.rearrange("p (k n) -> p k n", k=8)
        for tt in range(NT):
            i, b, tk = proj_t(wv4, 0, 512, XT, tt, 8, ut, xtt)
            e_ = E[:, tt % 2, :]
            ta = P.act(lambda e, e_=e_, b=b: e.activation(e_, b[:, :], AF.Exp, scale=-1.0), tk, efree[tt % 2])
            yield
            P.dve(lambda e, e_=e_: e.tensor_scalar(e_, e_, 1.0, None, A.add), ta)
            P.dve(lambda e, e_=e_: e.reciprocal(e_, e_))
            tv = P.dve(lambda e, e_=e_, b=b, tt=tt: e.tensor_tensor(og[:, tt, :], e_, b[:, :], A.mult))
            done(i, tv)
            efree[tt % 2] = [tv]
            yield
        unit_done(u_, tk)
        for tt in range(NT):
            i, b, fr = bank()
            t2 = P.pe([tr(b[:, h * 128:(h + 1) * 128], kr[:, h, tt * 128:(tt + 1) * 128], ident[:, :]) for h in range(4)], tqk, fr)
            tkt = evac(kt[:, tt, :], b[:, :], t2, tqk)
            done(i, tkt)
            yield
        ktdone = P.now("act", "dve")
        tz = P.dve(lambda e: e.memset(SC[:, 7, :], 0.0), cst)
        free_sc = [tz, tz]
        mfree = [tz, tz]
        tm = tz
        mask = mk[:, 0, :].unsqueeze(1).to_broadcast([128, 4, 128])
        for tt in range(NT):
            i, b, fr = bank()
            cs = slice(tt * 128, (tt + 1) * 128)
            t2 = P.pe([mm(b[:, h * 128:(h + 1) * 128], kr[:, h, cs], qr[:, h, cs], True, True) for h in range(4)], tqk, fr)
            scm = SB[:, tt % 2, :]
            t3 = P.dve(lambda e, scm=scm, b=b: e.copy_predicated(scm.rearrange("p (h n) -> p h n", h=4), mask, b[:, :].rearrange("p (h n) -> p h n", h=4)), t2, free_sc[tt % 2])
            done(i, t3)
            yield
            i, b, fr = bank()
            t4 = P.pe([mm(b[:, h * 128:(h + 1) * 128], scm[:, h * 128:(h + 1) * 128], v[:, tt, h * 128:(h + 1) * 128], h == 0, tt == 0) for h in range(4)], t3, fr, vdone)
            free_sc[tt % 2] = t4
            for hb in range(2):
                c = 2 * tt + hb
                c0 = c * 64
                p0 = hb * 64
                M = SB[:, 2 + c % 2, :]
                Mn = SB[:, 2 + (c + 1) % 2, :]
                if c:
                    t4 = P.pe([mm(b[p0:p0 + 64, h * 128:(h + 1) * 128], qr[:, h, c0:c0 + 64], M[:, h * 128:(h + 1) * 128], False, True) for h in range(4)], tm)
                    mfree[c % 2] = t4
                if c < 7:
                    i2, b2, fr2 = bank()
                    t5 = P.pe([mm(b2[:, h * 128:(h + 1) * 128], kt[p0:p0 + 64, tt, h * 128:(h + 1) * 128], v[p0:p0 + 64, tt, h * 128:(h + 1) * 128], True, True) for h in range(4)], fr2, ktdone)
                    t6 = P.dve(lambda e, M=M, Mn=Mn, b2=b2: e.tensor_tensor(Mn, M, b2[:, :], A.add), t5, mfree[(c + 1) % 2])
                    done(i2, t6)
                    tm = P.dve(lambda e, Mn=Mn, c=c: e.tensor_tensor(Mn.rearrange("p (h n) -> p h n", h=4), Mn.rearrange("p (h n) -> p h n", h=4), ee[:, :, c:c + 1].to_broadcast([128, 4, 128]), A.mult), tes)
                yield
            t7 = evac(o[:, tt, :], b[:, :], t4, tqk)
            done(i, t7)
        yield from heads_out(toh, o, P.now("act", "dve"), 128, pcol("hg_out_norm"), ohg, 1.0, P.now(), SC[:, 3, :], mul=og)
        toh[:] = [P.now()]

    def diff(tod, qk, att, xtt, w_in, odT):
        fr0 = P.now()
        XX = X[:, :, :].rearrange("p t n -> p (t n)")
        dq, dk, dv, o2 = scv(8, 4), scv(9, 4), scv(10, 4), scv(8, 4)
        qT, kT = (XX[:, 2048 * n:2048 * n + 2048].rearrange("p (a n) -> p a n", a=4) for n in range(2))
        ET = scv(11, 4)
        def proj(n, dst):
            u_, s_, ut = wcols(w_in, 2048 + 512 * n, 512)
            wn = s_.rearrange("p (k n) -> p k n", k=8)
            for tt in range(NT):
                i, b, tk = proj_t(wn, 0, 512, XT, tt, 8, ut, xtt)
                tv = evac(dst[:, tt, :], b[:, :], tk, fr0)
                done(i, tv)
                yield
            unit_done(u_, tk)

        for n, (src, dstT) in enumerate(((dq, qT), (dk, kT))):
            yield from proj(n, src)
            ss = st(32)
            t1 = P.act(lambda e, src=src: e.activation(ET, src, AF.Square), P.now())
            yield
            t2 = P.dve(lambda e, ss=ss: e.tensor_reduce(ss, ET.rearrange("p a (j b) -> p (a j) b", b=64), AX, A.add), t1)
            yield
            rs_, t3 = rsq(ss, 32, 1.0 / 64, 1e-6, t2)
            sv = src.rearrange("p a (j b) -> p (a j) b", b=64)
            P.dve(lambda e, sv=sv, rs_=rs_: e.tensor_tensor(sv, sv, rs_.unsqueeze(2).to_broadcast([128, 32, 64]), A.mult), t3)
            P.dve(lambda e, sv=sv, n=n: e.tensor_tensor(sv, sv, G64[:, n:n + 1, :].to_broadcast([128, 32, 64]), A.mult), par)
            yield
            for tt in range(NT):
                s3 = src[:, tt, :].rearrange("p (j b) -> p j b", b=64)
                x1, x2 = s3[:, :, 0:32], s3[:, :, 32:64]
                e1 = ET[:, 2 * (tt % 2), :].rearrange("p (j b) -> p j b", b=64)
                e2 = ET[:, 2 * (tt % 2) + 1, :].rearrange("p (j b) -> p j b", b=64)
                cb = ROPE[:, 0, tt:tt + 1, :].to_broadcast([128, 8, 32])
                sb_ = ROPE[:, 1, tt:tt + 1, :].to_broadcast([128, 8, 32])
                P.dve(lambda e, a=e1[:, :, 0:32], x=x1, c=cb: e.tensor_tensor(a, x, c, A.mult), t1)
                P.dve(lambda e, a=e1[:, :, 32:64], x=x2, c=cb: e.tensor_tensor(a, x, c, A.mult))
                P.dve(lambda e, a=e2[:, :, 0:32], x=x2, c=sb_: e.tensor_tensor(a, x, c, A.mult))
                P.dve(lambda e, a=e2[:, :, 32:64], x=x1, c=sb_: e.tensor_tensor(a, x, c, A.mult))
                P.dve(lambda e, a=x1, x=e1[:, :, 0:32], y=e2[:, :, 0:32]: e.tensor_tensor(a, x, y, A.subtract))
                tx = P.dve(lambda e, a=x2, x=e1[:, :, 32:64], y=e2[:, :, 32:64]: e.tensor_tensor(a, x, y, A.add))
                yield
            for h in range(4):
                i, b, fr = bank()
                t6 = P.pe([tr(b[:, j * 128:(j + 1) * 128], src[:, j, h * 128:(h + 1) * 128], ident[:, :]) for j in range(NT)], tx, fr)
                t7 = evac(dstT[:, h, :], b[:, :], t6, fr0)
                done(i, t7)
                yield
        yield from proj(2, dv)
        l = st(4)
        P.dve(lambda e: e.tensor_tensor_reduce(LAMP[:, 0:64], LAMP[:, 0:64], LAMP[:, 64:128], 1.0, 0.0, A.mult, A.add, l[:, 0:1]), par)
        t1 = P.dve(lambda e: e.tensor_tensor_reduce(LAMP[:, 128:192], LAMP[:, 128:192], LAMP[:, 192:256], 1.0, 0.0, A.mult, A.add, l[:, 1:2]))
        t1 = P.act(lambda e: e.activation(l[:, 0:2], l[:, 0:2], AF.Exp), t1)
        P.dve(lambda e: e.tensor_tensor(l[:, 2:3], l[:, 1:2], l[:, 0:1], A.subtract), t1)
        P.dve(lambda e: e.tensor_scalar(l[:, 3:4], l[:, 2:3], -LAM_INIT, None, A.add))
        qk += [qT, kT, dv, P.now(), l[:, 3:4], ET, o2]
        while len(att) < 2:
            yield
        yield from heads_out(tod, o2, att, 128, pcol("da_out_norm"), odT, 1.0 - LAM_INIT, P.now(), SC[:, 10, :])

    def diff_heads(sd, qk, att):
        while not qk:
            yield
        qT, kT, dv, tqk, nlam, ET, o2 = qk
        ps = [ET[:, 2 * sd + c, :] for c in range(2)]
        aT_ = SC[:, 6, 1024 + 512 * sd:1536 + 512 * sd]
        pfree = [tqk]
        afree = [tqk]
        for qt in range(NT):
            nk = 128 * (qt + 1)
            io, bo, fro = bank()
            for h in (2 * sd, 2 * sd + 1):
                sts = st(8)
                for c in range(2):
                    i, b, fr = bank()
                    t2 = P.pe([mm(b[:, 0:nk], qT[64 * c:64 * c + 64, h, qt * 128:(qt + 1) * 128], kT[64 * c:64 * c + 64, h, 0:nk], True, True)], tqk, fr)
                    P.dve(lambda e, b=b, nk=nk: e.tensor_tensor(b[:, nk - 128:nk], b[:, nk - 128:nk], diagm[:, :], A.add), t2, cst)
                    P.dve(lambda e, b=b, nk=nk, m=sts[:, c:c + 1]: e.tensor_reduce(m, b[:, 0:nk], AX, A.max))
                    t3 = P.dve(lambda e, m=sts[:, c:c + 1]: e.tensor_scalar(m, m, -0.125, None, A.mult))
                    t4 = P.act(lambda e, p_=ps[c][:, 0:nk], b=b, nk=nk, m=sts[:, c:c + 1], z=sts[:, 2 + c:3 + c]: e.activation(p_, b[:, 0:nk], AF.Exp, bias=m, scale=0.125, accum_out=z), t3, pfree)
                    done(i, t4)
                    yield
                P.dve(lambda e, a=sts: e.reciprocal(a[:, 4:6], a[:, 2:4]), t4)
                P.dve(lambda e, a=sts: e.tensor_tensor(a[:, 5:6], a[:, 5:6], nlam, A.mult))
                P.dve(lambda e, a=sts, p=ps[1][:, 0:nk]: e.tensor_scalar(p, p, a[:, 5:6], None, A.mult))
                t5 = P.dve(lambda e, a=sts, p=ps[0][:, 0:nk], p1=ps[1][:, 0:nk]: e.scalar_tensor_tensor(p, p, a[:, 4:5], p1, A.mult, A.add))
                yield
                i, b, fr = bank()
                t6 = P.pe([tr(b[:, j * 128:(j + 1) * 128], ps[0][:, j * 128:(j + 1) * 128], ident[:, :]) for j in range(qt + 1)], t5, fr)
                pfree = [t6]
                aT = aT_[:, 0:nk]
                t7 = evac(aT, b[:, 0:nk], t6, afree)
                done(i, t7)
                yield
                ho = (h - 2 * sd) * 128
                t8 = P.pe([mm(bo[:, ho:ho + 128], aT[:, j * 128:(j + 1) * 128], dv[:, j, h * 128:(h + 1) * 128], j == 0, j == qt) for j in range(qt + 1)], t7, fro)
                afree = [t8]
            t9 = evac(o2[:, qt, 256 * sd:256 * sd + 256], bo[:, 0:256], t8, tqk)
            done(io, t9)
            yield
        att.append(P.now())

    def first_hot(dst, vals, mx, n, *deps):
        tmp, m = st(NT * n).rearrange("p (a b) -> p a b", b=n), st(NT)
        io = iotm[:, 0:n].unsqueeze(1).to_broadcast([128, NT, n])
        P.dve(lambda e: e.tensor_tensor(dst, vals, mx.unsqueeze(2).to_broadcast([128, NT, n]), A.is_equal), *deps)
        P.dve(lambda e: e.tensor_tensor(tmp, dst, io, A.mult))
        P.dve(lambda e: e.tensor_reduce(m, tmp, AX, A.min))
        return P.dve(lambda e: e.tensor_tensor(dst, io, m.unsqueeze(2).to_broadcast([128, NT, n]), A.is_equal))

    def moe(bi):
        stn[0] = ST_KEEP
        wa, wb, wc, gname = ((("w1", "w3", "w2", "norm_moe"), ("w_e_gate_2", "w_e_up_2", "w_e_down_2", "norm_ffn_2"))[bi])
        W1, W3, W2 = t[wa][0], t[wb][0], t[wc][0]
        fr = P.now()
        xn = scv(0, 4, 2)
        gr = scv(2, 2)[:, 0, :]
        tg = P.dma("act", lambda e: e.dma_start(gr, t[gname].to_broadcast([128, D])), f"moeg{bi}", fr)
        WG = SC[:, 9, 0:288].rearrange("p (a b) -> p a b", b=36)
        twg = P.dve(lambda e: e.tensor_tensor(WG, WR[:, bi, :, :], pcols(gname, 8).unsqueeze(2).to_broadcast([128, 8, 36]), A.mult), par, pc, fr)
        xtt = []
        for k in range(8):
            i, b, frb = bank()
            tk = P.pe([tr(b[:, j * 128:(j + 1) * 128], X[:, j, k * 128:(k + 1) * 128], ident[:, :]) for j in range(NT)], keep["half", k // 4], frb, cst)
            t2 = P.dve(lambda e, k=k, b=b: e.tensor_copy(XT[:, k, :], b[:, :]), tk, P.now("pe"))
            done(i, t2)
            xtt.append(t2)
        rs, rt = rms(X, NT, D, keep["half", 1])
        for j in range(NT):
            ta = P.act(lambda e, j=j: e.activation(xn[:, j, :], X[:, j, :], AF.Identity, scale=rs[:, j:j + 1]), rt, fr)
            tx = P.pool(lambda e, j=j: e.tensor_tensor(xn[:, j, :], xn[:, j, :], gr, A.mult), ta, tg)
        txr = P.dma("act", lambda e: e.dma_start(xrows.rearrange("(t p) n -> p t n", p=128), xn), f"moex{bi}", tx)
        i, b, frb = bank()
        for k in range(8):
            tk = P.pe([mm(b[0:36, :], WG[:, k, :], XT[:, k, :], k == 0, k == 7)], frb, xtt[k], twg)
        LT = SC[0:36, 9, 512:1024]
        tl = P.dve(lambda e, b=b: e.tensor_copy(LT, b[0:36, :]), tk, fr)
        done(i, tl)
        i, b, frb = bank()
        tk = P.pe([tr(b[:, tt * 64:tt * 64 + 36], LT[:, tt * 128:(tt + 1) * 128], ident[0:36, 0:36]) for tt in range(NT)], frb, tl)
        L = st(NT * 36).rearrange("p (a b) -> p a b", b=36)
        for tt in range(NT):
            tl = P.dve(lambda e, b=b, tt=tt: e.scalar_tensor_tensor(L[:, tt, :], b[:, tt * 64:tt * 64 + 36], rs[:, tt:tt + 1], RB[:, bi, :], A.mult, A.add), tk, rt)
        done(i, tl)
        gl = L[:, :, 0:4]
        caps = st(T // CAP - 1)
        P.dve(lambda e: e.tensor_scalar(caps, iotf[:, 1:T // CAP], float(CAP), None, A.mult), cst)

        def s3(n):
            return st(NT * n).rearrange("p (a b) -> p a b", b=n)

        gm, gs, goh, ge, ein, tmp8, oh1, oh2 = st(NT), st(NT), s3(4), s3(4), s3(8), s3(8), s3(8), s3(8)
        P.dve(lambda e: e.tensor_reduce(gm, gl, AX, A.max))
        t1 = P.dve(lambda e: e.tensor_tensor(ge, gl, gm.unsqueeze(2).to_broadcast([128, NT, 4]), A.subtract))
        t1 = P.act(lambda e: e.activation(ge, ge, AF.Exp), t1)
        P.dve(lambda e: e.tensor_reduce(gs, ge, AX, A.add), t1)
        P.dve(lambda e: e.reciprocal(gs, gs))
        first_hot(goh, gl, gm, 4)
        goh4 = goh.unsqueeze(3).to_broadcast([128, NT, 4, 8])
        v4 = lambda x: x.rearrange("p a (g j) -> p a g j", g=4)
        OH = [s3(32), s3(32)]
        P.dve(lambda e: e.tensor_tensor(v4(OH[0]), v4(L[:, :, 4:36]), goh4, A.mult))
        P.dve(lambda e: e.tensor_reduce(ein, OH[0].rearrange("p a (g j) -> p a j g", g=4), AX, A.add))
        v1, v2, g1, g2 = st(NT), st(NT), st(NT), st(NT)
        P.dve(lambda e: e.tensor_reduce(v1, ein, AX, A.max))
        first_hot(oh1, ein, v1, 8)
        P.dve(lambda e: e.scalar_tensor_tensor(tmp8, oh1, NEG, ein, A.mult, A.add))
        P.dve(lambda e: e.tensor_reduce(v2, tmp8, AX, A.max))
        first_hot(oh2, tmp8, v2, 8)
        t1 = P.dve(lambda e: e.tensor_tensor(v2, v2, v1, A.subtract))
        t1 = P.act(lambda e: e.activation(v2, v2, AF.Exp), t1)
        P.dve(lambda e: e.tensor_scalar(v1, v2, 1.0, None, A.add), t1)
        P.dve(lambda e: e.reciprocal(v1, v1))
        P.dve(lambda e: e.tensor_tensor(g1, v1, gs, A.mult))
        P.dve(lambda e: e.tensor_tensor(g2, g1, v2, A.mult))
        M = s3(32)
        for k, oh in ((0, oh1), (1, oh2)):
            P.dve(lambda e, k=k, oh=oh: e.tensor_tensor(v4(OH[k]), oh.unsqueeze(2).to_broadcast([128, NT, 4, 8]), goh4, A.mult))
        tM = P.dve(lambda e: e.tensor_tensor(M, OH[0], OH[1], A.add))
        i, b, frb = bank()
        Mf = M.rearrange("p a b -> p (a b)")
        tk = P.pe([mm(b[:, 0:128], upper[:, :], Mf, True, True), mm(b[:, 128:256], ones[:, :], Mf, True, True)], frb, tM, cst)
        tot, ov, ove, hi, lo = st(32), st(32), st(32), st(32), st(32)
        pos, c1 = s3(32), s3(32)
        bef = SC[:, 9, 1168:1296].rearrange("p (a b) -> p a b", b=32)
        P.dve(lambda e: e.memset(bef[:, 0, :], 0.0))
        for tt in range(NT):
            dst = bef[:, tt + 1, :] if tt < NT - 1 else tot
            P.dve(lambda e, b=b, tt=tt, dst=dst: e.tensor_tensor(dst, bef[:, tt, :], b[:, 128 + 32 * tt:160 + 32 * tt], A.add), tk)
        big = SC[:, 8, 1536:2048]
        nb_ = T // CAP - 1
        bg = big[:, 0:32 * nb_].rearrange("p (a b) -> p a b", b=nb_)
        P.dve(lambda e: e.tensor_tensor(bg, tot.unsqueeze(2).to_broadcast([128, 32, nb_]), caps.unsqueeze(1).to_broadcast([128, 32, nb_]), A.is_gt), fr)
        P.dve(lambda e: e.tensor_reduce(ov, bg, AX, A.add))
        P.dve(lambda e: e.tensor_tensor_scan(ove, ones[:, 0:32], ov, 0.0, A.mult, A.add), cst)
        P.dve(lambda e: e.tensor_tensor(hi, ove, ov, A.subtract))
        P.dve(lambda e: e.tensor_scalar(hi, hi, float(CAP), float((NE - 1) * CAP), A.mult, A.add))
        P.dve(lambda e: e.tensor_scalar(lo, iotf[:, 0:32], float(CAP), None, A.mult))
        P.dve(lambda e: e.tensor_tensor(lo, lo, hi, A.subtract))
        tp = P.dve(lambda e, b=b: e.tensor_tensor(pos, bef, b[:, 0:128].rearrange("p (a b) -> p a b", b=32), A.add))
        done(i, tp)
        P.dve(lambda e: e.tensor_scalar(c1, pos, float(CAP), None, A.is_lt))
        P.dve(lambda e: e.tensor_tensor(c1, c1, lo.unsqueeze(1).to_broadcast([128, NT, 32]), A.mult))
        P.dve(lambda e: e.tensor_tensor(pos, pos, c1, A.add))
        P.dve(lambda e: e.tensor_tensor(pos, pos, hi.unsqueeze(1).to_broadcast([128, NT, 32]), A.add))
        pk, pki = st(2 * NT).rearrange("p (a b) -> p a b", a=2), st(2 * NT).bitcast(I32).rearrange("p (a b) -> p a b", a=2)
        for k in range(2):
            P.dve(lambda e, k=k: e.tensor_tensor(OH[k], OH[k], pos, A.mult))
            P.dve(lambda e, k=k: e.tensor_reduce(pk[:, k, :], OH[k], AX, A.add))
        tpk = P.dve(lambda e: e.tensor_copy(pki, pk))
        NP = (NE + NOV) * CAP // 128
        pr, pp = st(2 * NT).bitcast(I32).rearrange("p (a b) -> p a b", a=2), st(2 * NT).bitcast(I32).rearrange("p (a b) -> p a b", a=2)
        prf, ppf = st(2 * NT).rearrange("p (a b) -> p a b", a=2), st(2 * NT).rearrange("p (a b) -> p a b", a=2)
        P.dve(lambda e: e.tensor_scalar(pr, pki, 127, None, A.bitwise_and))
        P.dve(lambda e: e.tensor_scalar(pp, pki, 7, None, A.arith_shift_right))
        P.dve(lambda e: e.tensor_copy(prf, pr))
        P.dve(lambda e: e.tensor_copy(ppf, pp))
        RH = SC[:, 8, 0:1024].rearrange("p (a n) -> p a n", a=8)
        CHT = SC[:, 8, 1024:1024 + 8 * NP].rearrange("p (a n) -> p a n", a=8)
        f8 = lambda x: x.rearrange("p a b -> p (a b)").unsqueeze(2)
        P.dve(lambda e: e.tensor_tensor(CHT, iotf[:, 0:NP].unsqueeze(1).to_broadcast([128, 8, NP]), f8(ppf).to_broadcast([128, 8, NP]), A.is_equal), fr, cst)
        P.dve(lambda e: e.tensor_tensor(CHT, CHT, f8(fval[:, :, :]).to_broadcast([128, 8, NP]), A.mult))
        t1 = P.dve(lambda e: e.tensor_tensor(RH, iotf[:, :].unsqueeze(1).to_broadcast([128, 8, 128]), f8(prf).to_broadcast([128, 8, 128]), A.is_equal))
        i, b, frb = bank()
        tk = P.pe([mm(b[:, 0:NP], RH[:, n, :], CHT[:, n, :], n == 0, n == 7) for n in range(8)], t1, frb)
        sidx, gidx = st(NP).bitcast(I32), st(NP).bitcast(I32)
        t3 = P.dve(lambda e, b=b: e.tensor_scalar(sidx, b[:, 0:NP], float(4 * T), None, A.add), tk)
        done(i, t3)
        tix = P.dve(lambda e: e.tensor_scalar(gidx, sidx, 1, None, A.arith_shift_right))
        exb, nov = st(NOV), st(NOV + 1).bitcast(I32)
        b3 = big.rearrange("p (a b) -> p a b", b=32)
        P.dve(lambda e: e.tensor_tensor(b3, ove.unsqueeze(1).to_broadcast([128, NOV, 32]), iotf[:, 0:NOV].unsqueeze(2).to_broadcast([128, NOV, 32]), A.is_le))
        P.dve(lambda e: e.tensor_reduce(exb, b3, AX, A.add))
        P.dve(lambda e: e.tensor_scalar(exb, exb, float(NE - 1), None, A.min))
        P.dve(lambda e: e.tensor_copy(nov[:, 0:NOV], exb))
        tnov = P.dve(lambda e: e.tensor_copy(nov[:, NOV:NOV + 1], ove[:, 31:32]))
        XG, YS, XE, HD, HT = scv(5, 2), scv(6, 2), scv(7, 2), scv(8, 4), scv(9, 4)
        tz = P.pool(lambda e: e.memset(SC[:, 5, :], 0.0), fr)
        HALF = (slice(0, 64), slice(64, 128))

        def gather(Q, p, rdy, fr_):
            s = p % 2
            return Q.dma("pool", lambda e: e.indirect_dma_start(XG[:, s, :], None, xrows, bass.IndirectOffsetOnAxis(ap=gidx[:, p:p + 1], axis=0), bounds_check=T - 1, oob_is_err=False), f"g{s}", rdy, fr_.get("xg"))

        def turn(Q, p, tg_, fr_):
            s = p % 2
            ts = []
            for hf in range(2):
                i, b, fb = bank()
                t2 = Q.pe([tr(b[:, j * 128:(j + 1) * 128], XG[:, s, (4 * hf + j) * 128:(4 * hf + j + 1) * 128], ident[:, :]) for j in range(4)], tg_, fb)
                dst = XE[:, s, hf * 512:(hf + 1) * 512]
                if hf == 0:
                    t3 = Q.act(lambda e, dst=dst, b=b: e.activation(dst, b[:, :], AF.Copy), t2, fr_.get("xe"))
                else:
                    t3 = Q.dve(lambda e, dst=dst, b=b: e.tensor_copy(dst, b[:, :]), t2, fr_.get("xe"))
                done(i, t3)
                ts.append(t3)
            return t2, ts

        def up(Q, p, tx_, w1, w3, fr_):
            s = p % 2
            hd = HD[:, s, :]
            ks = []
            for w_ in (w1, w3):
                i, b, fb = bank()
                ks.append((i, b, Q.pe([mm(b[HALF[x], :], XE[:, s, k * 128 + 64 * x:k * 128 + 64 * x + 64], w_[x][1][:, k, :], k == 0, k == 7) for k in range(8) for x in range(2)], tx_, fb, [u[2] for u in w_])))
            (i1, b1, k1), (i3, b3, k3) = ks
            ta = Q.act(lambda e: e.activation(hd, b1[:, :], AF.Silu), k1, fr_.get("hd"))
            done(i1, ta)
            th = Q.dve(lambda e: e.tensor_tensor(hd, hd, b3[:, :], A.mult), ta, k3)
            done(i3, th)
            return k1, k3, th

        def down(Q, p, th, w2, fr_):
            s = p % 2
            hd, ht, ys = HD[:, s, :], HT[:, s, :], YS[:, s, :]
            i, b, fb = bank()
            t2 = Q.pe([tr(b[:, j * 128:(j + 1) * 128], hd[:, j * 128:(j + 1) * 128], ident[:, :]) for j in range(4)], th, fb)
            t3 = Q.act(lambda e, b=b: e.activation(ht, b[:, :], AF.Copy), t2, fr_.get("ht"))
            done(i, t3)
            tys = []
            for hf in range(2):
                i, b, fb = bank()
                k2 = Q.pe([mm(b[HALF[x], :], ht[:, k * 128 + 64 * x:k * 128 + 64 * x + 64], w2[x][1][:, k, hf * 512:(hf + 1) * 512], k == 0, k == 3) for k in range(4) for x in range(2)], t3, fb, [u[2] for u in w2])
                dst = ys[:, hf * 512:(hf + 1) * 512]
                if hf:
                    ty = Q.act(lambda e, dst=dst, b=b: e.activation(dst, b[:, :], AF.Copy), k2, fr_.get("ys"))
                else:
                    ty = Q.dve(lambda e, dst=dst, b=b: e.tensor_copy(dst, b[:, :]), k2, fr_.get("ys"))
                done(i, ty)
                tys.append(ty)
            return t2, k2, tys

        def scatter(Q, p, tys):
            s = p % 2
            return Q.dma("pool", lambda e: e.indirect_dma_start(ytab, bass.IndirectOffsetOnAxis(ap=sidx[:, p:p + 1], axis=0), YS[:, s, :], None, bounds_check=2 * T - 1, oob_is_err=False), f"y{s}", tys)

        def pairs(Q, n, first, rdy, fr0_, weights, used, end_of=None):
            fr_ = [dict(fr0_), dict(fr0_)]
            tg_ = gather(Q, first, rdy, fr_[first % 2])
            t2, tx_ = turn(Q, first, tg_, fr_[first % 2])
            fr_[first % 2]["xg"] = t2
            ty = [None, None]
            for p in range(first, first + n):
                s = p % 2
                more = p + 1 < first + n
                w1 = weights(p, 0)
                w3 = weights(p, 1)
                if more and end_of is None:
                    tg_ = gather(Q, p + 1, rdy, fr_[1 - s])
                k1, k3, th = up(Q, p, tx_, w1, w3, fr_[s])
                fr_[s]["xe"] = k3
                used(w1, k1)
                used(w3, k3)
                if more and end_of is None:
                    t2, tx_ = turn(Q, p + 1, tg_, fr_[1 - s])
                    fr_[1 - s]["xg"] = t2
                w2 = weights(p, 2)
                t2, k2, tys = down(Q, p, th, w2, fr_[s])
                fr_[s]["hd"], fr_[s]["ht"] = t2, k2
                used(w2, k2)
                fr_[s]["ys"] = ty[s] = scatter(Q, p, tys)
                if end_of is not None:
                    end_of(p)
                    if more:
                        tg_ = gather(Q, p + 1, rdy, fr_[1 - s])
                        t2, tx_ = turn(Q, p + 1, tg_, fr_[1 - s])
                        fr_[1 - s]["xg"] = t2
            return ty

        def view(slot, j):
            return slot.rearrange("p (k n) -> p k n", k=4 if j == 2 else 8)

        def src(w_, e_):
            return w_[e_].rearrange("(k p) n -> p k n", p=128)

        def weights(p, j):
            us = [unit([(lambda sl, j=j: view(sl, j), src((W1, W3, W2)[j], 2 * p + x))]) for x in range(2)]
            return [(u_[0], view(u_[1], j), u_[2]) for u_ in us]

        def used(us, tok):
            for u_ in us:
                unit_done(u_[0], tok)

        spare = [SC[:, 10:12, :], SC[:, 2:4, :], SC[:, 0:2, :]]
        slots.extend(x.rearrange("p a b -> p (a b)") for x in spare)
        ring_free.extend([fr + [rt], fr + [tx], [txr]])
        ring_order.extend(range(NRING, len(slots)))
        frx = {k: fr + [tk, tnov] for k in ("xe", "hd", "ht", "ys")}
        ty = pairs(P, NE // 2, 0, [tix, txr, tz], frx, weights, used)
        O = Prog(nc, ctx, f"o{bi}")
        saved = list(bank_free), bank_no[0]
        for i in range(8):
            bank_free[i] = []
        segs = []
        wfree = [None] * 3

        def oweights(p, j):
            res = []
            for x in range(2):
                slot = slots[2 * j + x]

                def load(e, slot=slot, x=x):
                    o_ = 2 * (p - NE // 2) + x
                    v = e.value_load(nov[0:1, o_:o_ + 1], min_val=0, max_val=NE - 1)
                    return e.dma_start(view(slot, j), (W1, W3, W2)[j][bass.ds(v, 1)].rearrange("a (k p) n -> p (a k) n", p=128))

                tok = O.dma("sp", load, f"w{2 * j + x}", wfree[j])
                res.append((j, view(slot, j), tok))
            return res

        def oused(us, tok):
            wfree[us[0][0]] = tok

        pairs(O, NOV // 2, NE // 2, None, {}, oweights, oused,
              lambda p: segs.append(({g: len(O.q[g]) for g in ENG}, list(O.n.items()))))
        bank_free[:] = saved[0]
        bank_no[0] = saved[1]
        barrier = P.now() + ty + [tnov] + [(f"ring{i}", P.n[f"ring{i}"]) for i in range(len(slots))]

        def branch(eng):
            def run(e):
                v = e.value_load(nov[0:1, NOV:NOV + 1], min_val=0, max_val=NOV)
                seen, at = {}, 0
                for j, (to, ends) in enumerate(segs):
                    with e.If(v > 2 * j):
                        O.emit(eng, e, at, to[eng], seen)
                        for name, val in ends:
                            e.wait_ge(O.sems[name], val)
                    at = to[eng]
            return run

        toks = []
        if "join" not in P.sems:
            P.sems["join"] = ctx.enter_context(nc.semaphore("m_join"))
        for eng in ENG:
            P.raw(eng, branch(eng), barrier)
            tok = P.count("join", 1)
            P.raw(eng, lambda e: e.sem_inc(P.sems["join"], 1))
        del slots[NRING:], ring_free[NRING:]
        del ring_order[:]
        for i in range(NRING):
            unit_done(i, tok)
        YB = [SC[:, tt, :] for tt in range(NT)]
        tys = [P.dma("act", lambda e, tt=tt: e.dma_start(YB[tt], ytab.rearrange("(t p c) n -> t p (c n)", p=128, c=2)[tt]), f"yb{tt}", tok) for tt in range(NT)]
        for tt in range(NT):
            for k, gk in ((0, g1), (1, g2)):
                fy = P.dve(lambda e, k=k, gk=gk, tt=tt: e.scalar_tensor_tensor(X[:, tt, :], YB[tt][:, k * D:(k + 1) * D], gk[:, tt:tt + 1], X[:, tt, :], A.mult, A.add), tys[tt])
        keep["x"] = fy
        keep["join"] = [tok]

    def block2_mix():
        stn[0] = 0
        w_in = t["w_in_2"][0]
        m0_ = P.now()
        rs, rt = rms(X, NT, D, m0_)
        xtt = to_xt(X, NT, rs, rt, pcols("norm_mix_2", 8), XT, scv(4, 4, 2), m0_)
        fr = [m0_, rt, xtt]
        QT, Y0, GH, BV, GT = scv(0, 4), scv(1, 4), SC[:, 2:4, :].rearrange("p s n -> p (s n)"), scv(4, 4), scv(5, 4)
        GTm = GH[:, 0:2048].rearrange("p (a n) -> p a n", a=4)
        Hm = GH[:, 2048:4096].rearrange("p (a n) -> p a n", a=4)
        tmp = [SC[:, 6 + i // 4, (i % 4) * 512:(i % 4 + 1) * 512] for i in range(22)]
        mu = pcols("shift_mu_2", 14)
        omu = st(14)
        P.dve(lambda e: e.tensor_scalar(omu, mu, -1.0, 1.0, A.mult, A.add))
        nw0, na0 = st(4), st(4)
        P.dve(lambda e: e.tensor_scalar(nw0, pcols("rw_w0_2", 4), -1.0, None, A.mult))
        tom = P.dve(lambda e: e.tensor_scalar(na0, pcols("rw_a0_2", 4), -1.0, None, A.mult))

        def shifted(wv, c, j, dst, wt, free=None):
            i, b, tk = proj_f(wv, c, 128, XT, 8, wt, xtt)
            ta = P.act(lambda e: e.activation(dst, b[:, :], AF.Identity, scale=omu[:, j:j + 1]), tk, tom, free)
            tv = P.dve(lambda e: e.scalar_tensor_tensor(dst[:, 1:512], b[:, 0:511], mu[:, j:j + 1], dst[:, 1:512], A.mult, A.add), ta)
            done(i, tv)
            return tk, tv

        wq = w_in.rearrange("(k p) n -> p k n", p=128)

        def part(o, n, c):
            return (lambda s: s[:, 0:3104].rearrange("p (k n) -> p k n", k=8)[:, :, o:o + n], wq[:, :, c:c + n])

        C_RW, C_Q, C_KV, C_QI, C_KI, C_WI = 0, 1792, 2304, 2432, 2688, 2752
        ul, sl, tl = unit([part(0, 256, 1536), part(256, 64, C_KI), part(320, 64, C_KI), part(384, 4, C_WI)])
        wl = sl[:, 0:3104].rearrange("p (k n) -> p k n", k=8)
        KI, WI = sb("KI", [128, T]), st(NT * 4).rearrange("p (a b) -> p a b", b=4)
        LW = tmp[18]
        XW, XG = tmp[20], tmp[21]
        tlw = P.dma("act", lambda e: e.dma_start(LW[0:64, :], t["rw_w2_2"][0]), "lw", fr)
        tlw = P.dma("act", lambda e: e.dma_start(LW[64:128, :], t["rw_a2_2"][0]), "lw")
        G2 = tmp[19]
        tlw = P.dma("act", lambda e: e.dma_start(G2, t["rw_g2_2"][0]), "lw")
        _, tv = shifted(wl, 0, 12, XW, tl, fr)
        txw = P.act(lambda e: e.activation(XW[0:64, :], XW[0:64, :], AF.Tanh), tv)
        _, tv = shifted(wl, 128, 13, XG, tl, fr)
        ta = P.act(lambda e: e.activation(XG, XG, AF.Exp, scale=-1.0), tv)
        P.dve(lambda e: e.tensor_scalar(XG, XG, 1.0, None, A.add), ta)
        txg = P.dve(lambda e: e.reciprocal(XG, XG))
        i, b, tk = proj_f(wl, 256, 128, XT, 8, tl, xtt)
        tki = P.act(lambda e, b=b: e.activation(KI[:, :], b[:, :], AF.Copy), tk)
        done(i, tki)
        for tt in range(NT):
            i, b, tk = proj_t(wl, 384, 4, XT, tt, 8, tl, xtt)
            twi = P.dve(lambda e, b=b, tt=tt: e.tensor_scalar(WI[:, tt, :], b[:, 0:4], 1.0 / 16.0, None, A.mult), tk)
            done(i, twi)
        unit_done(ul, tk)
        for j in range(4):
            i, b, fb = bank()
            tk = P.pe([mm(b[:, :], G2[:, j * 128:(j + 1) * 128], XG, True, True)], txg, tlw, fb)
            tg = evac(GT[:, j, :], b[:, :], tk, fr)
            done(i, tg)
        fr = P.now()
        xs = P.dma("act", lambda e: e.dma_start(xkeep.rearrange("(t p) n -> p t n", p=128), X[:, :, :]), "xs", m0_)
        ESC = math.exp(-0.5)
        eref = st(32).rearrange("p (a c) -> p a c", a=4)
        eend = st(32).rearrange("p (a c) -> p a c", a=4)
        bufs = [tmp[0:11], tmp[11:18] + [tmp[19], tmp[21], SC[:, 11, 1024:1536], SC[:, 11, 1536:2048]]]
        rkv = {}
        lead = []
        used = {}

        def rkv_load(pt):
            slot = pt % 2
            sl = RING[:, slot, :]
            wv = sl[:, 0:3072].rearrange("p (k n) -> p k n", k=8)
            for n in range(3):
                tok = P.dma("sp", lambda e, n=n: e.dma_start(wv[:, :, 128 * n:128 * n + 128], wq[:, :, 512 * n + 128 * pt:512 * n + 128 * pt + 128]), f"rkv{slot}", ring_free[slot])
            rkv[pt] = (wv, tok)
            used[pt] = []

        def half(hf):
            t0 = hf * 256
            ts = slice(t0, t0 + 256)
            U = bufs[hf]
            H2 = [u[:, 256 * n:256 * n + 256] for u in U for n in range(2)]
            r, k, v, a, b_, kk, t6, t7, al, be, kR, rR = H2[0:12]
            fam = [fr]
            v2 = lambda x: x.rearrange("p (t n) -> p t n", n=128)
            aT, bT, kT, vT = (v2(x) for x in H2[12:16])
            n0 = 1 if hf else 0
            while hf and not lead:
                yield
            for pt in range(4):
                while pt not in rkv:
                    yield
                wv, wt = rkv[pt]
                pf = fam[0]
                for n, dst in enumerate((r, k, v)):
                    j = 4 * n + pt
                    i, b, fb = bank()
                    tk = P.pe([mm(b[:, 0:256 + n0], wv[:, kc, 128 * n:128 * n + 128], XT[:, kc, t0 - n0:t0 + 256], kc == 0, kc == 7) for kc in range(8)], fb, wt, xtt)
                    ta = P.act(lambda e, b=b, dst=dst, j=j: e.activation(dst, b[:, n0:256 + n0], AF.Identity, scale=omu[:, j:j + 1]), tk, tom, pf)
                    tv = P.dve(lambda e, b=b, dst=dst, j=j: e.scalar_tensor_tensor(dst[:, 1 - n0:256], b[:, 0:255 + n0], mu[:, j:j + 1], dst[:, 1 - n0:256], A.mult, A.add), ta)
                    done(i, tv)
                    yield
                used[pt].append(tk)
                if len(used[pt]) == 2:
                    ring_free[pt % 2] = list(used[pt])
                    if pt + 2 < 4:
                        rkv_load(pt + 2)
                for c0, bias, dst in ((64, na0, a), (0, nw0, t6)):
                    i, b, fb = bank()
                    tk = P.pe([mm(b[:, 0:256], LW[c0:c0 + 64, pt * 128:(pt + 1) * 128], XW[c0:c0 + 64, ts], True, True)], fb, txw, tlw, tom)
                    ta = P.act(lambda e, b=b, dst=dst, bias=bias, pt=pt: e.activation(dst, b[:, 0:256], AF.Exp, scale=-1.0, bias=bias[:, pt:pt + 1]), tk, pf)
                    done(i, ta)
                    yield
                for dst in (a, t6):
                    P.dve(lambda e, dst=dst: e.tensor_scalar(dst, dst, 1.0, None, A.add), ta)
                    P.dve(lambda e, dst=dst: e.reciprocal(dst, dst), ns=1100)
                    yield
                P.dve(lambda e: e.tensor_scalar(t6, t6, -ESC, None, A.mult))
                P.dve(lambda e: e.tensor_tensor_scan(b_, CH[:, 0:256], t6, 0.0, A.mult, A.add), pf)
                P.dve(lambda e: e.tensor_tensor(t6, b_, t6, A.subtract))
                yield
                P.dve(lambda e, pt=pt: e.tensor_scalar(kk, k, pcol("rw_k_k_2", pt), None, A.mult))
                tv = P.dve(lambda e: e.tensor_tensor(t7, kk, kk, A.mult))
                i, b, fb = bank()
                tk = P.pe([mm(b[:, 0:256], BO[:, :], t7, True, True)], tv, fb)
                yield
                t1 = P.dve(lambda e, b=b: e.tensor_scalar(t7, b[:, 0:256], 1e-24, 2.0 ** 20, A.max, A.mult), tk)
                done(i, t1)
                P.act(lambda e: e.activation(al, t7, AF.Ln), t1)
                t1 = P.act(lambda e: e.activation(al, al, AF.Exp, scale=-0.5))
                yield
                P.dve(lambda e, pt=pt: e.tensor_scalar(kR, a, 1.0, pcol("rw_k_a_2", pt), A.subtract, A.mult), pf)
                P.dve(lambda e: e.scalar_tensor_tensor(k, kR, 1.0, k, A.add, A.mult))
                P.dve(lambda e, pt=pt: e.tensor_scalar(kR, r, pcol("rw_r_k_2", pt), None, A.mult))
                tv = P.dve(lambda e: e.tensor_tensor(kR, kR, k, A.mult))
                i, b, fb = bank()
                tk = P.pe([mm(b[:, 0:256], BO[:, :], kR, True, True)], tv, fb)
                yield
                P.dve(lambda e: e.scalar_tensor_tensor(be, al, -0.5, al, A.mult, A.mult), t1, pf)
                P.dve(lambda e: e.tensor_tensor(be, be, t7, A.mult))
                P.dve(lambda e: e.scalar_tensor_tensor(al, be, 1.5, al, A.add, A.mult))
                P.dve(lambda e: e.scalar_tensor_tensor(kk, kk, 2.0 ** 10, al, A.mult, A.mult))
                yield
                tb = P.dve(lambda e, b=b, pt=pt: e.tensor_tensor(BV[:, pt, ts], v, b[:, 0:256], A.mult), tk, fr)
                done(i, tb)
                P.dve(lambda e: e.tensor_tensor(be, kk, a, A.mult))
                c3 = lambda x: x.rearrange("p (c j) -> p c j", j=64)
                bc, p3, s3_ = c3(b_), c3(t6), c3(t7)
                mid = bc[:, :, 31:32].to_broadcast([128, 4, 64])
                cr = slice(4 * hf, 4 * hf + 4)
                yield
                t1 = P.dve(lambda e, pt=pt: e.tensor_tensor(eend[:, pt, cr], bc[:, :, 63], bc[:, :, 31], A.subtract))
                P.dve(lambda e: e.tensor_tensor(p3, p3, mid, A.subtract))
                P.act(lambda e, pt=pt: e.activation(eend[:, pt, cr], eend[:, pt, cr], AF.Exp), t1)
                P.act(lambda e, pt=pt: e.activation(eref[:, pt, cr], bc[:, :, 31], AF.Exp))
                t1 = P.dve(lambda e: e.tensor_tensor(s3_, bc, mid, A.subtract))
                yield
                P.act(lambda e: e.activation(t6, t6, AF.Exp), t1)
                ta = P.act(lambda e: e.activation(rR, t7, AF.Exp), pf)
                t1 = P.act(lambda e: e.activation(t7, t7, AF.Exp, scale=-1.0))
                P.dve(lambda e: e.scalar_tensor_tensor(al, kk, -1.0, t6, A.mult, A.mult), ta)
                P.dve(lambda e: e.tensor_tensor(rR, rR, r, A.mult))
                P.dve(lambda e: e.tensor_tensor(be, be, t7, A.mult), t1)
                tf = P.dve(lambda e: e.tensor_tensor(kR, k, t7, A.mult))
                yield
                for (s0, s1), dst in (((al, be), U[6]), ((kR, v), U[7])):
                    i, b, fb = bank()
                    tk = P.pe([tr(b[:, 256 * n + j * 128:256 * n + (j + 1) * 128], src[:, j * 128:(j + 1) * 128], ident[:, :]) for n, src in enumerate((s0, s1)) for j in range(2)], tf, fb)
                    td = evac(dst, b[:, :], tk)
                    done(i, td)
                    yield
                tT = P.now("act", "dve", "pe")
                lead.append(pt)
                for par_ in range(2):
                    yield from head(par_, hf, pt, U, H2, aT, bT, kT, vT, tT, fam)
            halves[hf] = P.now()

        halves = {}

        def head(par_, hf, pt, U, H2, aT, bT, kT, vT, tT, fam):
            h = 2 * pt + par_
            q0 = par_ * 64
            hs = slice(q0, q0 + 64)
            tl0 = 2 * hf
            al, be, kR, rR = H2[8:12]
            N16, L16, N32, L32, Pm, Qm, N2, L2 = H2[0:8]
            L64, AkT, RbT, RkT, X1, X2 = H2[16:22]
            fz = [tT, fam[0]]
            for n in (0, 1, 8, 9):
                tz = P.pool(lambda e, u=U[n]: e.memset(u, 0.0), fz)
            yield

            def scores(prs, outs):
                i, b, fb = bank()
                tk = P.pe([mm(b[:, 256 * n + j * 128:256 * n + (j + 1) * 128], l[hs, j * 128:(j + 1) * 128], rr[hs, j * 128:(j + 1) * 128], True, True) for n, (l, rr) in enumerate(prs) for j in range(2)], fb, tT)
                for dst, mask, o, w_ in outs:
                    m = mask.unsqueeze(2).to_broadcast([128, w_, 2, 128])
                    tv = P.dve(lambda e, dst=dst, m=m, b=b, o=o, w_=w_: e.copy_predicated(dst.rearrange("p (a t n) -> p a t n", a=w_, n=128), m, b[:, 256 * o:256 * (o + w_)].rearrange("p (a t n) -> p a t n", a=w_, n=128)), tk, tz)
                done(i, tv)
                return tv

            tsc0 = scores([(be, al), (al, be)], [(U[0], mband[:, 0:2, :], 0, 2), (U[1], mband[:, 2:4, :], 0, 2), (L64, mband[:, 4:5, :], 1, 1)])
            yield

            def mul2(x, y, *deps, n=2):
                i, b, fb = bank()
                return i, b[:, 0:256 * n], P.pe([mm(b[:, 256 * m + j * 128:256 * m + (j + 1) * 128], x[m][:, j * 128:(j + 1) * 128], y[m][:, j * 128:(j + 1) * 128], True, True) for m in range(n) for j in range(2)], fb, *deps)

            def cp(dst, ibk, *deps):
                i, b, tk = ibk
                tv = P.act(lambda e: e.activation(dst, b, AF.Copy), tk, *deps, ns=500)
                done(i, tv)
                return tv

            def addto(dst, ibk, *deps):
                i, b, tk = ibk
                tv = P.dve(lambda e: e.tensor_tensor(dst, dst, b, A.add), tk, *deps, ns=620)
                done(i, tv)
                return tv

            v4 = lambda x: x.rearrange("p (t n) -> p t n", n=128)
            PQ = (Pm, Qm)
            tpq = P.dve(lambda e: e.tensor_tensor(v4(U[2]), v4(U[0]), ident[:, :].unsqueeze(1).to_broadcast([128, 4, 128]), A.add))
            cur, new = U[0], U[3]
            for lev in range(3):
                n_, l_ = cur[:, 0:256], cur[:, 256:512]
                c1 = cp(new, mul2((l_, n_), (n_, l_), tsc0 if lev == 0 else c1), fz)
                yield
                if lev == 0:
                    scores([(kR, al)], [(AkT, mband[:, 5:6, :], 0, 1)])
                if lev == 1:
                    tsc = scores([(be, rR), (kR, rR)], [(RbT, mk[:, 0:1, :], 0, 1), (RkT, mk[:, 0:1, :], 1, 1)])
                n_, l_ = new[:, 0:256], new[:, 256:512]
                tpq = addto(U[2], mul2((l_, n_), PQ, c1, tpq))
                yield
                cur, new = new, (U[10], U[3])[lev % 2]
            a1 = cp(U[0], mul2((L32, N32), PQ, tpq), P.now("pe"))
            yield
            tpq = addto(U[2], mul2((Qm, Pm), (N16, L16), a1))
            yield
            hc = slice(q0, q0 + 64)
            a1 = cp(N16, mul2((L64,), (Pm,), tpq, n=1))
            i, b, fb = bank()
            tk = P.pe([mm(b[:, j * 64:(j + 1) * 64], AkT[:, j * 128:(j + 1) * 128], vT[:, j, hc], True, True) for j in range(2)], fb, tsc)
            Z, W1, UV = N2[:, 0:128], L2[:, 0:128], L2[:, 128:256]
            tz_ = P.act(lambda e, b=b: e.activation(Z, b[:, 0:128], AF.Copy), tk, tpq)
            done(i, tz_)
            yield
            tP = addto(Pm, mul2((Qm,), (N16,), a1, n=1))
            yield
            i, b, fb = bank()
            tk = P.pe([mm(b[:, j * 64:(j + 1) * 64], Pm[:, j * 128:(j + 1) * 128], aT[:, j, hc], True, True) for j in range(2)]
                      + [mm(b[:, 128 + j * 64:128 + (j + 1) * 64], Pm[:, j * 128:(j + 1) * 128], Z[:, j * 64:(j + 1) * 64], True, True) for j in range(2)], fb, tz_, tP)
            tw = P.act(lambda e, b=b: e.activation(L2, b[:, 0:256], AF.Copy), tk)
            done(i, tw)
            yield
            i, b, fb = bank()
            tk = P.pe([mm(b[hs, j * 128:(j + 1) * 128], W1[:, j * 64:(j + 1) * 64], RbT[:, j * 128:(j + 1) * 128], True, True) for j in range(2)], fb, tw, tsc)
            tq = P.dve(lambda e, b=b: e.tensor_tensor(QT[hs, pt, 256 * hf:256 * hf + 256], b[hs, 0:256], rR[hs, :], A.add), tk, fr)
            done(i, tq)
            i, b, fb = bank()
            tk = P.pe([f for j in range(2) for f in (mm(b[:, j * 64:(j + 1) * 64], RbT[:, j * 128:(j + 1) * 128], UV[:, j * 64:(j + 1) * 64], True, False),
                                                     mm(b[:, j * 64:(j + 1) * 64], RkT[:, j * 128:(j + 1) * 128], vT[:, j, hc], False, True))], fb)
            ty = P.act(lambda e, b=b: e.activation(Y0[:, tl0:tl0 + 2, h * 64:(h + 1) * 64], b[:, 0:128].rearrange("p (t n) -> p t n", t=2), AF.Copy), tk, fr)
            done(i, ty)
            yield
            for ev in range(2):
                i, b, fb = bank()
                ps_ = slice(ev * 64, ev * 64 + 64)
                fs = []
                for tt in range(2):
                    o_, o2 = slice(tt * 64, tt * 64 + 64), slice(128 + tt * 64, 192 + tt * 64)
                    fs += [mm(b[hs, o_], W1[ps_, tt * 64:(tt + 1) * 64], bT[ps_, tt, hc], True, True),
                           mm(b[hs, o2], bT[ps_, tt, hc], UV[ps_, tt * 64:(tt + 1) * 64], True, False),
                           mm(b[hs, o2], kT[ps_, tt, hc], vT[ps_, tt, hc], False, True)]
                tk = P.pe(fs, fb)
                d = GH5[hs, :, pt, tl0:tl0 + 2, ev, :]
                s_ = b[hs, 0:256].rearrange("p (g t n) -> p g t n", g=2, n=64)
                if ev:
                    tg = P.act(lambda e, d=d, s_=s_: e.activation(d, s_, AF.Copy), tk, fr)
                else:
                    tg = P.dve(lambda e, d=d, s_=s_: e.tensor_copy(d, s_), tk, fr)
                done(i, tg)
            fam[0] = P.now("pe", "act", "dve")
            yield

        GH5 = GH.rearrange("p (g a t c n) -> p g a t c n", g=2, a=4, c=2, n=64)
        rkv_load(0)
        rkv_load(1)
        dsa_end = {}
        mem, sel_ = {}, {}
        P.weave(half(0), half(1), tail(halves, QT, Y0, GTm, Hm, BV, GT, tmp, eref, eend),
                (dsa(dsa_end, sel_, xtt, KI, WI, w_in, P.now(), [xs]), SLOW1), (dsa_heads(0, sel_), SLOW2), (dsa_heads(1, sel_), SLOW2), gate2(halves, dsa_end, w_in, xtt), memory(mem))
        cross(mem)

    def tail(halves, QT, Y0, GTm, Hm, BV, GT, tmp, eref, eend):
        while len(halves) < 2:
            yield
        fam_free = list(halves.values())
        P.dve(lambda e: e.tensor_tensor(eend[:, :, 0:7], eend[:, :, 0:7], eref[:, :, 1:8], A.mult), fam_free)
        MB = [tmp[i] for i in range(8)]
        M4 = [m[:, 0:256].rearrange("p (a n) -> p a n", a=4) for m in MB]
        H5 = Hm.rearrange("p a (c n) -> p a c n", c=8)
        tm = None
        for c in range(7):
            dst = M4[c + 1]
            ec = eend[:, :, c:c + 1].to_broadcast([128, 4, 64])
            if c == 0:
                P.dve(lambda e, dst=dst: e.tensor_copy(dst, H5[:, :, 0, :]), fam_free)
            else:
                i, b, fb = bank()
                i2, b2, fb2 = bank()
                fs = []
                for pt in range(4):
                    for hs, bb in ((slice(0, 64), b), (slice(64, 128), b2)):
                        fs.append(mm(bb[hs, pt * 64:(pt + 1) * 64], GTm[hs, pt, c * 64:(c + 1) * 64], M4[c][hs, pt, :], True, True))
                tk = P.pe(fs, fb, fb2, tm, fam_free)
                P.dve(lambda e, dst=dst, c=c: e.tensor_tensor(dst, M4[c], H5[:, :, c, :], A.add))
                P.dve(lambda e, dst=dst, b=b: e.tensor_tensor(dst[0:64], dst[0:64], b[0:64, 0:256].rearrange("p (a n) -> p a n", a=4), A.add), tk)
                t2 = P.dve(lambda e, dst=dst, b2=b2: e.tensor_tensor(dst[64:128], dst[64:128], b2[64:128, 0:256].rearrange("p (a n) -> p a n", a=4), A.add), tk)
                done(i, t2)
                done(i2, t2)
            tm = P.dve(lambda e, dst=dst, ec=ec: e.tensor_tensor(dst, dst, ec, A.mult))
            yield
        for c in range(1, 8):
            tt, pp = c // 2, (c % 2) * 64
            for ev in range(2):
                hs = slice(ev * 64, ev * 64 + 64)
                i, b, fb = bank()
                tk = P.pe([mm(b[pp:pp + 64, pt * 64:(pt + 1) * 64], QT[hs, pt, c * 64:(c + 1) * 64], M4[c][hs, pt, :], True, True) for pt in range(4)], fb, tm)
                yield
                yh = Y0[pp:pp + 64, tt, :].rearrange("p (a e n) -> p a e n", e=2, n=64)[:, :, ev, :]
                ty = P.dve(lambda e, b=b, yh=yh, pp=pp: e.tensor_tensor(yh, yh, b[pp:pp + 64, 0:256].rearrange("p (a n) -> p a n", n=64), A.add), tk)
                done(i, ty)
        yield
        yv = Y0.rearrange("p t (h n) -> p (t h) n", n=64)
        junk = SC[:, NSC - 1, :]
        jv = junk.rearrange("p (a n) -> p a n", n=64)
        mean, var = st(32), st(32)
        P.dve(lambda e: e.tensor_reduce(mean, yv, AX, A.add))
        P.dve(lambda e: e.tensor_scalar(mean, mean, 1.0 / 64, None, A.mult))
        t1 = P.dve(lambda e: e.tensor_tensor(yv, yv, mean.unsqueeze(2).to_broadcast([128, 32, 64]), A.subtract))
        yield
        t1 = P.act(lambda e: e.activation(jv, yv, AF.Square), t1)
        t1 = P.dve(lambda e: e.tensor_reduce(var, jv, AX, A.add), t1)
        yield
        rs2, t1 = rsq(var, 32, 1.0 / 64, 64e-5, t1)
        t1 = P.dve(lambda e: e.tensor_tensor(yv, yv, rs2.unsqueeze(2).to_broadcast([128, 32, 64]), A.mult))
        YA = QT
        for j in range(4):
            i, b, fb = bank()
            tk = P.pe([tr(b[:, n * 128:(n + 1) * 128], Y0[:, n, j * 128:(j + 1) * 128], ident[:, :]) for n in range(NT)], t1, fb)
            t2 = P.dve(lambda e, b=b, j=j: e.tensor_scalar(YA[:, j, :], b[:, :], pcol("rw_ln_w_2", j), pcol("rw_ln_b_2", j), A.mult, A.add), tk)
            done(i, t2)
            P.dve(lambda e, j=j: e.tensor_tensor(YA[:, j, :], YA[:, j, :], BV[:, j, :], A.add))
            tya = P.dve(lambda e, j=j: e.tensor_tensor(YA[:, j, :], YA[:, j, :], GT[:, j, :], A.mult))
            yield
        keep["tail"] = P.now()
        keep["ya"] = tya

    def dsa(end, sel_, xtt, KI, WI, w_in, fr, xs):
        XX = X[:, :, :].rearrange("p t n -> p (t n)")
        R2, R3 = RING[:, 2, :], RING[:, 3, :]
        qF = XX[:, 0:2048].rearrange("p (a n) -> p a n", a=4)
        YB = qF
        ct, cT = XX[:, 2048:2560].rearrange("p (t n) -> p t n", t=4), XX[:, 2560:3072]
        QI = XX[:, 3072:4096].rearrange("p (a n) -> p a n", a=2)
        wuk, wuv = R3[:, 3072:3584], R3[:, 3584:4096]
        wq, wd = R2.rearrange("p (k n) -> p k n", k=8), R3[:, 0:3072].rearrange("p (k n) -> p k n", k=8)
        tw = P.dma("act", lambda e: e.dma_start(wuk, t["w_uk_2"].rearrange("l r h n -> (l r) (h n)")), "dsw", fr)
        tw = P.dma("act", lambda e: e.dma_start(wuv, t["w_uv_2"].rearrange("l r h n -> (l r) (h n)")), "dsw", fr)
        wi_ = w_in.rearrange("(k p) n -> p k n", p=128)
        td_ = P.dma("sp", lambda e: e.dma_start(wd, wi_[:, :, 2304:2688]), "dsd", fr)
        tq_ = P.dma("sp", lambda e: e.dma_start(wq, wi_[:, :, 1792:2304]), "dsq", fr)
        U2 = [R2[:, 512 * n:512 * n + 512] for n in range(8)]
        acc, work, eq, cum, junk, wukT_, rel0, rel1 = U2
        wukT = wukT_.rearrange("p (a n) -> p a n", a=4)
        rel = [rel0, rel1]
        BM = R3[:, 0:2048].rearrange("p (a n) -> p a n", a=4)
        ql = [R3[:, 2048:2560], R3[:, 2560:3072]]
        pb = [(acc, work), (eq, cum)]
        pT = [junk, wuk]
        oT = [rel0, rel1]
        yield
        for j in range(2):
            i, b, tk = proj_f(wd, 128 + 128 * j, 128, XT, 8, td_, xtt)
            t1 = evac(QI[:, j, :], b[:, :], tk, xs)
            done(i, t1)
            yield
        ss = st(NT)
        for tt in range(NT):
            i, b, tk = proj_t(wd, 0, 128, XT, tt, 8, td_, xtt)
            tc = P.act(lambda e, b=b, tt=tt: e.activation(ct[:, tt, :], b[:, 0:128], AF.Copy), tk, xs)
            done(i, tc)
            tc = P.act(lambda e, tt=tt: e.activation(cT[:, 0:128], ct[:, tt, :], AF.Square, accum_out=ss[:, tt:tt + 1]))
            yield
        for j in range(4):
            i, b, tk = proj_f(wq, 128 * j, 128, XT, 8, tq_, xtt)
            t1 = evac(qF[:, j, :], b[:, :], tk, xs)
            done(i, t1)
            yield
        fr = P.now("pe")
        i, b, fb = bank()
        tk = P.pe([tr(b[:, j * 128:(j + 1) * 128], wuk[:, j * 128:(j + 1) * 128], ident[:, :]) for j in range(4)], tw, fb)
        t1 = evac(wukT.rearrange("p a n -> p (a n)"), b[:, :], tk, fr)
        done(i, t1)
        rs, rt = rsq(ss, NT, 1.0 / 128, 1e-6, tc)
        for tt in range(NT):
            tc = P.dve(lambda e, tt=tt: e.tensor_scalar(ct[:, tt, :], ct[:, tt, :], rs[:, tt:tt + 1], None, A.mult), rt)
        i, b, fb = bank()
        tk = P.pe([tr(b[:, j * 128:(j + 1) * 128], ct[:, j, :], ident[:, :]) for j in range(4)], tc, fb)
        tcT = evac(cT, b[:, :], tk, fr, scale=pcol("kv_norm_2"))
        done(i, tcT)
        ready = P.now("act", "dve")
        relf = [fr] * 2
        n = 0
        tbm = {0: None}
        for qt in range(1, NT):
            nk = 128 * (qt + 1)
            for h in range(4):
                s = n % 2
                n += 1
                hs = slice((h % 2) * 64, (h % 2) * 64 + 64)
                i, b, fb = bank()
                tk = P.pe([mm(b[:, 0:nk], QI[hs, h // 2, qt * 128:(qt + 1) * 128], KI[hs, 0:nk], True, True)], ready, fb)
                ta = P.act(lambda e, b=b, s=s, nk=nk: e.activation(rel[s][:, 0:nk], b[:, 0:nk], AF.Relu), tk, relf[s])
                done(i, ta)
                if h == 0:
                    tv = P.dve(lambda e, s=s, nk=nk, w=WI[:, qt, 0:1]: e.tensor_scalar(acc[:, 0:nk], rel[s][:, 0:nk], w, None, A.mult), ta, fr)
                else:
                    tv = P.dve(lambda e, s=s, nk=nk, w=WI[:, qt, h:h + 1]: e.scalar_tensor_tensor(acc[:, 0:nk], rel[s][:, 0:nk], w, acc[:, 0:nk], A.mult, A.add), ta)
                relf[s] = tv
                yield
            av, wv_, ev, cv = acc[:, 0:nk], work[:, 0:nk], eq[:, 0:nk], cum[:, 0:nk]
            P.dve(lambda e, nk=nk: e.tensor_tensor(acc[:, nk - 128:nk], acc[:, nk - 128:nk], diagm[:, :], A.add))
            yield
            m8 = st(8)
            for r_ in range(16):
                src = av if r_ == 0 else wv_
                P.dve(lambda e, src=src, m8=m8: e.max(m8, src))
                if r_ < 15:
                    P.dve(lambda e, src=src, m8=m8, wv_=wv_: e.match_replace(wv_, m8, src, -3.0e38))
                yield
            thr = m8[:, 7:8]
            need = st(1)
            P.dve(lambda e, a=av, o=wv_, thr=thr: e.tensor_scalar(o, a, thr, None, A.is_gt))
            yield
            P.dve(lambda e, o=wv_, need=need: e.tensor_reduce(need, o, AX, A.add))
            P.dve(lambda e, need=need: e.tensor_scalar(need, need, -1.0, 128.0, A.mult, A.add))
            P.dve(lambda e, a=av, o=ev, thr=thr: e.tensor_scalar(o, a, thr, None, A.is_equal))
            yield
            P.dve(lambda e, a=ev, o=cv: e.tensor_tensor_scan(o, a, a, 0.0, A.add, A.max))
            P.dve(lambda e, a=cv, o=ev, need=need: e.scalar_tensor_tensor(o, a, need, o, A.is_le, A.mult))
            yield
            P.dve(lambda e, a=wv_, o=ev: e.tensor_tensor(o, a, o, A.add))
            tbm[qt] = P.dve(lambda e, a=ev, o=BM[:, qt, 0:nk]: e.tensor_scalar(o, a, 1.0, -NEG, A.subtract, A.mult), fr)
        sel_.update(ql=ql, pb=pb, pT=pT, oT=oT, BM=BM, qF=qF, YB=YB, ct=ct, cT=cT, wukT=wukT, wuv=wuv, tbm=P.now(), ready=ready, tcT=tcT, tw=tw)
        while "h0" not in sel_ or "h1" not in sel_:
            yield
        end["t"] = [sel_["h0"], sel_["h1"]]
        end["yb"] = qF

    def dsa_heads(sd, sel_):
        while not sel_:
            yield
        ql, pT, oT = sel_["ql"][sd], sel_["pT"][sd], sel_["oT"][sd]
        pb = sel_["pb"][sd]
        BM, qF, YB, ct, cT, wukT, wuv, fr, ready, tcT, tw = (sel_[k] for k in ("BM", "qF", "YB", "ct", "cT", "wukT", "wuv", "tbm", "ready", "tcT", "tw"))
        qlf, pbf, pTf, oTf = [fr], [fr] * 2, [fr], [fr]
        n = 0
        for h in range(sd, 8, 2):
            pt, q0 = h // 2, (h % 2) * 64
            hs = slice(q0, q0 + 64)
            s2 = 0
            i, b, fb = bank()
            tk = P.pe([mm(b[:, :], wukT[hs, pt, :], qF[hs, pt, :], True, True)], ready, fb)
            tql = evac(ql, b[:, :], tk, qlf[s2])
            done(i, tql)
            io, bo, fo = bank()
            for qt in range(NT):
                nk = 128 * (qt + 1)
                s = n % 2
                sp = 0
                n += 1
                stt = st(3)
                p_ = pb[s][:, 0:nk]
                i, b, fb = bank()
                tk = P.pe([mm(b[:, 0:nk], ql[:, qt * 128:(qt + 1) * 128], cT[:, 0:nk], True, True)], tql, tcT, fb)
                bias = diagm[:, :] if qt == 0 else BM[:, qt, 0:nk]
                t1 = P.dve(lambda e, p_=p_, b=b, nk=nk, bias=bias, m=stt[:, 0:1]: e.tensor_tensor_reduce(p_, b[:, 0:nk], bias, 1.0, -3.0e38, A.add, A.max, m), tk, pbf[s], ns=70 + 1.1 * nk)
                done(i, t1)
                t1 = P.dve(lambda e, m=stt[:, 0:1]: e.tensor_scalar(m, m, -0.125, None, A.mult), ns=100)
                yield
                t2 = P.act(lambda e, p_=p_, m=stt: e.activation(p_, p_, AF.Exp, bias=m[:, 0:1], scale=0.125, accum_out=m[:, 1:2]), t1)
                P.dve(lambda e, m=stt: e.reciprocal(m[:, 2:3], m[:, 1:2]), t2, ns=100)
                t3 = P.dve(lambda e, p_=p_, m=stt: e.tensor_scalar(p_, p_, m[:, 2:3], None, A.mult))
                yield
                i, b, fb = bank()
                tk = P.pe([tr(b[:, j * 128:(j + 1) * 128], p_[:, j * 128:(j + 1) * 128], ident[:, :]) for j in range(qt + 1)], t3, fb)
                pbf[s] = tk
                t4 = P.act(lambda e, b=b, nk=nk, d=pT[:, 0:nk]: e.activation(d, b[:, 0:nk], AF.Copy), tk, pTf[sp])
                done(i, t4)
                tk = P.pe([mm(bo[:, qt * 128:(qt + 1) * 128], ct[:, j, :], pT[:, j * 128:(j + 1) * 128], j == 0, j == qt) for j in range(qt + 1)], t4, fo)
                pTf[sp] = tk
                yield
            qlf[s2] = tk
            t5 = P.act(lambda e, bo=bo, s2=s2: e.activation(oT, bo[:, :], AF.Identity, scale=pcol("kv_norm_2")), tk, oTf[s2])
            done(io, t5)
            i, b, fb = bank()
            tk = P.pe([mm(b[hs, :], wuv[:, h * 64:(h + 1) * 64], oT, True, True)], t5, fb, tw)
            oTf[s2] = tk
            t6 = P.act(lambda e, b=b, hs=hs, pt=pt: e.activation(YB[hs, pt, :], b[hs, :], AF.Copy), tk, fr)
            done(i, t6)
            yield
        sel_[f"h{sd}"] = P.now()

    def gate2(halves, end, w_in, xtt):
        while len(halves) < 2 or "t" not in end:
            yield
        fr = [halves[0], halves[1], end["t"]]
        ring_order[:] = range(NRING)
        for i in range(NRING):
            ring_free[i] = list(fr)
        nbg = st(16)
        tn = P.dve(lambda e: e.tensor_scalar(nbg, pcols("b_gate_2", 16), -1.0, None, A.mult))
        YA = scv(0, 4)
        E4 = scv(10, 4)
        toks = []

        def ya():
            if len(toks) == 1:
                toks.append(P.dma("act", lambda e: e.dma_start(X[:, :, :], xkeep.rearrange("(t p) n -> p t n", p=128)), "xl", end["t"], toks[0]))
                keep["xback"] = toks[1]
            return (YA, keep["ya"]) if "ya" in keep else None

        yield from gated(w_in, 2756, ((1, t["w_proj_b_2"][0], lambda: (end["yb"], end["t"])), (0, t["w_proj_a_2"][0], ya)), nbg,
                         t["w_out_2"][0], xtt, scv(8, 8, 2), ([E4[:, 0, :], E4[:, 1, :]], [E4[:, 2, :], E4[:, 3, :]]), [fr, tn], toks)

    def memory(mem):
        while "ya" not in keep:
            yield
        fr = [keep["ya"], keep["tail"]]
        MEM, MN, MT = scv(6, 2), scv(7, 2), scv(1, 8)
        tm = P.dma("act", lambda e: e.dma_start(MEM, t["mem_2"][0].rearrange("(t p) n -> p t n", p=128)), "mem", fr)
        rm, rmt = rms(MEM, 2, D, tm, fr)
        yield
        for i in range(2):
            tx = P.dve(lambda e, i=i: e.tensor_scalar(MN[:, i, :], MEM[:, i, :], rm[:, i:i + 1], None, A.mult), rmt, fr)
        yield
        gain = pcols("norm_mem_2", 8)
        tmt = []
        for k in range(8):
            i, b, fr_ = bank()
            t1 = P.pe([tr(b[:, j * 128:(j + 1) * 128], MN[:, j, k * 128:(k + 1) * 128], ident[:, :]) for j in range(2)], tx, fr_)
            t2 = evac(MT[:, k, :], b[:, 0:256], t1, fr, scale=gain[:, k:k + 1])
            done(i, t2)
            tmt.append(t2)
            yield
        mem["MT"], mem["t"] = MT, tmt[-2:]

    def cross(mem):
        fr = P.now()
        MT, tmt = mem["MT"], mem["t"]
        kT, V, qF = scv(2, 8), scv(3, 2), scv(4, 8, 2)
        PT = [SC[:, 6, 1024 * i:1024 * (i + 1)].rearrange("p (a n) -> p a n", a=2) for i in range(2)]
        oT = scv(8, 8, 2)
        xn = scv(8, 4, 2)
        rs, rt = rms(X, NT, D, fr)
        for i in range(NT):
            txn = P.dve(lambda e, i=i: e.tensor_scalar(xn[:, i, :], X[:, i, :], rs[:, i:i + 1], None, A.mult), rt, fr)
        for half in range(2):
            u_, s_, ut = wcols(t["w_ckv_2"][0], half * 512, 512)
            wv = s_.rearrange("p (k n) -> p k n", k=8)
            for j in range(4):
                i, b, tk = proj_f(wv, j * 128, 128, MT, 8, ut, tmt)
                t1 = evac(kT[:, half * 4 + j, :], b[:, 0:256], tk, fr)
                done(i, t1)
            unit_done(u_, tk)
        for half in range(2):
            u_, s_, ut = wcols(t["w_ckv_2"][0], 1024 + half * 512, 512)
            wv = s_.rearrange("p (k n) -> p k n", k=8)
            for j in range(2):
                i, b, tk = proj_t(wv, 0, 512, MT, j, 8, ut, tmt)
                t1 = evac(V[:, j, half * 512:(half + 1) * 512], b[:, :], tk, fr)
                done(i, t1)
            unit_done(u_, tk)
        xtt = transposed(xn, NT, pcols("norm_cross_2", 8), XT, txn, fr)
        for half in range(2):
            u_, s_, ut = wcols(t["w_cq_2"][0], half * 512, 512)
            wv = s_.rearrange("p (k n) -> p k n", k=8)
            for j in range(4):
                i, b, tk = proj_f(wv, j * 128, 128, XT, 8, ut, xtt)
                t1 = evac(qF[:, half * 4 + j, :], b[:, :], tk, fr)
                done(i, t1)
            unit_done(u_, tk)
        ready = P.now("act", "dve", "pe") 

        def heads(sd):
            pb = [SC[:, 7, 1024 * sd + 256 * i:1024 * sd + 256 * (i + 1)] for i in range(4)]
            pbf, PTf = [ready] * 4, [ready]
            n = 0
            for h in (sd, sd + 2):
                for qt in range(NT):
                    s = n % 4
                    n += 1
                    stt = st(3)
                    i, b, fb = bank()
                    tk = P.pe([mm(b[:, 0:256], qF[:, 2 * h + c, qt * 128:(qt + 1) * 128], kT[:, 2 * h + c, :], c == 0, c == 1) for c in range(2)], ready, fb)
                    P.dve(lambda e, b=b, m=stt[:, 0:1]: e.tensor_reduce(m, b[:, 0:256], AX, A.max), tk)
                    t1 = P.dve(lambda e, m=stt[:, 0:1]: e.tensor_scalar(m, m, -0.0625, None, A.mult), ns=100)
                    t2 = P.act(lambda e, p_=pb[s], b=b, m=stt: e.activation(p_, b[:, 0:256], AF.Exp, bias=m[:, 0:1], scale=0.0625, accum_out=m[:, 1:2]), t1, pbf[s])
                    done(i, t2)
                    yield
                    P.dve(lambda e, m=stt: e.reciprocal(m[:, 2:3], m[:, 1:2]), t2, ns=100)
                    t3 = P.dve(lambda e, p_=pb[s], m=stt: e.tensor_scalar(p_, p_, m[:, 2:3], None, A.mult))
                    yield
                    i, b, fb = bank()
                    tk = P.pe([tr(b[:, j * 128:(j + 1) * 128], pb[s][:, j * 128:(j + 1) * 128], ident[:, :]) for j in range(2)], t3, fb)
                    pbf[s] = tk
                    tp = P.act(lambda e, b=b, d=PT[sd][:, :, qt * 128:(qt + 1) * 128]: e.activation(d, b[:, 0:256].rearrange("p (a n) -> p a n", a=2), AF.Copy), tk, PTf[0])
                    done(i, tp)
                    yield
                for c in range(2):
                    i, b, fb = bank()
                    tk = P.pe([mm(b[:, :], V[:, m, h * 256 + c * 128:h * 256 + (c + 1) * 128], PT[sd][:, m, :], m == 0, m == 1) for m in range(2)], tp, fb)
                    to = evac(oT[:, 2 * h + c, :], b[:, :], tk, ready)
                    done(i, to)
                    yield
                PTf[0] = tk

        P.weave(heads(0), heads(1))
        P.weave(add_proj(t["w_co_2"][0], oT, P.now("act", "dve"), []))

    def finish():
        stn[0] = 0
        fr = P.now()
        gr = scv(0, 2)[:, 0, :]
        Y = scv(1, 4, 2)
        tg = P.dma("act", lambda e: e.dma_start(gr, t["norm_final_2"].rearrange("(a n) -> a n", a=1).to_broadcast([128, D])), "fg", fr)
        rs, rt = rms(X, NT, D, fr)
        for i in range(NT):
            t1 = P.dve(lambda e, i=i: e.scalar_tensor_tensor(Y[:, i, :], X[:, i, :], rs[:, i:i + 1], gr, A.mult, A.mult), rt, tg)
            P.dma("sp", lambda e, i=i: e.dma_start(out[0, i * 128:(i + 1) * 128, :], Y[:, i, :]), "out", t1)


    keep = {}
    ST_KEEP = 0
    for phase in (block1_mix, lambda: moe(0), block2_mix, lambda: moe(1), finish):
        phase()
    block = ctx.enter_context(nc.Block())
    for nm, deco in (("sp", block.sync), ("act", block.scalar), ("dve", block.vector), ("pool", block.gpsimd), ("pe", block.tensor)):
        @deco
        def _(e, nm=nm):
            P.emit(nm, e)
            if nm == "sp" and "out" in P.sems:
                e.wait_ge(P.sems["out"], P.n["out"])


_INS = ["x", "norm_mix", "w_in", "hg_lb", "hg_out_norm", "da_q_norm", "da_k_norm", "da_lambda", "da_out_norm",
        "w_branch_hg", "w_branch_da", "w_out", "norm_moe", "w_router_group", "b_router_group", "w_router_expert",
        "b_router_expert", "w1", "w3", "w2", "mem_2", "norm_mix_2", "w_in_2", "shift_mu_2", "rw_w0_2", "rw_w2_2",
        "rw_a0_2", "rw_a2_2", "rw_g2_2", "rw_k_k_2", "rw_k_a_2", "rw_r_k_2", "rw_ln_w_2", "rw_ln_b_2", "kv_norm_2",
        "w_uk_2", "w_uv_2", "w_proj_a_2", "w_proj_b_2", "b_gate_2", "w_out_2", "norm_cross_2", "norm_mem_2", "w_cq_2",
        "w_ckv_2", "w_co_2", "norm_ffn_2", "w_router_g_2", "b_router_g_2", "w_router_e_2", "b_router_e_2",
        "w_e_gate_2", "w_e_up_2", "w_e_down_2", "norm_final_2"]


def rope_tables():
    half = 32
    inv = np.float32(10000.0) ** (-np.arange(half, dtype=np.float32) / np.float32(half))
    ang = np.arange(T, dtype=np.float32)[:, None] * inv.astype(np.float32)[None, :]
    return np.cos(ang).astype(np.float32), np.sin(ang).astype(np.float32)


def kernel(**inputs):
    import concourse.bacc as _bacc
    from concourse.bass_utils import run_bass_kernel_spmd as _run

    nc = _bacc.Bacc("TRN2", target_bir_lowering=False, num_devices=1, dynamic_dma_scratch_size=8192)
    arrays, t = {}, {}
    cos, sin = rope_tables()
    for name, a in [(n, np.ascontiguousarray(inputs[n])) for n in _INS] + [("rope_cos", cos), ("rope_sin", sin)]:
        arrays[f"in_{name}"] = a
        t[name] = nc.dram_tensor(f"in_{name}", a.shape, F, kind="ExternalInput").ap()
    out = nc.dram_tensor("out_0", (1, T, D), F, kind="ExternalOutput").ap()
    program(nc, t, out)
    r = _run(nc, [arrays], core_ids=[0])
    return r.results[0]["out_0"]
```
